# Optimizing a Trainium2 kernel written in Bass

```python
import math
import jax, jax.numpy as jnp
from jax import lax
import numpy as np
import jax
import jax.numpy as jnp

D_MODEL = 1024
BATCH = 1
SEQ = 256
DEPTH = 2

HEAD_DIM = 64
N_Q_HEADS = 8
N_KV_HEADS = 2
GQA_GROUP = N_Q_HEADS // N_KV_HEADS
ATTN_WIDTH = N_Q_HEADS * HEAD_DIM
KV_WIDTH = N_KV_HEADS * HEAD_DIM
N_CONV_GROUPS = 8
CONV_WIDTH = N_CONV_GROUPS * HEAD_DIM
MIX_WIDTH = ATTN_WIDTH + CONV_WIDTH
CONV_K = 3
WINDOW = 128
BLOCK = 128
D_FF = 2816
NORM_EPS = 1e-6

Q_END = ATTN_WIDTH
K_END = Q_END + KV_WIDTH
V_END = K_END + KV_WIDTH
CB_END = V_END + CONV_WIDTH
CC_END = CB_END + CONV_WIDTH
CH_END = CC_END + CONV_WIDTH
IN_WIDTH = CH_END


def rms_norm(x, gain):
    xf = x.astype(jnp.float32)
    inv = lax.rsqrt(jnp.mean(xf * xf, axis=-1, keepdims=True) + NORM_EPS)
    return (xf * inv).astype(x.dtype) * gain

def swiglu(h, w_gate, w_up, w_down):
    return (jax.nn.silu(h @ w_gate) * (h @ w_up)) @ w_down

def alibi_slopes(n_heads):
    return jnp.exp2(-8.0 * jnp.arange(1, n_heads + 1, dtype=jnp.float32) / n_heads)

def short_conv(b_gate, c_gate, h_conv, conv_w):
    u = c_gate * h_conv
    w = conv_w.astype(u.dtype)[:, None, :]
    y = lax.conv_general_dilated(
        u, w, window_strides=(1,), padding=[(CONV_K - 1, 0)],
        dimension_numbers=("NWC", "WIO", "NWC"), feature_group_count=CONV_WIDTH)
    return b_gate * y

def sliding_window_attention(q, k, v, sink):
    bsz, seq = q.shape[0], q.shape[1]
    nb = seq // BLOCK
    qb = q.reshape(bsz, nb, BLOCK, N_KV_HEADS, GQA_GROUP, HEAD_DIM)
    kb = k.reshape(bsz, nb, BLOCK, N_KV_HEADS, HEAD_DIM)
    vb = v.reshape(bsz, nb, BLOCK, N_KV_HEADS, HEAD_DIM)
    pad = ((0, 0), (1, 0), (0, 0), (0, 0), (0, 0))
    k_band = jnp.concatenate([jnp.pad(kb, pad)[:, :-1], kb], axis=2)
    v_band = jnp.concatenate([jnp.pad(vb, pad)[:, :-1], vb], axis=2)

    scale = 1.0 / math.sqrt(HEAD_DIM)
    scores = jnp.einsum("bnqkgd,bnskd->bnkgqs", qb, k_band).astype(jnp.float32) * scale

    qi = jnp.arange(BLOCK)[:, None]
    kj = jnp.arange(2 * BLOCK)[None, :]
    dist = qi + BLOCK - kj
    in_window = (dist >= 0) & (dist < WINDOW)
    blk = jnp.arange(nb)[:, None, None]
    mask = in_window[None] & ((blk > 0) | (kj[None] >= BLOCK))

    slopes = alibi_slopes(N_Q_HEADS).reshape(N_KV_HEADS, GQA_GROUP)
    bias = -slopes[:, :, None, None] * dist.astype(jnp.float32)[None, None]
    scores = scores + bias[None, None]
    mask_b = mask[None, :, None, None]
    scores = jnp.where(mask_b, scores, -jnp.inf)

    sink_l = sink.astype(jnp.float32).reshape(1, 1, N_KV_HEADS, GQA_GROUP, 1, 1)
    m = jnp.maximum(jnp.max(scores, axis=-1, keepdims=True), sink_l)
    p = jnp.where(mask_b, jnp.exp(scores - m), 0.0)
    denom = jnp.sum(p, axis=-1, keepdims=True) + jnp.exp(sink_l - m)
    probs = (p / denom).astype(v.dtype)
    out = jnp.einsum("bnkgqs,bnskd->bnqkgd", probs, v_band)
    return out.reshape(bsz, seq, ATTN_WIDTH)

def first_inputs(seed: int = 0) -> dict:
    key = jax.random.key(seed)
    ks = jax.random.split(key, 20)
    f32 = jnp.float32

    def w(k, shape, fan_in):
        return jax.random.normal(k, shape, f32) * (fan_in ** -0.5)

    def gain(k, shape):
        return 1.0 + 0.05 * jax.random.normal(k, shape, f32)

    return {
        "x": jax.random.normal(ks[0], (BATCH, SEQ, D_MODEL), f32),
        "ffn1_norm": gain(ks[1], (DEPTH, D_MODEL)),
        "ffn1_wg": w(ks[2], (DEPTH, D_MODEL, D_FF), D_MODEL),
        "ffn1_wu": w(ks[3], (DEPTH, D_MODEL, D_FF), D_MODEL),
        "ffn1_wd": w(ks[4], (DEPTH, D_FF, D_MODEL), D_FF),
        "mix_norm": gain(ks[5], (DEPTH, D_MODEL)),
        "w_in": w(ks[6], (DEPTH, D_MODEL, IN_WIDTH), D_MODEL),
        "conv_w": w(ks[7], (DEPTH, CONV_K, CONV_WIDTH), CONV_K),
        "attn_sink": 0.5 * jax.random.normal(ks[8], (DEPTH, N_Q_HEADS), f32),
        "w_out": w(ks[9], (DEPTH, MIX_WIDTH, D_MODEL), MIX_WIDTH),
        "ffn2_norm": gain(ks[10], (DEPTH, D_MODEL)),
        "ffn2_wg": w(ks[11], (DEPTH, D_MODEL, D_FF), D_MODEL),
        "ffn2_wu": w(ks[12], (DEPTH, D_MODEL, D_FF), D_MODEL),
        "ffn2_wd": w(ks[13], (DEPTH, D_FF, D_MODEL), D_FF),
        "final_norm": gain(ks[14], (D_MODEL,)),
    }

def first_block(x, ffn1_norm, ffn1_wg, ffn1_wu, ffn1_wd, mix_norm, w_in, conv_w,
              attn_sink, w_out, ffn2_norm, ffn2_wg, ffn2_wu, ffn2_wd, final_norm):
    bsz, seq, _ = x.shape
    for l in range(DEPTH):
        x = x + 0.5 * swiglu(rms_norm(x, ffn1_norm[l]), ffn1_wg[l], ffn1_wu[l], ffn1_wd[l])

        h = rms_norm(x, mix_norm[l])
        z = h @ w_in[l]
        q = z[..., :Q_END].reshape(bsz, seq, N_Q_HEADS, HEAD_DIM)
        k = z[..., Q_END:K_END].reshape(bsz, seq, N_KV_HEADS, HEAD_DIM)
        v = z[..., K_END:V_END].reshape(bsz, seq, N_KV_HEADS, HEAD_DIM)
        attn_out = sliding_window_attention(q, k, v, attn_sink[l])
        conv_out = short_conv(z[..., V_END:CB_END], z[..., CB_END:CC_END],
                              z[..., CC_END:CH_END], conv_w[l])
        x = x + jnp.concatenate([attn_out, conv_out], axis=-1) @ w_out[l]

        x = x + 0.5 * swiglu(rms_norm(x, ffn2_norm[l]), ffn2_wg[l], ffn2_wu[l], ffn2_wd[l])
    return rms_norm(x, final_norm)


DEPTH_2 = 1

N_META = 16
GRID_W = 64
EPS = 1e-6

MLA_HEADS = 8
MLA_NOPE = 128
MLA_ROPE = 64
MLA_V = 128
MLA_Q_RANK = 256
MLA_KV_RANK = 256
MLA_WIDTH = MLA_HEADS * MLA_V
ROPE_BASE = 10000.0
Q_BLOCK = 128

NA_HEADS = 16
NA_HEAD_DIM = 64
NA_WIDTH = NA_HEADS * NA_HEAD_DIM
NA_WIN_R = 8
NA_WIN_C = 16

D_INNER = MLA_WIDTH + NA_WIDTH
IN_SIZES = (MLA_Q_RANK, MLA_KV_RANK, MLA_ROPE, MLA_WIDTH, NA_WIDTH, NA_WIDTH, NA_WIDTH, NA_WIDTH)
D_IN_PROJ = sum(IN_SIZES)


def _rmsnorm(x, w):
    xf = x.astype(jnp.float32)
    y = xf * lax.rsqrt(jnp.mean(xf * xf, axis=-1, keepdims=True) + EPS)
    return (y * w.astype(jnp.float32)).astype(x.dtype)

def _rope(x, cos, sin):
    x1, x2 = jnp.split(x.astype(jnp.float32), 2, axis=-1)
    return jnp.concatenate([x1 * cos - x2 * sin, x2 * cos + x1 * sin], axis=-1).astype(x.dtype)

def _mla(q_lat, kv_lat, k_pe, w_uq, w_ukv, q_lat_w, kv_lat_w, qn_w, qpe_w, kn_w, kpe_w):
    B, L, _ = q_lat.shape
    q = (_rmsnorm(q_lat, q_lat_w) @ w_uq).reshape(B, L, MLA_HEADS, MLA_NOPE + MLA_ROPE)
    kv = (_rmsnorm(kv_lat, kv_lat_w) @ w_ukv).reshape(B, L, MLA_HEADS, MLA_NOPE + MLA_V)
    q_nope, q_pe = q[..., :MLA_NOPE], q[..., MLA_NOPE:]
    k_nope, v = kv[..., :MLA_NOPE], kv[..., MLA_NOPE:]
    q_nope = _rmsnorm(q_nope, qn_w)
    k_nope = _rmsnorm(k_nope, kn_w)
    pos = jnp.arange(L, dtype=jnp.float32)
    inv_freq = ROPE_BASE ** (-(jnp.arange(0, MLA_ROPE, 2, dtype=jnp.float32) / MLA_ROPE))
    ang = pos[:, None] * inv_freq[None, :]
    cos, sin = jnp.cos(ang), jnp.sin(ang)
    q_pe = _rope(_rmsnorm(q_pe, qpe_w), cos[None, :, None, :], sin[None, :, None, :])
    k_pe = _rope(_rmsnorm(k_pe, kpe_w), cos[None], sin[None])
    scale = (MLA_NOPE + MLA_ROPE) ** -0.5

    n_blk = -(-L // Q_BLOCK)
    pad = n_blk * Q_BLOCK - L
    qn = jnp.pad(q_nope, ((0, 0), (0, pad), (0, 0), (0, 0)))
    qn = qn.reshape(B, n_blk, Q_BLOCK, MLA_HEADS, MLA_NOPE).transpose(1, 0, 2, 3, 4)
    qp = jnp.pad(q_pe, ((0, 0), (0, pad), (0, 0), (0, 0)))
    qp = qp.reshape(B, n_blk, Q_BLOCK, MLA_HEADS, MLA_ROPE).transpose(1, 0, 2, 3, 4)

    def block(args):
        qn_b, qp_b = args
        s = (jnp.einsum('bqhd,bkhd->bhqk', qn_b, k_nope)
             + jnp.einsum('bqhr,bkr->bhqk', qp_b, k_pe))
        p = jax.nn.softmax(s.astype(jnp.float32) * scale, axis=-1).astype(v.dtype)
        return jnp.einsum('bhqk,bkhd->bqhd', p, v)

    o = lax.map(block, (qn, qp))
    o = o.transpose(1, 0, 2, 3, 4).reshape(B, n_blk * Q_BLOCK, MLA_WIDTH)
    return o[:, :L]

def _na(q, k, v, q_w, k_w, rel_bias, meta_bias):
    B, L, _ = q.shape
    n_real = L - N_META
    rows = n_real // GRID_W
    win_r = min(NA_WIN_R, rows)
    n_win = win_r * NA_WIN_C
    scale = NA_HEAD_DIM ** -0.5
    q = _rmsnorm(q.reshape(B, L, NA_HEADS, NA_HEAD_DIM), q_w)
    k = _rmsnorm(k.reshape(B, L, NA_HEADS, NA_HEAD_DIM), k_w)
    v = v.reshape(B, L, NA_HEADS, NA_HEAD_DIM)
    q_meta, k_meta, v_meta = q[:, :N_META], k[:, :N_META], v[:, :N_META]
    q_grid = q[:, N_META:].reshape(B, rows, GRID_W, NA_HEADS, NA_HEAD_DIM)
    k_grid = k[:, N_META:].reshape(B, rows, GRID_W, NA_HEADS, NA_HEAD_DIM)
    v_grid = v[:, N_META:].reshape(B, rows, GRID_W, NA_HEADS, NA_HEAD_DIM)

    cols = np.arange(GRID_W)
    c0 = np.clip(cols - NA_WIN_C // 2, 0, GRID_W - NA_WIN_C)
    col_idx_np = c0[:, None] + np.arange(NA_WIN_C)[None, :]
    col_idx = jnp.asarray(col_idx_np, dtype=jnp.int32)
    dc_idx = jnp.asarray(col_idx_np - cols[:, None] + (NA_WIN_C - 1), dtype=jnp.int32)
    meta_b = meta_bias.astype(jnp.float32)[None, :, None, :]

    def row_block(args):
        r, q_row = args
        r0 = jnp.clip(r - win_r // 2, 0, rows - win_r)
        k_rows = lax.dynamic_slice_in_dim(k_grid, r0, win_r, axis=1)
        v_rows = lax.dynamic_slice_in_dim(v_grid, r0, win_r, axis=1)
        k_win = k_rows[:, :, col_idx]
        v_win = v_rows[:, :, col_idx]
        dr_idx = r0 + jnp.arange(win_r, dtype=jnp.int32) - r + (NA_WIN_R - 1)
        bias = rel_bias[:, dr_idx[None, :, None], dc_idx[:, None, :]]
        s_win = (jnp.einsum('bqhd,brqchd->bhqrc', q_row, k_win).astype(jnp.float32) * scale
                 + bias.astype(jnp.float32)[None])
        s_meta = jnp.einsum('bqhd,bmhd->bhqm', q_row, k_meta).astype(jnp.float32) * scale + meta_b
        s = jnp.concatenate([s_win.reshape(B, NA_HEADS, GRID_W, n_win), s_meta], axis=-1)
        p = jax.nn.softmax(s, axis=-1).astype(v.dtype)
        p_win = p[..., :n_win].reshape(B, NA_HEADS, GRID_W, win_r, NA_WIN_C)
        p_meta = p[..., n_win:]
        return (jnp.einsum('bhqrc,brqchd->bqhd', p_win, v_win)
                + jnp.einsum('bhqm,bmhd->bqhd', p_meta, v_meta))

    o_grid = lax.map(row_block, (jnp.arange(rows, dtype=jnp.int32), q_grid.transpose(1, 0, 2, 3, 4)))
    o_real = o_grid.transpose(1, 0, 2, 3, 4).reshape(B, n_real, NA_WIDTH)

    s_mm = jnp.einsum('bqhd,bmhd->bhqm', q_meta, k_meta).astype(jnp.float32) * scale + meta_b
    p_mm = jax.nn.softmax(s_mm, axis=-1).astype(v.dtype)
    o_meta = jnp.einsum('bhqm,bmhd->bqhd', p_mm, v_meta).reshape(B, N_META, NA_WIDTH)
    return jnp.concatenate([o_meta, o_real], axis=1)

def second_inputs(seed: int = 0) -> dict:
    key = jax.random.key(seed)
    ks = jax.random.split(key, 20)
    f32 = jnp.float32

    def nrm(k, shape, scale):
        return jax.random.normal(k, shape, f32) * scale

    def gain(k, shape):
        return 1.0 + 0.05 * jax.random.normal(k, shape, f32)

    return {
        "x": jax.random.normal(ks[0], (BATCH, SEQ, D_MODEL), f32),
        "meta_tokens": nrm(ks[1], (N_META, D_MODEL), 1.0),
        "norm_w": gain(ks[2], (DEPTH_2, D_MODEL)),
        "w_in": nrm(ks[3], (DEPTH_2, D_MODEL, D_IN_PROJ), D_MODEL ** -0.5),
        "q_lat_norm_w": gain(ks[4], (DEPTH_2, MLA_Q_RANK)),
        "kv_lat_norm_w": gain(ks[5], (DEPTH_2, MLA_KV_RANK)),
        "w_uq": nrm(ks[6], (DEPTH_2, MLA_Q_RANK, MLA_HEADS * (MLA_NOPE + MLA_ROPE)), MLA_Q_RANK ** -0.5),
        "w_ukv": nrm(ks[7], (DEPTH_2, MLA_KV_RANK, MLA_HEADS * (MLA_NOPE + MLA_V)), MLA_KV_RANK ** -0.5),
        "mla_qn_w": gain(ks[8], (DEPTH_2, MLA_NOPE)),
        "mla_qpe_w": gain(ks[9], (DEPTH_2, MLA_ROPE)),
        "mla_kn_w": gain(ks[10], (DEPTH_2, MLA_NOPE)),
        "mla_kpe_w": gain(ks[11], (DEPTH_2, MLA_ROPE)),
        "na_q_norm_w": gain(ks[12], (DEPTH_2, NA_HEAD_DIM)),
        "na_k_norm_w": gain(ks[13], (DEPTH_2, NA_HEAD_DIM)),
        "na_rel_bias": nrm(ks[14], (DEPTH_2, NA_HEADS, 2 * NA_WIN_R - 1, 2 * NA_WIN_C - 1), 0.5),
        "na_meta_bias": nrm(ks[15], (DEPTH_2, NA_HEADS, N_META), 0.5),
        "w_out": nrm(ks[16], (DEPTH_2, D_INNER, D_MODEL), D_INNER ** -0.5),
    }

def second_block(x, meta_tokens, norm_w, w_in, q_lat_norm_w, kv_lat_norm_w, w_uq, w_ukv,
              mla_qn_w, mla_qpe_w, mla_kn_w, mla_kpe_w, na_q_norm_w, na_k_norm_w,
              na_rel_bias, na_meta_bias, w_out):
    B = x.shape[0]
    meta = jnp.broadcast_to(meta_tokens.astype(x.dtype)[None], (B, N_META, D_MODEL))
    h_res = jnp.concatenate([meta, x], axis=1)
    split_at = [int(s) for s in np.cumsum(IN_SIZES)[:-1]]
    for l in range(DEPTH_2):
        h = _rmsnorm(h_res, norm_w[l])
        proj = h @ w_in[l]
        q_lat, kv_lat, k_pe, g_mla, na_q, na_k, na_v, g_na = jnp.split(proj, split_at, axis=-1)
        y_mla = _mla(q_lat, kv_lat, k_pe, w_uq[l], w_ukv[l], q_lat_norm_w[l], kv_lat_norm_w[l],
                     mla_qn_w[l], mla_qpe_w[l], mla_kn_w[l], mla_kpe_w[l]) * jax.nn.silu(g_mla)
        y_na = _na(na_q, na_k, na_v, na_q_norm_w[l], na_k_norm_w[l],
                   na_rel_bias[l], na_meta_bias[l]) * jax.nn.silu(g_na)
        h_res = h_res + jnp.concatenate([y_mla, y_na], axis=-1) @ w_out[l]
    return h_res[:, N_META:]


def setup_inputs(seed=0):
    out = dict(first_inputs(seed))
    for name, value in second_inputs(seed + 1).items():
        if name != "x":
            out[name + "_2"] = value
    return out


def reference(
    x, ffn1_norm, ffn1_wg, ffn1_wu, ffn1_wd, mix_norm, w_in, conv_w, attn_sink, w_out,
    ffn2_norm, ffn2_wg, ffn2_wu, ffn2_wd, final_norm, meta_tokens_2, norm_w_2, w_in_2,
    q_lat_norm_w_2, kv_lat_norm_w_2, w_uq_2, w_ukv_2, mla_qn_w_2, mla_qpe_w_2, mla_kn_w_2,
    mla_kpe_w_2, na_q_norm_w_2, na_k_norm_w_2, na_rel_bias_2, na_meta_bias_2, w_out_2,
):
    x = first_block(
        x, ffn1_norm, ffn1_wg, ffn1_wu, ffn1_wd, mix_norm, w_in, conv_w, attn_sink, w_out,
        ffn2_norm, ffn2_wg, ffn2_wu, ffn2_wd, final_norm,
    )
    return second_block(
        x, meta_tokens_2, norm_w_2, w_in_2, q_lat_norm_w_2, kv_lat_norm_w_2, w_uq_2, w_ukv_2,
        mla_qn_w_2, mla_qpe_w_2, mla_kn_w_2, mla_kpe_w_2, na_q_norm_w_2, na_k_norm_w_2,
        na_rel_bias_2, na_meta_bias_2, w_out_2,
    )


_drawn_inputs = setup_inputs


def setup_inputs(seed=0):
    import zlib

    import numpy as np

    out = dict(_drawn_inputs(seed))
    spreads = {}
    factors = {'attn_sink': 4.513,
     'norm_w_2': 6.012,
     'q_lat_norm_w_2': 8.0,
     'kv_lat_norm_w_2': 8.0,
     'mla_qn_w_2': 8.0,
     'mla_qpe_w_2': 8.0,
     'mla_kn_w_2': 8.0,
     'mla_kpe_w_2': 8.0,
     'na_q_norm_w_2': 8.0,
     'na_k_norm_w_2': 8.0,
     'na_meta_bias_2': 3.65}
    for name, (base, spread) in spreads.items():
        noise = np.random.default_rng([zlib.crc32(name.encode()), seed]).standard_normal(out[name].shape)
        drawn = base * np.exp(spread * noise) if base else spread * noise
        out[name] = jnp.asarray(drawn.astype(out[name].dtype))
    for name, factor in factors.items():
        out[name] = (out[name] * factor).astype(out[name].dtype)
    return out
```

```python
from contextlib import ExitStack

import numpy as np
import concourse.bass as bass
from concourse import mybir

F32 = mybir.dt.float32
F32R = mybir.dt.float32r
ACT = mybir.ActivationFunctionType
ALU = mybir.AluOpType
AX_X = mybir.AxisListType.X

P = 128
D = 1024
KT = D // P
T = 256
META = 16
TM = T + META
LAYERS = 2
FF = 2816
FT = FF // P
EPS = 1e-6
MASKED = -1e30
HEADS, HD, BLK = 8, 64, 128
QT = HEADS * HD // P
CT = 4
MH, MN, MR = 8, 128, 64
NH = 16
GW, WR, WC = 64, 4, 16
RELR, RELC = 15, 31
SLOTS = 4
LEAD = SLOTS - 1
PT8 = 8 * P
HALF = FT // 2
PTD = HALF * P
GU, DN, QKV, CONV, WOUT = 2 * FT, 2 * KT, QT + 2, 3 * CT, KT
W8_LAYER = 2 * GU + QKV + CONV + WOUT


def slot_uses(pieces, start=0):
    return [len(range((s - start) % SLOTS, pieces, SLOTS)) for s in range(SLOTS)]


class Phase:

    def __init__(self, pieces, start, before, w8, cols):
        self.pieces, self.start, self.before, self.w8, self.cols = pieces, start, before, w8, cols

    def slot(self, i):
        return (self.start + i) % SLOTS

    def uses(self, i, lap=0):
        return self.before[self.slot(i)] + i // SLOTS + 1 + lap


def plan_layer():
    phases, before, w8 = {}, [0] * SLOTS, 0
    for name, pieces, start, cols in (
        ("gu1", GU, 0, PT8), ("dn1", DN, 0, PTD), ("qkv", QKV, 0, PT8), ("conv", CONV, QKV % SLOTS, PT8),
        ("wout", WOUT, (QKV + CONV) % SLOTS, PT8), ("gu2", GU, 0, PT8), ("dn2", DN, 0, PTD),
    ):
        phases[name] = Phase(pieces, start, list(before), w8, cols)
        before = [b + u for b, u in zip(before, slot_uses(pieces, start))]
        if cols == PT8:
            w8 += pieces
    return phases, before


PHASES, LAYER_USES = plan_layer()

MLA_PIECES = 2 + 1 + 2 + 2 + 2 + 2 + 1
NA_PIECES = 24
SECOND = MLA_PIECES + 8 + NA_PIECES + 8 + 16


def mla_outputs():
    outs = [("kv", 0, 0), ("kv", 1, 1), ("kpe", 0, 2), ("ql", 0, 3), ("ql", 1, 4)]
    outs += [("kn", h, 5 + h // 4) for h in range(MH)]
    outs += [("uv", 3 * c + t, 7 + c) for c in range(2) for t in range(3)]
    outs += [("qn", h, 9 + h // 4) for h in range(MH)]
    outs += [("qpe", j, 11) for j in range(MH // 2)]
    return outs


def na_outputs():
    base = MLA_PIECES + 8
    outs = [("naq", j, base + j) for j in range(8)]
    outs += [("nak", j, base + 8 + j) for j in range(8)]
    outs += [("nav", 3 * c + t, base + 16 + 4 * c + 3) for c in range(2) for t in range(3)]
    return outs


NORM_WIDTH = {"kv": 256, "kpe": 64, "ql": 256, "kn": 128, "qn": 128, "qpe": 64, "naq": 64, "nak": 64}
TOKENS = {"kv": TM, "kpe": TM, "ql": T, "kn": TM, "qn": T, "qpe": T, "naq": T, "nak": TM}

G_NORM = 0
G_CONV = G_NORM + 8 * KT
G_SINK = G_CONV + LAYERS * CT * 3
G_HEAD = G_SINK + LAYERS * HEADS
HEAD_GAIN = {"kv": 0, "ql": 2, "kn": 4, "qn": 5, "kpe": 6, "qpe": 7, "naq": 8, "nak": 9}
SMALL = G_HEAD + 10


def build(nc, xT, metaT, w8, wd, small, mats, btab, rope, colmask, metabias, relbias, out):
    with ExitStack() as ctx:
        def sem(name):
            return ctx.enter_context(nc.semaphore(name))

        def sb(name, shape, dt=F32, stack=ctx):
            return stack.enter_context(nc.sbuf_tensor(name, shape, dt))

        x = sb("x_res", [P, KT, TM])
        raw = sb("w_raw", [P, SLOTS, PTD])
        whi = sb("w_hi", [P, SLOTS, PTD], F32R)
        wlo = sb("w_lo", [P, SLOTS, PTD], F32R)
        hhi = sb("h_hi", [P, KT * TM + P - META], F32R)
        hlo = sb("h_lo", [P, KT * TM + P - META], F32R)
        sq = sb("squares", [P, 2, TM])
        h32 = sb("h_32", [P, 4, TM])
        sg = sb("silu_gate", [P, 2, T])
        g32 = sb("gated_32", [P, 2, T])
        lnv = sb("ln_mean", [P, 2, TM])
        rs = sb("rstd", [P, 2, TM])
        S = sb("scores_sb", [P, 2, 3 * BLK])
        Pr = sb("probs", [P, 2, 3 * BLK])
        PT = sb("probs_T", [P, 2, 3 * BLK])
        O32 = sb("attn_out", [P, 2, D])
        sml = sb("small_sb", [P, SMALL])
        mat = sb("mats_sb", [P, 3, P])
        ones = sb("ones_sb", [P, P])
        rop = sb("rope_sb", [P, 2, TM])
        cmask = sb("colmask_sb", [P, GW])
        metab = sb("metabias_sb", [P, NH, META])
        mx = sb("row_max", [P, 2 * NH])
        nm = sb("neg_max", [P, 2 * NH])
        sums = sb("row_sums", [P, 2 * NH])
        es = sb("sink_terms", [P, 2 * HEADS])
        den = sb("denominators", [P, 2 * NH])
        rec = sb("reciprocals", [P, 2 * NH])
        ident, ones64, rot = mat[:, 0, :], mat[:, 1, :], mat[:, 2, :]
        with ExitStack() as first:
            ghi = sb("g_hi", [P, FT, T], F32R, first)
            glo = sb("g_lo", [P, FT, T], F32R, first)
            bt = sb("btab_sb", [P, HEADS, 3 * BLK], F32, first)
            q32 = sb("q_32", [P, QT, T], F32, first)
            k32 = sb("k_32", [P, T], F32, first)
            v32 = sb("v_32", [P, 2, P], F32, first)
            cc32 = sb("conv_c", [P, T], F32, first)
            u = sb("conv_u", [P, T + 2], F32, first)
            ya = sb("conv_ya", [P, T], F32, first)
            yb = sb("conv_yb", [P, T], F32, first)
            m32 = sb("mix_32", [P, 2, T], F32, first)
        with ExitStack() as second:
            yhi = sb("y_hi", [P, 16 * T], F32R, second)
            ylo = sb("y_lo", [P, 16 * T], F32R, second)
            kn = sb("k_heads", [P, 8, TM], F32, second)
            qn = sb("q_heads", [P, 8, T], F32, second)
            qp = sb("q_rope", [P, MH // 2, T], F32, second)
            V = sb("v_heads", [P, 3, D], F32, second)
            kp = sb("k_rope", [P, TM], F32, second)
            rel = sb("rel_bias", [P, 2, 6, GW], F32, second)
        QL0 = 2 * TM + P - META
        latw = {"kv": (0, TM), "ql": (QL0, T)}

        bank = [ctx.enter_context(nc.psum_tensor(f"bank{i}", [P, 512], F32)) for i in range(8)]
        SCORE, TRANS, OUT, SUM = 4, 5, 6, 7

        raw_full = [sem(f"raw_full{s}") for s in range(SLOTS)]
        hi_ready = [sem(f"hi_ready{s}") for s in range(SLOTS)]
        lo_ready = [sem(f"lo_ready{s}") for s in range(SLOTS)]
        w_used = [sem(f"w_used{s}") for s in range(SLOTS)]
        x_loaded, c_loaded, b_loaded = sem("x_loaded"), sem("c_loaded"), sem("b_loaded")
        const_set, pad_set = sem("const_set"), sem("pad_set")
        sq_done = [sem(f"sq_done{p}") for p in range(2)]
        sq_used = [sem(f"sq_used{p}") for p in range(2)]
        ln_done, rstd_done = sem("ln_done"), sem("rstd_done")
        h32_done, h_hi, h_lo = sem("h32_done"), sem("h_hi_done"), sem("h_lo_done")
        x_ready = [sem(f"x_ready{p}") for p in range(2)]
        silu_done = [sem(f"silu_done{p}") for p in range(2)]
        g_mul = [sem(f"g_mul{p}") for p in range(2)]
        g_hi = [sem(f"g_hi_done{p}") for p in range(2)]
        g_lo = [sem(f"g_lo_done{p}") for p in range(2)]
        qkv_done = sem("qkv_done")
        cc_done, u_done, y_step = sem("cc_done"), sem("u_done"), sem("y_step")
        m_done, mix_hi, mix_lo = sem("m_done"), sem("mix_hi"), sem("mix_lo")
        sc_done, s_add, mx_done, nm_done = sem("sc_done"), sem("s_add"), sem("mx_done"), sem("nm_done")
        exp_done, den_done, rec_done = sem("exp_done"), sem("den_done"), sem("rec_done")
        tr_done, pt_done, pv_done, o_done = sem("tr_done"), sem("pt_done"), sem("pv_done"), sem("o_done")
        ot_done = sem("ot_done")
        fx_done = sem("fx_done")
        pj_done, pj_taken = sem("pj_done"), sem("pj_taken")
        rot_done, rt_done, rope_done = sem("rot_done"), sem("rt_done"), sem("rope_done")
        rel_loaded = [sem(f"rel_loaded{p}") for p in range(2)]
        rel_ready = sem("rel_ready")
        gs_done, y_done, y_hi, y_lo = sem("gs_done"), sem("y_done"), sem("y_hi_done"), sem("y_lo_done")
        res_done, stored = sem("res_done"), sem("stored")

        block = ctx.enter_context(nc.Block())

        def uses(phase, i, layer, lap=0):
            ph = PHASES[phase]
            return ph.uses(i, lap) + layer * LAYER_USES[ph.slot(i)]

        def uses2(i):
            return LAYERS * LAYER_USES[i % SLOTS] + i // SLOTS + 1

        def wait_output(eng, outs, n):
            piece = outs[n][2]
            if ends_piece(outs, n):
                eng.wait_ge(w_used[piece % SLOTS], uses2(piece))
            else:
                eng.wait_ge(pj_done, mid_outputs(outs, n))

        C_LOADS = 16 * 6

        @block.sync
        def _(sp):
            sp.dma_start(x[:, :, 0:T], xT).then_inc(x_loaded, 16)

            def load(src, cols, slot, count):
                sp.wait_ge(lo_ready[slot], count - 1)
                sp.dma_start(raw[:, slot, 0:cols], src).then_inc(raw_full[slot], 16)

            def load_phase(name, l, ffn=None):
                ph = PHASES[name]

                def piece(i, j):
                    src = w8[l * W8_LAYER + (ph.w8 + i) + j * SLOTS] if ffn is None else \
                        wd[l * (2 * DN) + (ffn * DN + i) + j * SLOTS]
                    load(src, ph.cols, ph.slot(i), uses(name, i, l, j))

                with sp.Fori(0, ph.pieces // SLOTS) as j:
                    for r in range(SLOTS):
                        piece(r, j)
                for i in range(ph.pieces // SLOTS * SLOTS, ph.pieces):
                    piece(i, 0)

            with sp.Fori(0, LAYERS) as l:
                load_phase("gu1", l)
                load_phase("dn1", l, 0)
                load_phase("qkv", l)
                load_phase("conv", l)
                load_phase("wout", l)
                load_phase("gu2", l)
                load_phase("dn2", l, 1)
            with sp.Fori(0, SECOND // SLOTS) as j:
                for r in range(SLOTS):
                    load(w8[(LAYERS * W8_LAYER + r) + j * SLOTS], PT8, r, uses2(r) + j)
            for o in range(KT):
                sp.wait_ge(res_done, o + 1)
                sp.dma_start(out[o], x[:, o, 0:T]).then_inc(stored, 16)
            sp.wait_ge(stored, 16 * KT)

        @block.gpsimd
        def _(pool):
            pool.memset(ones[:], 1.0).then_inc(const_set, 1)
            pool.memset(u[:, 0:2], 0.0).then_inc(const_set, 1)
            pool.memset(hhi[:, KT * TM:].bitcast(F32), 0.0).then_inc(pad_set, 1)
            pool.memset(hlo[:, KT * TM:].bitcast(F32), 0.0).then_inc(pad_set, 1)
            pool.wait_ge(fx_done, KT)
            pool.memset(yhi[:, 2 * TM:QL0].bitcast(F32), 0.0).then_inc(pad_set, 1)
            pool.memset(ylo[:, 2 * TM:QL0].bitcast(F32), 0.0).then_inc(pad_set, 1)
            for h in range(NH):
                if h >= 2:
                    pool.wait_ge(s_add, LAYERS * HEADS + 2 * (2 * (h - 1)))
                pool.dma_start(rel[:, h % 2], relbias[h]).then_inc(rel_loaded[h % 2], 16)
                pool.wait_ge(rel_loaded[h % 2], 16 * (h // 2 + 1))
                if h == 0:
                    pool.wait_ge(c_loaded, C_LOADS)
                pool.tensor_tensor(rel[:, h % 2], rel[:, h % 2],
                                   cmask[:].unsqueeze(1).broadcast_to([P, 6, GW]), ALU.add).then_inc(rel_ready, 1)

        @block.scalar
        def _(act):
            act.dma_start(sml[:], small).then_inc(c_loaded, 16)
            act.dma_start(mat[:], mats).then_inc(c_loaded, 16)
            act.dma_start(rop[:], rope).then_inc(c_loaded, 16)
            act.dma_start(cmask[:], colmask).then_inc(c_loaded, 16)
            act.dma_start(metab[:], metabias).then_inc(c_loaded, 16)
            act.dma_start(x[:, :, T:TM], metaT).then_inc(c_loaded, 16)
            act.dma_start(bt[:], btab).then_inc(b_loaded, 16)

            def split(slot, cols, count):
                act.wait_ge(raw_full[slot], count * 16)
                act.wait_ge(w_used[slot], count - 1)
                act.activation(whi[:, slot, 0:cols], raw[:, slot, 0:cols], ACT.Copy).then_inc(hi_ready[slot], 1)

            def split_ahead(name, nxt, l, i, j=0, last=True):
                ph, t = PHASES[name], i + LEAD
                if last and t >= ph.pieces:
                    n, t = PHASES[nxt], t - ph.pieces
                    split(n.slot(t), n.cols, uses(nxt, t, l + 1 if nxt == "gu1" else l))
                else:
                    split(ph.slot(t), ph.cols, uses(name, t, l, j))

            def square(p, count, src):
                act.wait_ge(sq_used[p], count - 1)
                act.activation(sq[:, p, 0:src.shape[-1]], src, ACT.Square).then_inc(sq_done[p], 1)

            def rstd(total, slot, width, n, count):
                act.activation(lnv[:, slot, 0:n], total, ACT.Ln, scale=1.0 / width, bias=EPS).then_inc(ln_done, 1)
                act.wait_ge(ln_done, count)
                act.activation(rs[:, slot, 0:n], lnv[:, slot, 0:n], ACT.Exp, scale=-0.5).then_inc(rstd_done, 1)

            def norm(q, n=T, h=None):
                h = q if h is None else h
                act.wait_ge(sq_used[1], q * 4 + 4)
                rstd(bank[SUM][:, 0:n], 0, D, n, q + 1)
                for k in range(KT):
                    act.wait_ge(h32_done, h * KT + k + 1)
                    act.activation(hhi[:, k * TM:k * TM + n], h32[:, k % 4, 0:n], ACT.Copy).then_inc(h_hi, 1)

            def gate_up(name, nxt, l, w):
                n11 = l * (2 * HALF) + w * HALF
                act.preload_act_table(ACT.Silu)

                def lap(j, last):
                    for r in range(SLOTS):
                        i = r if not last else GU - SLOTS + r
                        p = r // 2
                        split_ahead(name, nxt, l, i, j, last)
                        if r % 2 == 0:
                            act.wait_ge(w_used[r], uses(name, i, l, j))
                            act.activation(sg[:, p], bank[2 * p][:, 0:T], ACT.Silu).then_inc(silu_done[p], 1)
                        else:
                            count = n11 + j + 1 + (HALF - 1 if last else 0)
                            act.wait_ge(g_mul[p], count)
                            f = j * 2 + p if not last else FT - 2 + p
                            act.activation(ghi[:, f, :], g32[:, p], ACT.Copy).then_inc(g_hi[p], 1)

                with act.Fori(0, GU // SLOTS - 1) as j:
                    lap(j, False)
                lap(0, True)

            def down(name, nxt, l, q):
                act.preload_act_table_set("natural_log_exp_and_others")

                def lap(j, last):
                    for r in range(SLOTS):
                        i = r if not last else DN - SLOTS + r
                        split_ahead(name, nxt, l, i, j, last)
                        if r % 2:
                            p, o2 = r // 2, j if not last else KT // 2 - 1
                            act.wait_ge(x_ready[p], (q * 4 - 4) + o2 + 1)
                            square(p, q * 4 + o2 + 1, x[:, o2 * 2 + p, 0:T])

                with act.Fori(0, DN // SLOTS - 1) as j:
                    lap(j, False)
                lap(0, True)

            def qkv(l):
                dst = [q32[:, j, :] for j in range(QT)] + [k32[:], v32[:].rearrange("p t c -> p (t c)")]
                for i in range(QKV):
                    split_ahead("qkv", "conv", l, i)
                    act.wait_ge(w_used[PHASES["qkv"].slot(i)], uses("qkv", i, l))
                    act.activation(dst[i], bank[i % 4][:, 0:T], ACT.Copy).then_inc(qkv_done, 1)

            def exp_first(l, h):
                act.wait_ge(nm_done, l * HEADS + h + 1)
                s = h % 2
                act.activation(Pr[:, s, 0:BLK], S[:, s, 0:BLK], ACT.Exp, bias=nm[:, 2 * h:2 * h + 1],
                               accum_out=sums[:, 2 * h:2 * h + 1])
                act.activation(Pr[:, s, BLK:3 * BLK], S[:, s, BLK:3 * BLK], ACT.Exp,
                               bias=nm[:, 2 * h + 1:2 * h + 2], accum_out=sums[:, 2 * h + 1:2 * h + 2])
                sink = sml[:, bass.ds(l * HEADS + (G_SINK + h), 1)]
                act.activation(es[:, 2 * h:2 * h + 2], nm[:, 2 * h:2 * h + 2], ACT.Exp, bias=sink)\
                   .then_inc(exp_done, 1)

            def pt_first(l, h):
                act.wait_ge(tr_done, l * HEADS + h + 1)
                act.activation(PT[:, h % 2], bank[TRANS][:, 0:3 * BLK], ACT.Copy).then_inc(pt_done, 1)

            def conv(l):
                for i in range(CONV):
                    if 0 <= i - 3 < HEADS:
                        pt_first(l, i - 3)
                    if 0 <= i - 1 < HEADS:
                        exp_first(l, i - 1)
                    split_ahead("conv", "wout", l, i)
                    jj, kind = i // 3, i % 3
                    if kind == 0:
                        act.wait_ge(w_used[PHASES["conv"].slot(i)], uses("conv", i, l))
                        act.wait_ge(u_done, l * CT + jj)
                        act.activation(cc32[:], bank[2][:, 0:T], ACT.Copy).then_inc(cc_done, 1)
                    elif kind == 2:
                        act.wait_ge(m_done, l * CT + jj + 1)
                        act.activation(ghi[:, 4 + jj, :], m32[:, jj % 2], ACT.Copy).then_inc(mix_hi, 1)
                for j in range(QT):
                    act.wait_ge(ot_done, l * QT + j + 1)
                    act.activation(ghi[:, j, :], bank[4 + j][:, 0:T], ACT.Copy).then_inc(mix_hi, 1)

            def wout(l, q):
                for o in range(KT):
                    if o < KT - LEAD:
                        split_ahead("wout", "gu2", l, o)
                    act.wait_ge(x_ready[o % 2], (q * 4 - 4) + o // 2 + 1)
                    square(o % 2, q * 4 + o // 2 + 1, x[:, o, 0:T])
                    if o >= KT - LEAD:
                        split_ahead("wout", "gu2", l, o)

            for i in range(LEAD):
                split(i, PT8, 1)
            act.preload_act_table_set("natural_log_exp_and_others")
            act.wait_ge(x_loaded, 16)
            for k in range(KT):
                square(k % 2, k // 2 + 1, x[:, k, 0:T])
            with act.Fori(0, LAYERS) as l:
                norm(l * 3)
                gate_up("gu1", "dn1", l, 0)
                down("dn1", "qkv", l, l * 3 + 1)
                norm(l * 3 + 1)
                qkv(l)
                conv(l)
                wout(l, l * 3 + 2)
                norm(l * 3 + 2)
                gate_up("gu2", "dn2", l, 1)
                down("dn2", "gu1", l, l * 3 + 3)
            act.preload_act_table_set("natural_log_exp_and_others")
            act.wait_ge(sq_used[1], 6 * 4 + 4)
            rstd(bank[SUM][:, 0:T], 0, D, T, 7)
            act.wait_ge(c_loaded, C_LOADS)
            for k in range(KT):
                act.wait_ge(fx_done, k + 1)
                square(k % 2, 7 * 4 + k // 2 + 1, x[:, k, :])
            norm(7, TM, 6)

            def split2(piece):
                if piece < SECOND:
                    split(piece % SLOTS, PT8, uses2(piece))

            def projections(outs, st):
                for n in range(len(outs) + 3):
                    g = st["done_at"].get(n - 2)
                    if g is not None and outs[st["groups"][g][0]][0] in latw:
                        for i in st["groups"][g]:
                            kind, k, _ = outs[i]
                            c = st["latent"][i]
                            act.wait_ge(h32_done, 7 * KT + c + 1)
                            off, wid = latw[kind]
                            act.activation(yhi[:, off + k * wid:off + (k + 1) * wid], h32[:, c, 0:wid],
                                           ACT.Copy).then_inc(h_hi, 1)
                    g = st["done_at"].get(n - 1)
                    if g is not None:
                        members = st["groups"][g]
                        kind = outs[members[0]][0]
                        m = st["normed"][members[-1]]
                        act.wait_ge(sq_used[m % 2], 32 + m // 2 + 1)
                        if g - st["g0"] >= 2:
                            act.wait_ge(pj_taken, st["n0"] + st["groups"][g - 2][-1] + 1)
                        rstd(bank[6 + g % 2][:, 0:TOKENS[kind]], g % 2, NORM_WIDTH[kind], TOKENS[kind], 8 + g + 1)
                    if n < len(outs):
                        for piece in st["pieces"][n]:
                            split2(piece + LEAD)
                        if n in st["normed"]:
                            kind = outs[n][0]
                            m = st["normed"][n]
                            wait_output(act, outs, n)
                            square(m % 2, 32 + m // 2 + 1, bank[n % 4][:, 0:TOKENS[kind]])

            def probs_T(v):
                act.wait_ge(tr_done, LAYERS * HEADS + v + 1)
                b = 2 + v % 2
                act.activation(PT[:, v % 2, 0:2 * BLK], bank[b][:, 0:2 * BLK], ACT.Copy)
                act.activation(PT[0:META, v % 2, 2 * BLK:3 * BLK], bank[b][0:META, 2 * BLK:3 * BLK],
                               ACT.Copy).then_inc(pt_done, 1)

            def attention(v0, units, scale, from_psum):
                for i in range(units + 2):
                    if i >= 2:
                        probs_T(v0 + i - 2)
                    if i < units:
                        v = v0 + i
                        act.wait_ge(nm_done, LAYERS * HEADS + v + 1)
                        src = bank[v % 2][:, 0:TM] if from_psum else S[:, v % 2, 0:TM]
                        act.activation(Pr[:, v % 2, 0:TM], src, ACT.Exp, bias=nm[:, v % 32:v % 32 + 1], scale=scale,
                                       accum_out=sums[:, v % 32:v % 32 + 1]).then_inc(exp_done, 1)

            def gates(piece0, y0):
                act.preload_act_table(ACT.Silu)
                for j in range(8):
                    y = y0 + j
                    split2(piece0 + j + LEAD)
                    act.wait_ge(w_used[(piece0 + j) % SLOTS], uses2(piece0 + j))
                    if y >= 2:
                        act.wait_ge(y_done, y - 1)
                    act.activation(sg[:, j % 2], bank[j % 4][:, 0:T], ACT.Silu).then_inc(gs_done, 1)
                    act.wait_ge(y_done, y + 1)
                    act.activation(yhi[:, y * T:(y + 1) * T], g32[:, j % 2], ACT.Copy).then_inc(y_hi, 1)

            projections(MLA, ST_MLA)
            attention(0, 2 * MH, MLA_SCALE, True)
            gates(MLA_PIECES, 0)
            act.preload_act_table_set("natural_log_exp_and_others")
            projections(NA, ST_NA)
            attention(2 * MH, 2 * NH, 1.0, False)
            gates(MLA_PIECES + 8 + NA_PIECES, 8)
            for i in range(SECOND - 16, SECOND):
                split2(i + LEAD)

        @block.vector
        def _(dve):
            def split(slot, cols, count):
                dve.wait_ge(hi_ready[slot], count)
                dve.tensor_tensor(wlo[:, slot, 0:cols], raw[:, slot, 0:cols],
                                  whi[:, slot, 0:cols].bitcast(F32), ALU.subtract).then_inc(lo_ready[slot], 1)

            def split_ahead(name, nxt, l, i, j=0, last=True):
                ph, t = PHASES[name], i + LEAD
                if last and t >= ph.pieces:
                    n, t = PHASES[nxt], t - ph.pieces
                    split(n.slot(t), n.cols, uses(nxt, t, l + 1 if nxt == "gu1" else l))
                else:
                    split(ph.slot(t), ph.cols, uses(name, t, l, j))

            def norm(q, n=T, h=None):
                h = q if h is None else h
                dve.wait_ge(rstd_done, q + 1)
                for k in range(KT + 1):
                    if k < KT:
                        dve.scalar_tensor_tensor(out=h32[:, k % 4, 0:n], in0=x[:, k, 0:n],
                                                 scalar=sml[:, bass.ds(q * KT + k, 1)], in1=rs[:, 0, 0:n],
                                                 op0=ALU.mult, op1=ALU.mult).then_inc(h32_done, 1)
                    if k > 0:
                        dve.wait_ge(h_hi, h * KT + k)
                        c = (k - 1) * TM
                        dve.tensor_tensor(hlo[:, c:c + n], h32[:, (k - 1) % 4, 0:n], hhi[:, c:c + n].bitcast(F32),
                                          ALU.subtract).then_inc(h_lo, 1)

            def gate_up(name, nxt, l, w):
                n11 = l * (2 * HALF) + w * HALF

                def lap(j, last):
                    for r in range(SLOTS):
                        i = r if not last else GU - SLOTS + r
                        p = r // 2
                        split_ahead(name, nxt, l, i, j, last)
                        if r % 2:
                            count = n11 + j + 1 + (HALF - 1 if last else 0)
                            dve.wait_ge(silu_done[p], count)
                            dve.wait_ge(w_used[r], uses(name, i, l, j))
                            dve.tensor_tensor(g32[:, p], bank[2 * p + 1][:, 0:T], sg[:, p], ALU.mult)\
                               .then_inc(g_mul[p], 1)
                            dve.wait_ge(g_hi[p], count)
                            f = j * 2 + p if not last else FT - 2 + p
                            dve.tensor_tensor(glo[:, f, :], g32[:, p], ghi[:, f, :].bitcast(F32), ALU.subtract)\
                               .then_inc(g_lo[p], 1)

                with dve.Fori(0, GU // SLOTS - 1) as j:
                    lap(j, False)
                lap(0, True)

            def down(name, nxt, l, q):
                def lap(j, last):
                    for r in range(SLOTS):
                        i = r if not last else DN - SLOTS + r
                        split_ahead(name, nxt, l, i, j, last)
                        if r % 2:
                            p, o2 = r // 2, j if not last else KT // 2 - 1
                            dve.wait_ge(w_used[r], uses(name, i, l, j))
                            xo = x[:, o2 * 2 + p, 0:T]
                            dve.scalar_tensor_tensor(out=xo, in0=bank[p][:, 0:T], scalar=0.5, in1=xo,
                                                     op0=ALU.mult, op1=ALU.add).then_inc(x_ready[p], 1)

                with dve.Fori(0, DN // SLOTS - 1) as j:
                    lap(j, False)
                lap(0, True)

            def qkv(l):
                for i in range(QKV):
                    split_ahead("qkv", "conv", l, i)

            def add_max(l, h):
                n, s = l * HEADS + h, h % 2
                dve.wait_ge(sc_done, n + 1)
                dve.scalar_tensor_tensor(out=S[:, s], in0=bank[SCORE][:, 0:3 * BLK], scalar=HD ** -0.5,
                                         in1=bt[:, h, :], op0=ALU.mult, op1=ALU.add).then_inc(s_add, 1)
                dve.wait_ge(s_add, n + 1)
                dve.reduce_max(mx[:, 2 * h:2 * h + 1], S[:, s, 0:BLK], AX_X)
                dve.reduce_max(mx[:, 2 * h + 1:2 * h + 2], S[:, s, BLK:3 * BLK], AX_X).then_inc(mx_done, 1)
                dve.wait_ge(mx_done, n + 1)
                sink = sml[:, bass.ds(l * HEADS + (G_SINK + h), 1)]
                dve.tensor_scalar(nm[:, 2 * h:2 * h + 2], mx[:, 2 * h:2 * h + 2], sink, -1.0, ALU.max, ALU.mult)\
                   .then_inc(nm_done, 1)

            def denominators(n, a, b, add_sink):
                dve.wait_ge(exp_done, n + 1)
                src = sums
                if add_sink:
                    dve.tensor_tensor(den[:, a:b], sums[:, a:b], es[:, a:b], ALU.add).then_inc(den_done, 1)
                    dve.wait_ge(den_done, n + 1)
                    src = den
                dve.reciprocal(rec[:, a:b], src[:, a:b]).then_inc(rec_done, 1)

            def out_first(l, h):
                n = l * HEADS + h
                dve.wait_ge(pv_done, n + 1)
                dve.wait_ge(rec_done, n + 1)
                col = (h % QT) * P + h // QT * HD
                for b in range(2):
                    o = dve.tensor_scalar(O32[:, b, col:col + HD], bank[OUT][:, b * HD:(b + 1) * HD],
                                          rec[:, 2 * h + b:2 * h + b + 1], None, ALU.mult)
                o.then_inc(o_done, 1)

            def conv(l):
                for i in range(CONV):
                    split_ahead("conv", "wout", l, i)
                    jj, kind = i // 3, i % 3
                    c = l * CT + jj
                    slot, count = PHASES["conv"].slot(i), uses("conv", i, l)
                    tap = [sml[:, bass.ds(l * (3 * CT) + (G_CONV + 3 * jj + t), 1)] for t in range(3)]
                    if kind == 1:
                        dve.wait_ge(w_used[slot], count)
                        dve.wait_ge(cc_done, c + 1)
                        dve.wait_ge(y_step, c * 3)
                        dve.tensor_tensor(u[:, 2:T + 2], bank[3][:, 0:T], cc32[:], ALU.mult).then_inc(u_done, 1)
                        dve.wait_ge(u_done, c + 1)
                        dve.tensor_scalar(ya[:], u[:, 2:T + 2], tap[2], None, ALU.mult).then_inc(y_step, 1)
                        dve.wait_ge(y_step, c * 3 + 1)
                        dve.scalar_tensor_tensor(out=yb[:], in0=u[:, 1:T + 1], scalar=tap[1], in1=ya[:],
                                                 op0=ALU.mult, op1=ALU.add).then_inc(y_step, 1)
                        dve.wait_ge(y_step, c * 3 + 2)
                        dve.scalar_tensor_tensor(out=ya[:], in0=u[:, 0:T], scalar=tap[0], in1=yb[:],
                                                 op0=ALU.mult, op1=ALU.add).then_inc(y_step, 1)
                    elif kind == 2:
                        dve.wait_ge(w_used[slot], count)
                        dve.wait_ge(y_step, c * 3 + 3)
                        dve.tensor_tensor(m32[:, jj % 2], bank[0][:, 0:T], ya[:], ALU.mult).then_inc(m_done, 1)
                        dve.wait_ge(mix_hi, l * 8 + jj + 1)
                        dve.tensor_tensor(glo[:, 4 + jj, :], m32[:, jj % 2], ghi[:, 4 + jj, :].bitcast(F32),
                                          ALU.subtract).then_inc(mix_lo, 1)
                    if 0 <= i - 1 < HEADS:
                        denominators(l * HEADS + i - 1, 2 * (i - 1), 2 * i, True)
                    if 0 <= i - 4 < HEADS:
                        out_first(l, i - 4)
                    if i < HEADS:
                        add_max(l, i)
                for j in range(QT):
                    dve.wait_ge(mix_hi, l * 8 + CT + j + 1)
                    dve.tensor_tensor(glo[:, j, :], bank[4 + j][:, 0:T], ghi[:, j, :].bitcast(F32),
                                      ALU.subtract).then_inc(mix_lo, 1)

            def wout(l, q):
                for o in range(KT):
                    if o < KT - LEAD:
                        split_ahead("wout", "gu2", l, o)
                    dve.wait_ge(w_used[PHASES["wout"].slot(o)], uses("wout", o, l))
                    xo = x[:, o, 0:T]
                    dve.tensor_tensor(xo, bank[o % 2][:, 0:T], xo, ALU.add).then_inc(x_ready[o % 2], 1)
                    if o >= KT - LEAD:
                        split_ahead("wout", "gu2", l, o)

            dve.wait_ge(c_loaded, C_LOADS)
            dve.wait_ge(b_loaded, 16)
            dve.wait_ge(const_set, 2)
            for i in range(LEAD):
                split(i, PT8, 1)
            dve.wait_ge(x_loaded, 16)
            with dve.Fori(0, LAYERS) as l:
                norm(l * 3)
                gate_up("gu1", "dn1", l, 0)
                down("dn1", "qkv", l, l * 3 + 1)
                norm(l * 3 + 1)
                qkv(l)
                conv(l)
                wout(l, l * 3 + 2)
                norm(l * 3 + 2)
                gate_up("gu2", "dn2", l, 1)
                down("dn2", "gu1", l, l * 3 + 3)
            dve.wait_ge(rstd_done, 7)
            for k in range(KT):
                dve.scalar_tensor_tensor(out=x[:, k, 0:T], in0=x[:, k, 0:T], scalar=sml[:, 6 * KT + k:6 * KT + k + 1],
                                         in1=rs[:, 0, 0:T], op0=ALU.mult, op1=ALU.mult).then_inc(fx_done, 1)
            dve.wait_ge(fx_done, KT)
            norm(7, TM, 6)

            def split2(piece):
                if piece < SECOND:
                    split(piece % SLOTS, PT8, uses2(piece))

            def normed_dst(kind, k, c):
                if kind in latw:
                    return h32[:, c, 0:TOKENS[kind]]
                if kind in ("kpe", "qpe"):
                    return S[:, c % 2, 0:TOKENS[kind]]
                return {"kn": kn, "nak": kn, "qn": qn, "naq": qn}[kind][:, k, :]

            def projections(outs, st):
                for n in range(len(outs) + 4):
                    i = n - 3
                    if i in st["ropes"]:
                        c, nt = st["ropes"][i], TOKENS[outs[i][0]]
                        dst = kp[:] if outs[i][0] == "kpe" else qp[:, outs[i][1], :]
                        dve.wait_ge(rot_done, c + 1)
                        if c > 0:
                            dve.wait_ge(rope_done, c)
                        dve.tensor_tensor(Pr[:, 0, 0:nt], bank[SCORE][:, 0:nt], rop[:, 1, 0:nt], ALU.mult)
                        dve.tensor_tensor(Pr[:, 1, 0:nt], S[:, c % 2, 0:nt], rop[:, 0, 0:nt], ALU.mult)\
                           .then_inc(rt_done, 1)
                        dve.wait_ge(rt_done, c + 1)
                        dve.tensor_tensor(dst, Pr[:, 0, 0:nt], Pr[:, 1, 0:nt], ALU.add).then_inc(rope_done, 1)
                    g = st["done_at"].get(n - 2)
                    if g is not None and outs[st["groups"][g][0]][0] in latw:
                        for i in st["groups"][g]:
                            kind, k, _ = outs[i]
                            c = st["latent"][i]
                            off, wid = latw[kind]
                            dve.wait_ge(h_hi, 7 * KT + c + 1)
                            dve.tensor_tensor(ylo[:, off + k * wid:off + (k + 1) * wid], h32[:, c, 0:wid],
                                              yhi[:, off + k * wid:off + (k + 1) * wid].bitcast(F32), ALU.subtract)\
                               .then_inc(pj_taken, 1)
                    g = st["done_at"].get(n - 1)
                    if g is not None:
                        dve.wait_ge(rstd_done, 8 + g + 1)
                        for i in st["groups"][g]:
                            kind, k, _ = outs[i]
                            c = st["latent"].get(i, st["ropes"].get(i))
                            if i in st["ropes"] and c >= 2:
                                dve.wait_ge(rope_done, c - 1)
                            gain = G_HEAD + HEAD_GAIN[kind] + (k if kind in latw else 0)
                            nt = TOKENS[kind]
                            ins = dve.scalar_tensor_tensor(
                                out=normed_dst(kind, k, c), in0=bank[i % 4][:, 0:nt], scalar=sml[:, gain:gain + 1],
                                in1=rs[:, g % 2, 0:nt], op0=ALU.mult, op1=ALU.mult)
                            if kind in latw:
                                ins.then_inc(h32_done, 1)
                            else:
                                ins.then_inc(pj_taken, 1)
                    if n < len(outs):
                        for piece in st["pieces"][n]:
                            split2(piece + LEAD)
                        kind, k, _ = outs[n]
                        if kind in ("uv", "nav"):
                            c, tt = divmod(k, 3)
                            np_ = P if tt < 2 else META
                            wait_output(dve, outs, n)
                            dve.tensor_copy(V[0:np_, tt, c * 512:(c + 1) * 512], bank[n % 4][0:np_, :])\
                               .then_inc(pj_taken, 1)

            def out_second(v, width, dst):
                dve.wait_ge(pv_done, LAYERS * HEADS + v + 1)
                dve.wait_ge(rec_done, LAYERS * HEADS + v + 1)
                dve.tensor_scalar(dst, bank[4 + v % 2][:, 0:width], rec[:, v % 32:v % 32 + 1], None, ALU.mult)\
                   .then_inc(o_done, 1)

            def attention(v0, units, width, mla):
                for i in range(units + 2):
                    if i < units:
                        v = v0 + i
                        h, t = i // 2, i % 2
                        c = v % 32
                        dve.wait_ge(sc_done, LAYERS * HEADS + v + 1)
                        if mla:
                            dve.reduce_max(mx[:, c:c + 1], bank[v % 2][:, 0:TM], AX_X).then_inc(mx_done, 1)
                        else:
                            if t == 0:
                                dve.wait_ge(rel_ready, h + 1)
                            if i >= 2:
                                dve.wait_ge(exp_done, LAYERS * HEADS + v - 1)
                            dve.scalar_tensor_tensor(
                                out=S[:, v % 2, 0:T], in0=bank[v % 2][:, 0:T], scalar=HD ** -0.5,
                                in1=rel[:, h % 2, 2 - 2 * t:6 - 2 * t, :].rearrange("p r c -> p (r c)"),
                                op0=ALU.mult, op1=ALU.add).then_inc(s_add, 1)
                            dve.scalar_tensor_tensor(
                                out=S[:, v % 2, T:TM], in0=bank[v % 2][:, T:TM], scalar=HD ** -0.5,
                                in1=metab[:, h, :], op0=ALU.mult, op1=ALU.add).then_inc(s_add, 1)
                            dve.wait_ge(s_add, LAYERS * HEADS + 2 * (i + 1))
                            dve.reduce_max(mx[:, c:c + 1], S[:, v % 2, 0:TM], AX_X).then_inc(mx_done, 1)
                        dve.wait_ge(mx_done, LAYERS * HEADS + v + 1)
                        dve.tensor_scalar(nm[:, c:c + 1], mx[:, c:c + 1], -(MLA_SCALE if mla else 1.0), None,
                                          ALU.mult).then_inc(nm_done, 1)
                    if i >= 1 and i <= units:
                        v = v0 + i - 1
                        denominators(LAYERS * HEADS + v, v % 32, v % 32 + 1, False)
                    if i >= 2:
                        h, t = (i - 2) // 2, (i - 2) % 2
                        out_second(v0 + i - 2, width, O32[:, t, h * width:(h + 1) * width])

            def gates(piece0, y0):
                for j in range(8):
                    y = y0 + j
                    split2(piece0 + j + LEAD)
                    dve.wait_ge(gs_done, y + 1)
                    dve.wait_ge(ot_done, LAYERS * QT + y + 1)
                    dve.tensor_tensor(g32[:, j % 2], bank[4 + j % 2][:, 0:T], sg[:, j % 2], ALU.mult)\
                       .then_inc(y_done, 1)
                    dve.wait_ge(y_hi, y + 1)
                    dve.tensor_tensor(ylo[:, y * T:(y + 1) * T], g32[:, j % 2],
                                      yhi[:, y * T:(y + 1) * T].bitcast(F32), ALU.subtract).then_inc(y_lo, 1)

            projections(MLA, ST_MLA)
            attention(0, 2 * MH, P, True)
            gates(MLA_PIECES, 0)
            projections(NA, ST_NA)
            attention(2 * MH, 2 * NH, HD, False)
            gates(MLA_PIECES + 8 + NA_PIECES, 8)
            for i in range(16):
                piece = SECOND - 16 + i
                split2(piece + LEAD)
                if i % 2:
                    o = i // 2
                    dve.wait_ge(w_used[piece % SLOTS], uses2(piece))
                    dve.tensor_tensor(x[:, o, 0:T], bank[o % 2][:, 0:T], x[:, o, 0:T], ALU.add)\
                       .then_inc(res_done, 1)

        @block.tensor
        def _(pe):
            def product(o, slot, t, xh, xl, first, last, n=P):
                h, lo = whi[:, slot, t * P:(t + 1) * P], wlo[:, slot, t * P:(t + 1) * P]
                pe.matmul(o, h, xh, start=first, stop=False)
                pe.matmul(o, h, xl, start=False, stop=False)
                return pe.matmul(o, lo, xh, start=False, stop=last)

            def hcols(k, n=T):
                return hhi[:, k * TM:k * TM + n], hlo[:, k * TM:k * TM + n]

            def tile8(o, slot, n=T):
                for k in range(KT):
                    mm = product(o, slot, k, *hcols(k, n), k == 0, k == KT - 1)
                mm.then_inc(w_used[slot], 1)

            def first_pair(o0, o1, slot0, slot1, q):
                for k in range(KT):
                    pe.wait_ge(h_lo, q * KT + k + 1)
                    a = product(o0, slot0, k, *hcols(k), k == 0, k == KT - 1)
                    b = product(o1, slot1, k, *hcols(k), k == 0, k == KT - 1)
                a.then_inc(w_used[slot0], 1)
                b.then_inc(w_used[slot1], 1)

            def sum_squares(p, count, first, last, n=T, total=SUM, lhs=None):
                pe.wait_ge(sq_done[p], count)
                pe.matmul(bank[total][:, 0:n], ones[:] if lhs is None else lhs, sq[:, p, 0:n], start=first, stop=last)\
                  .then_inc(sq_used[p], 1)

            def gate_up(name, l, w, q):
                n11 = l * (2 * HALF) + w * HALF

                def ready(r, j):
                    pe.wait_ge(lo_ready[r], uses(name, r, l, j))
                    pe.wait_ge(silu_done[r // 2] if r % 2 == 0 else g_mul[r // 2], n11 + j)

                ready(0, 0)
                ready(1, 0)
                first_pair(bank[0][:, 0:T], bank[1][:, 0:T], 0, 1, q)
                for r in (2, 3):
                    ready(r, 0)
                    tile8(bank[r][:, 0:T], r)
                with pe.Fori(1, GU // SLOTS) as j:
                    for r in range(SLOTS):
                        ready(r, j)
                        tile8(bank[r][:, 0:T], r)

            def down(name, l, w, q):
                n11 = l * (2 * HALF) + w * HALF

                def lap(j, first):
                    for r in range(SLOTS):
                        p, half = r // 2, r % 2
                        pe.wait_ge(lo_ready[r], uses(name, r, l, j))
                        if half == 0:
                            pe.wait_ge(x_ready[p], (q * 4 - 4) + j)
                        pe.wait_ge(g_lo[0], n11 + (HALF + 1) // 2 if half == 0 else n11 + HALF)
                        pe.wait_ge(g_lo[1], n11 + HALF // 2 if half == 0 else n11 + HALF)
                        for k in range(HALF):
                            f = half * HALF + k
                            mm = product(bank[p][:, 0:T], r, k, ghi[:, f, :], glo[:, f, :], f == 0, f == FT - 1)
                        mm.then_inc(w_used[r], 1)
                        if r == 1 and not first:
                            sum_squares(1, q * 4 + j, False, False)
                        if r == 3:
                            sum_squares(0, q * 4 + j + 1, first, False)

                pe.wait_ge(silu_done[0], n11 + HALF)
                lap(0, True)
                with pe.Fori(1, DN // SLOTS) as j:
                    lap(j, False)
                sum_squares(1, q * 4 + 4, False, True)

            def qkv(l, q):
                for i in range(2):
                    pe.wait_ge(lo_ready[PHASES["qkv"].slot(i)], uses("qkv", i, l))
                first_pair(bank[0][:, 0:T], bank[1][:, 0:T], 0, 1, q)
                for i in range(2, QKV):
                    slot = PHASES["qkv"].slot(i)
                    pe.wait_ge(lo_ready[slot], uses("qkv", i, l))
                    if i >= 4:
                        pe.wait_ge(qkv_done, l * QKV + i - 3)
                    if i < QKV - 1:
                        tile8(bank[i % 4][:, 0:T], slot)
                        continue
                    for t in range(2):
                        for k in range(KT):
                            xh, xl = (a[:, t * P:(t + 1) * P] for a in hcols(k))
                            wh, wl = whi[:, slot, k * P:(k + 1) * P], wlo[:, slot, k * P:(k + 1) * P]
                            o = bank[i % 4][:, t * P:(t + 1) * P]
                            pe.matmul(o, xh, wh, start=k == 0, stop=False)
                            pe.matmul(o, xl, wh, start=False, stop=False)
                            mm = pe.matmul(o, xh, wl, start=False, stop=k == KT - 1)
                    mm.then_inc(w_used[slot], 1)

            def scores_first(l, h):
                n, j, r = l * HEADS + h, h % QT, h // QT * HD
                pe.wait_ge(qkv_done, l * QKV + QKV - 1)
                pe.wait_ge(s_add, n)
                pe.matmul(bank[SCORE][:, 0:BLK], q32[r:r + HD, j, 0:BLK], k32[r:r + HD, 0:BLK], start=True, stop=True)
                pe.matmul(bank[SCORE][:, BLK:3 * BLK], q32[r:r + HD, j, BLK:T], k32[r:r + HD, :], start=True,
                          stop=True).then_inc(sc_done, 1)

            def transpose_first(l, h):
                n = l * HEADS + h
                pe.wait_ge(exp_done, n + 1)
                pe.wait_ge(pt_done, n)
                for b in range(3):
                    tr = pe.transpose(bank[TRANS][:, b * BLK:(b + 1) * BLK], Pr[:, h % 2, b * BLK:(b + 1) * BLK], ident)
                tr.then_inc(tr_done, 1)

            def pv_first(l, h):
                n, c = l * HEADS + h, h // QT * HD
                pe.wait_ge(qkv_done, l * QKV + QKV)
                pe.wait_ge(pt_done, n + 1)
                pe.wait_ge(o_done, n)
                pt = PT[:, h % 2]
                pe.matmul(bank[OUT][:, 0:HD], pt[:, 0:BLK], v32[:, 0, c:c + HD], start=True, stop=True)
                pe.matmul(bank[OUT][:, HD:2 * HD], pt[:, BLK:2 * BLK], v32[:, 0, c:c + HD], start=True, stop=False)
                pe.matmul(bank[OUT][:, HD:2 * HD], pt[:, 2 * BLK:3 * BLK], v32[:, 1, c:c + HD], start=False,
                          stop=True).then_inc(pv_done, 1)

            def conv(l):
                for i in range(CONV):
                    jj, kind = i // 3, i % 3
                    slot = PHASES["conv"].slot(i)
                    pe.wait_ge(lo_ready[slot], uses("conv", i, l))
                    if i == 0:
                        pe.wait_ge(qkv_done, l * QKV + QKV - 1)
                    pe.wait_ge([cc_done, u_done, m_done][kind], l * CT + jj)
                    tile8(bank[(2, 3, 0)[kind]][:, 0:T], slot)
                    if i < HEADS:
                        scores_first(l, i)
                    if 0 <= i - 2 < HEADS:
                        transpose_first(l, i - 2)
                    if 0 <= i - 3 < HEADS:
                        pv_first(l, i - 3)
                pe.wait_ge(o_done, (l + 1) * HEADS)
                for j in range(QT):
                    for t in range(2):
                        tr = pe.transpose(bank[4 + j][:, t * P:(t + 1) * P], O32[:, t, j * P:(j + 1) * P], ident)
                    tr.then_inc(ot_done, 1)

            order = list(range(QT, QT + CT)) + list(range(QT))

            def wout(l, q):
                for i in range(2):
                    slot = PHASES["wout"].slot(i)
                    pe.wait_ge(lo_ready[slot], uses("wout", i, l))
                pe.wait_ge(qkv_done, l * QKV + QKV)
                pe.wait_ge(m_done, (l + 1) * CT)
                s0, s1 = PHASES["wout"].slot(0), PHASES["wout"].slot(1)
                for n, k in enumerate(order):
                    pe.wait_ge(mix_lo, l * 8 + n + 1)
                    a = product(bank[0][:, 0:T], s0, k, ghi[:, k, :], glo[:, k, :], n == 0, n == KT - 1)
                    b = product(bank[1][:, 0:T], s1, k, ghi[:, k, :], glo[:, k, :], n == 0, n == KT - 1)
                a.then_inc(w_used[s0], 1)
                b.then_inc(w_used[s1], 1)
                for o in range(2, KT):
                    slot = PHASES["wout"].slot(o)
                    pe.wait_ge(lo_ready[slot], uses("wout", o, l))
                    pe.wait_ge(x_ready[o % 2], (q * 4 - 4) + o // 2)
                    for k in range(KT):
                        mm = product(bank[o % 2][:, 0:T], slot, k, ghi[:, k, :], glo[:, k, :], k == 0, k == KT - 1)
                    mm.then_inc(w_used[slot], 1)
                    sum_squares(o % 2, q * 4 + o // 2, o == 2, False)
                for o in (6, 7):
                    sum_squares(o % 2, q * 4 + o // 2 + 1, False, o == 7)

            pe.wait_ge(const_set, 2)
            pe.wait_ge(pad_set, 2)
            pe.wait_ge(c_loaded, C_LOADS)
            for k in range(KT):
                sum_squares(k % 2, k // 2 + 1, k == 0, k == KT - 1)
            with pe.Fori(0, LAYERS) as l:
                gate_up("gu1", l, 0, l * 3)
                down("dn1", l, 0, l * 3 + 1)
                qkv(l, l * 3 + 1)
                conv(l)
                wout(l, l * 3 + 2)
                gate_up("gu2", l, 1, l * 3 + 2)
                down("dn2", l, 1, l * 3 + 3)
            for k in range(KT):
                if k == 0:
                    pe.wait_ge(rstd_done, 7)
                sum_squares(k % 2, 7 * 4 + k // 2 + 1, k == 0, k == KT - 1, TM)

            def begin(piece):
                pe.wait_ge(lo_ready[piece % SLOTS], uses2(piece))

            def run(outs, n):
                kind, k, piece = outs[n]
                slot, last = piece % SLOTS, ends_piece(outs, n)
                o = bank[n % 4]
                if kind in ("kv", "kpe", "ql", "naq", "nak"):
                    begin(piece)
                    if piece == 0:
                        pe.wait_ge(h_lo, 7 * KT)
                    for i in range(KT):
                        mm = product(o[:, 0:TOKENS[kind]], slot, i, *hcols(i, TOKENS[kind]), i == 0, i == KT - 1)
                elif kind in ("kn", "qn", "qpe"):
                    src, wid = latw["kv" if kind == "kn" else "ql"]
                    if k % 4 == 0:
                        begin(piece)
                    if k == 0:
                        pe.wait_ge(pj_taken, 2 if kind == "kn" else 5)
                    for i in range(2):
                        c = src + i * wid
                        mm = product(o[:, 0:TOKENS[kind]], slot, 2 * (k % 4) + i, yhi[:, c:c + wid],
                                     ylo[:, c:c + wid], i == 0, i == 1)
                elif kind == "uv":
                    tt = k % 3
                    if tt == 0:
                        begin(piece)
                    if k == 0:
                        pe.wait_ge(pad_set, 4)
                    for i in range(2):
                        c = latw["kv"][0] + i * TM + tt * P
                        wh, wl = whi[:, slot, i * 512:(i + 1) * 512], wlo[:, slot, i * 512:(i + 1) * 512]
                        pe.matmul(o[:], yhi[:, c:c + P], wh, start=i == 0, stop=False)
                        pe.matmul(o[:], ylo[:, c:c + P], wh, start=False, stop=False)
                        mm = pe.matmul(o[:], yhi[:, c:c + P], wl, start=False, stop=i == 1)
                else:
                    tt = k % 3

                    def values(kp_, tile):
                        s = (piece - 3 + kp_) % SLOTS
                        for i in range(2):
                            c = (2 * kp_ + i) * TM + tile * P
                            b = bank[(n - tt + tile) % 4]
                            wh, wl = whi[:, s, i * 512:(i + 1) * 512], wlo[:, s, i * 512:(i + 1) * 512]
                            pe.matmul(b[:], hhi[:, c:c + P], wh, start=kp_ + i == 0, stop=False)
                            pe.matmul(b[:], hlo[:, c:c + P], wh, start=False, stop=False)
                            mm = pe.matmul(b[:], hhi[:, c:c + P], wl, start=False, stop=kp_ == 3 and i == 1)
                        return mm

                    if tt == 0:
                        for kp_ in range(3):
                            begin(piece - 3 + kp_)
                            for tile in range(3):
                                mm = values(kp_, tile)
                            mm.then_inc(w_used[(piece - 3 + kp_) % SLOTS], 1)
                        begin(piece)
                    mm = values(3, tt)
                mm.then_inc(w_used[slot] if last else pj_done, 1)

            def sums_of(outs, st, n):
                g = st["done_at"].get(n)
                if g is not None:
                    kind = outs[st["groups"][g][0]][0]
                    lhs = ones64 if NORM_WIDTH[kind] == 64 else ones[:]
                    if g - st["g0"] >= 2:
                        pe.wait_ge(rstd_done, 8 + g - 1)
                    for a, i in enumerate(st["groups"][g]):
                        m = st["normed"][i]
                        sum_squares(m % 2, 32 + m // 2 + 1, a == 0, i == st["groups"][g][-1], TOKENS[kind],
                                    6 + g % 2, lhs)

            def projections(outs, st):
                for n in range(len(outs) + 3):
                    if n < len(outs) and outs[n][0] == "nav":
                        sums_of(outs, st, n - 1)
                    if n < len(outs):
                        ahead = 2 if outs[n][0] == "nav" and outs[n][1] % 3 == 0 else 0
                        if n + ahead >= 4:
                            pe.wait_ge(pj_taken, st["n0"] + n + ahead - 3)
                        run(outs, n)
                    if n >= len(outs) or outs[n][0] != "nav":
                        sums_of(outs, st, n - 1)
                    i = n - 2
                    if i in st["ropes"]:
                        c, nt = st["ropes"][i], TOKENS[outs[i][0]]
                        pe.wait_ge(pj_taken, st["n0"] + i + 1)
                        if c >= 1:
                            pe.wait_ge(rt_done, c)
                        pe.matmul(bank[SCORE][:, 0:nt], rot, S[:, c % 2, 0:nt], start=True, stop=True)\
                          .then_inc(rot_done, 1)

            def transposes(v):
                pe.wait_ge(exp_done, LAYERS * HEADS + v + 1)
                pe.wait_ge(pt_done, LAYERS * HEADS + v - 1)
                o, pr = bank[2 + v % 2], Pr[:, v % 2]
                pe.transpose(o[:, 0:BLK], pr[:, 0:BLK], ident)
                pe.transpose(o[:, BLK:2 * BLK], pr[:, BLK:2 * BLK], ident)
                pe.transpose(o[0:META, 2 * BLK:3 * BLK], pr[:, 2 * BLK:TM], ident).then_inc(tr_done, 1)

            def values_of(v, h, width):
                pe.wait_ge(pt_done, LAYERS * HEADS + v + 1)
                pe.wait_ge(o_done, LAYERS * HEADS + v - 1)
                o, pt = bank[4 + v % 2][:, 0:width], PT[:, v % 2]
                c = slice(h * width, (h + 1) * width)
                pe.matmul(o, pt[:, 0:BLK], V[:, 0, c], start=True, stop=False)
                pe.matmul(o, pt[:, BLK:2 * BLK], V[:, 1, c], start=False, stop=False)
                pe.matmul(o, pt[0:META, 2 * BLK:3 * BLK], V[0:META, 2, c], start=False, stop=True)\
                  .then_inc(pv_done, 1)

            def attention(v0, units, width, mla):
                for i in range(units + 3):
                    if i < units:
                        v, h, t = v0 + i, i // 2, i % 2
                        if i >= 2:
                            if mla:
                                pe.wait_ge(exp_done, LAYERS * HEADS + v - 1)
                            else:
                                pe.wait_ge(s_add, LAYERS * HEADS + 2 * (i - 1))
                        o, tok = bank[v % 2][:, 0:TM], slice(t * P, (t + 1) * P)
                        if mla:
                            r = h % 2 * MR
                            pe.matmul(o, qn[:, h, tok], kn[:, h, :], start=True, stop=False)
                            pe.matmul(o, qp[r:r + MR, h // 2, tok], kp[r:r + MR, :], start=False, stop=True)\
                              .then_inc(sc_done, 1)
                        else:
                            r = h % 2 * HD
                            pe.matmul(o, qn[r:r + HD, h // 2, tok], kn[r:r + HD, h // 2, :], start=True, stop=True)\
                              .then_inc(sc_done, 1)
                    if 1 <= i <= units:
                        transposes(v0 + i - 1)
                    if 2 <= i <= units + 1:
                        values_of(v0 + i - 2, (i - 2) // 2, width)

            def gates(piece0, y0):
                for j in range(8):
                    y, slot = y0 + j, (piece0 + j) % SLOTS
                    begin(piece0 + j)
                    if j >= 4:
                        pe.wait_ge(gs_done, y - 3)
                    tile8(bank[j % 4][:, 0:T], slot)
                    if j == 0:
                        pe.wait_ge(o_done, LAYERS * HEADS + 2 * MH + (2 * NH if y0 else 0))
                    if j >= 2:
                        pe.wait_ge(y_done, y - 1)
                    for t in range(2):
                        tr = pe.transpose(bank[4 + j % 2][:, t * P:(t + 1) * P], O32[:, t, j * P:(j + 1) * P], ident)
                    tr.then_inc(ot_done, 1)

            projections(MLA, ST_MLA)
            pe.wait_ge(rope_done, 1 + MH // 2)
            pe.wait_ge(pj_taken, len(MLA))
            attention(0, 2 * MH, P, True)
            gates(MLA_PIECES, 0)
            pe.wait_ge(gs_done, 8)
            projections(NA, ST_NA)
            pe.wait_ge(pj_taken, len(MLA) + len(NA))
            pe.wait_ge(y_done, 8)
            attention(2 * MH, 2 * NH, HD, False)
            gates(MLA_PIECES + 8 + NA_PIECES, 8)
            pe.wait_ge(gs_done, 16)
            for i in range(16):
                piece, o, half = SECOND - 16 + i, i // 2, i % 2
                begin(piece)
                if half == 0 and o >= 2:
                    pe.wait_ge(res_done, o - 1)
                for k in range(KT):
                    y = half * KT + k
                    if o == 0:
                        pe.wait_ge(y_lo, y + 1)
                    mm = product(bank[o % 2][:, 0:T], piece % SLOTS, k, yhi[:, y * T:(y + 1) * T],
                                 ylo[:, y * T:(y + 1) * T], y == 0, y == 2 * KT - 1)
                mm.then_inc(w_used[piece % SLOTS], 1)


def ends_piece(outs, n):
    return n + 1 == len(outs) or outs[n + 1][2] != outs[n][2]


def mid_outputs(outs, n):
    before = 0 if outs is MLA else sum(not ends_piece(MLA, i) for i in range(len(MLA)))
    return before + sum(not ends_piece(outs, i) for i in range(n + 1))


def structure(outs, n0, g0, m0, base):
    st = {"n0": n0, "g0": g0, "groups": {}, "done_at": {}, "normed": {}, "latent": {}, "ropes": {}, "pieces": {}}
    g, seen = g0, base
    for n, (kind, k, piece) in enumerate(outs):
        st["pieces"][n] = list(range(seen, piece + 1))
        seen = piece + 1
        if kind in NORM_WIDTH:
            st["normed"][n] = m0 + len(st["normed"])
            if kind in ("kv", "ql"):
                st["latent"][n] = len(st["latent"])
            if kind in ("kpe", "qpe"):
                st["ropes"][n] = len(st["ropes"])
            st["groups"].setdefault(g, []).append(n)
            if kind not in ("kv", "ql") or k == 1:
                st["done_at"][n] = g
                g += 1
    return st


MLA, NA = mla_outputs(), na_outputs()
ST_MLA = structure(MLA, 0, 0, 0, 0)
ST_NA = structure(NA, len(MLA), len(ST_MLA["groups"]), len(ST_MLA["normed"]), MLA_PIECES + 8)
MLA_SCALE = float(np.float32((MN + MR) ** -0.5))


def tiles(w):
    k, n = w.shape
    return w.reshape(k // P, P, n // P, P).transpose(0, 2, 1, 3)


def by_output(w):
    t = tiles(w)
    kt, nt = t.shape[:2]
    t = t.transpose(1, 0, 2, 3).reshape(nt * (kt // 8), 8, P, P)
    return t.transpose(0, 2, 1, 3).reshape(-1, P, PT8)


def short_k(w):
    t = tiles(w).transpose(1, 0, 2, 3)
    return t.reshape(-1, 8, P, P).transpose(0, 2, 1, 3).reshape(-1, P, PT8)


def by_columns(w):
    k, n = w.shape
    t = w.reshape(k // (2 * P), 2, P, n // 512, 512).transpose(3, 0, 2, 1, 4)
    return t.reshape(-1, P, PT8)


def kernel(**inputs):
    import concourse.bacc as bacc
    from concourse.bass_utils import run_bass_kernel_spmd

    a = {k: np.asarray(v) for k, v in inputs.items()}
    heads = np.arange(HEADS).reshape(2, QT).T.reshape(-1)
    hcol = (heads[:, None] * HD + np.arange(HD)[None]).reshape(-1)
    pieces, downs = [], []
    for l in range(LAYERS):
        def ffn(name):
            g, up = by_output(a[name + "_wg"][l]), by_output(a[name + "_wu"][l])
            pieces.append(np.stack([g, up], 1).reshape(-1, P, PT8))
            d = tiles(a[name + "_wd"][l]).transpose(1, 0, 2, 3).reshape(DN, HALF, P, P)
            downs.append(d.transpose(0, 2, 1, 3).reshape(DN, P, PTD))

        ffn("ffn1")
        w = a["w_in"][l]
        attn = HEADS * HD
        qkv = np.concatenate([w[:, 0:attn][:, hcol], w[:, attn:attn + 2 * P]], 1)
        cb, cc, ch = (w[:, attn + 2 * P + i * 512:attn + 2 * P + (i + 1) * 512] for i in range(3))
        pieces.append(by_output(qkv))
        pieces.append(np.stack([by_output(cc), by_output(ch), by_output(cb)], 1).reshape(-1, P, PT8))
        wo = a["w_out"][l]
        pieces.append(by_output(np.concatenate([wo[0:attn][hcol], wo[attn:]], 0)))
        ffn("ffn2")
    w = a["w_in_2"][0]
    cut = np.cumsum([0, 256, 256, MR, D, D, D, D, D])
    qlat, kvlat, kpe, gmla, naq, nak, nav, gna = (w[:, cut[i]:cut[i + 1]] for i in range(8))
    ukv = a["w_ukv_2"][0].reshape(256, MH, 2, P)
    uq = a["w_uq_2"][0].reshape(256, MH, MN + MR)
    pieces += [by_output(kvlat), by_output(np.concatenate([kpe, kpe], 1)), by_output(qlat),
               short_k(ukv[:, :, 0].reshape(256, -1)), by_columns(ukv[:, :, 1].reshape(256, -1)),
               short_k(uq[:, :, 0:MN].reshape(256, -1)), short_k(uq[:, :, MN:].reshape(256, -1)),
               by_output(gmla), by_output(naq), by_output(nak), by_columns(nav), by_output(gna),
               by_output(a["w_out_2"][0])]
    w8, wd = np.concatenate(pieces, 0), np.concatenate(downs, 0)

    def cols(v):
        return v.reshape(-1, P).T

    def twice(v):
        return np.concatenate([v, v])[:, None]

    norms = [a[n][l] for l in range(LAYERS) for n in ("ffn1_norm", "mix_norm", "ffn2_norm")]
    norms += [a["final_norm"], a["norm_w_2"][0]]
    conv = a["conv_w"].reshape(LAYERS, 3, CT, P).transpose(3, 0, 2, 1).reshape(P, -1)
    small = np.concatenate(
        [cols(np.concatenate(norms)), conv, np.broadcast_to(a["attn_sink"].reshape(1, -1), (P, LAYERS * HEADS)),
         cols(a["kv_lat_norm_w_2"][0]), cols(a["q_lat_norm_w_2"][0]), cols(a["mla_kn_w_2"][0]), cols(a["mla_qn_w_2"][0]),
         twice(a["mla_kpe_w_2"][0]), twice(a["mla_qpe_w_2"][0]), twice(a["na_q_norm_w_2"][0]),
         twice(a["na_k_norm_w_2"][0])], 1)

    f = np.float32
    i = np.arange(P)
    same = (i[:, None] // 64 == i[None] // 64)
    swap = same & (i[:, None] % 64 == (i[None] + 32) % 64)
    mats = np.stack([np.eye(P), same, np.where(swap, np.where(i[None] % 64 < 32, -1, 1), 0)], 1).astype(f)
    qi, kj = np.arange(BLK)[:, None], np.arange(2 * BLK)[None]
    dist = qi + BLK - kj
    slopes = np.exp2(-8.0 * np.arange(1, HEADS + 1, dtype=f) / HEADS).astype(f)
    band = np.where((dist >= 0) & (dist < BLK), -slopes[:, None, None] * dist.astype(f), f(MASKED)).astype(f)
    btab = np.concatenate([band[:, :, BLK:], band], 2).transpose(1, 0, 2)
    pos = np.concatenate([np.arange(META, TM), np.arange(META)]).astype(f)
    freq = (f(10000.0) ** -(np.arange(0, MR, 2, dtype=f) / f(MR))).astype(f)
    ang = (pos[None] * freq[i % 32][:, None]).astype(f)
    rope = np.stack([np.cos(ang), np.sin(ang)], 1).astype(f)
    c = np.arange(GW)
    c0 = np.clip(c - WC // 2, 0, GW - WC)[:, None]
    mask = np.where((c[None] >= c0) & (c[None] < c0 + WC), 0, MASKED).astype(f)
    bias = a["na_rel_bias_2"][0].reshape(NH, -1)
    at = [((np.arange(6)[None, :, None] + 5 - half) * RELC + WC - 1 + c[None, None, :] - c[:, None, None])
          for half in range(2)]
    rel = bias[:, np.concatenate(at, 0)]
    arrays = {
        "in_xT": a["x"][0].T.reshape(KT, P, T).transpose(1, 0, 2),
        "in_metaT": a["meta_tokens_2"].T.reshape(KT, P, META).transpose(1, 0, 2),
        "in_w8": w8, "in_wd": wd, "in_small": small, "in_mats": mats, "in_btab": btab, "in_rope": rope,
        "in_colmask": np.concatenate([mask, mask], 0),
        "in_metabias": np.broadcast_to(a["na_meta_bias_2"][0][None], (P, NH, META)),
        "in_relbias": rel,
    }
    arrays = {k: np.ascontiguousarray(v) for k, v in arrays.items()}
    nc = bacc.Bacc("TRN2", target_bir_lowering=False, num_devices=1)
    args = [nc.dram_tensor(k, v.shape, F32, kind="ExternalInput").ap() for k, v in arrays.items()]
    out = nc.dram_tensor("out_T", (KT, P, T), F32, kind="ExternalOutput").ap()
    build(nc, *args, out)
    r = run_bass_kernel_spmd(nc, [arrays], core_ids=[0])
    return r.results[0]["out_T"].reshape(1, D, T).transpose(0, 2, 1)
```

```python
from contextlib import ExitStack

import numpy as np
import concourse.bass as bass
from concourse import mybir

F32 = mybir.dt.float32
F32R = mybir.dt.float32r
ACT = mybir.ActivationFunctionType
ALU = mybir.AluOpType
AX_X = mybir.AxisListType.X

P = 128
D = 1024
KT = D // P
T = 256
META = 16
TM = T + META
LAYERS = 2
FF = 2816
FT = FF // P
EPS = 1e-6
MASKED = -1e30
HEADS, HD, BLK = 8, 64, 128
QT = HEADS * HD // P
CT = 4
MH, MN, MR = 8, 128, 64
NH = 16
GW, WR, WC = 64, 4, 16
RELR, RELC = 15, 31
SLOTS = 4
PRIME = 1
LEAD = SLOTS - 1
PT8 = 8 * P
HALF = FT // 2
PTD = HALF * P
GU, DN, QKV, CONV, WOUT = 2 * FT, 2 * KT, QT + 2, 3 * CT, KT
W8_LAYER = 2 * GU + QKV + CONV + WOUT


def slot_uses(pieces, start=0):
    return [len(range((s - start) % SLOTS, pieces, SLOTS)) for s in range(SLOTS)]


class Phase:

    def __init__(self, pieces, start, before, w8, cols):
        self.pieces, self.start, self.before, self.w8, self.cols = pieces, start, before, w8, cols

    def slot(self, i):
        return (self.start + i) % SLOTS

    def uses(self, i, lap=0):
        return self.before[self.slot(i)] + i // SLOTS + 1 + lap


def plan_layer():
    phases, before, w8 = {}, [0] * SLOTS, 0
    for name, pieces, start, cols in (
        ("gu1", GU, 0, PT8), ("dn1", DN, 0, PTD), ("qkv", QKV, 0, PT8), ("conv", CONV, QKV % SLOTS, PT8),
        ("wout", WOUT, (QKV + CONV) % SLOTS, PT8), ("gu2", GU, 0, PT8), ("dn2", DN, 0, PTD),
    ):
        phases[name] = Phase(pieces, start, list(before), w8, cols)
        before = [b + u for b, u in zip(before, slot_uses(pieces, start))]
        if cols == PT8:
            w8 += pieces
    return phases, before


PHASES, LAYER_USES = plan_layer()

MLA_PIECES = 2 + 1 + 2 + 2 + 2 + 2 + 1 + 8
NA_PIECES = 24
FILL = 8 + 8
FILL0 = MLA_PIECES + NA_PIECES
SECOND = FILL0 + FILL + 8


def mla_outputs():
    outs, piece = [], 0
    for kinds in ([("kv", 0)], [("kv", 1)], [("kpe", 0)], [("ql", 0)], [("ql", 1)], [("gate", 0)],
                  [("uv", t) for t in range(3)], [("kn", h) for h in range(4)], [("gate", 1)],
                  [("kn", h) for h in range(4, 8)], [("gate", 2)], [("uv", 3 + t) for t in range(3)],
                  [("qn", h) for h in range(4)], [("gate", 3)], [("qn", h) for h in range(4, 8)], [("gate", 4)],
                  [("qpe", j) for j in range(MH // 2)], [("gate", 5)], [("gate", 6)], [("gate", 7)]):
        outs += [(kind, k, piece) for kind, k in kinds]
        piece += 1
    return outs


def na_outputs():
    base = MLA_PIECES
    outs = [("naq", j, base + j) for j in range(8)]
    outs += [("nak", j, base + 8 + j) for j in range(8)]
    outs += [("nav", 3 * c + t, base + 16 + 4 * c + 3) for c in range(2) for t in range(3)]
    return outs


LAG = 1
NORM_WIDTH = {"kv": 256, "kpe": 64, "ql": 256, "kn": 128, "qn": 128, "qpe": 64, "naq": 64, "nak": 64}
TOKENS = {"kv": TM, "kpe": TM, "ql": T, "kn": TM, "qn": T, "qpe": T, "naq": T, "nak": TM, "gate": T}

G_NORM = 0
G_CONV = G_NORM + 8 * KT
G_SINK = G_CONV + LAYERS * CT * 3
G_HEAD = G_SINK + LAYERS * HEADS
HEAD_GAIN = {"kv": 0, "ql": 2, "kn": 4, "qn": 5, "kpe": 6, "qpe": 7, "naq": 8, "nak": 9}
SMALL = G_HEAD + 10


def build(nc, xT, metaT, w8, wd, small, mats, btab, rope, colmask, metabias, relbias, out):
    with ExitStack() as ctx:
        def sem(name):
            return ctx.enter_context(nc.semaphore(name))

        def sb(name, shape, dt=F32, stack=ctx):
            return stack.enter_context(nc.sbuf_tensor(name, shape, dt))

        x = sb("x_res", [P, KT, TM])
        raw = sb("w_raw", [P, SLOTS, PTD])
        whi = sb("w_hi", [P, SLOTS, PTD], F32R)
        wlo = sb("w_lo", [P, SLOTS, PTD], F32R)
        hhi = sb("h_hi", [P, KT * TM + P - META], F32R)
        hlo = sb("h_lo", [P, KT * TM + P - META], F32R)
        sq = sb("squares", [P, 2, TM])
        h32 = sb("h_32", [P, 4, TM])
        sg = sb("silu_gate", [P, 2, T])
        g32 = sb("gated_32", [P, 2, T])
        lnv = sb("ln_mean", [P, 2, TM])
        rs = sb("rstd", [P, 2, TM])
        S = sb("scores_sb", [P, 2, 3 * BLK])
        Pr = sb("probs", [P, 2, 3 * BLK])
        PT = sb("probs_T", [P, 2, 3 * BLK])
        O32 = sb("attn_out", [P, 2, D])
        sml = sb("small_sb", [P, SMALL])
        mat = sb("mats_sb", [P, 3, P])
        ones = sb("ones_sb", [P, P])
        rop = sb("rope_sb", [P, 2, TM])
        cmask = sb("colmask_sb", [P, GW])
        metab = sb("metabias_sb", [P, NH, META])
        mx = sb("row_max", [P, 2 * NH])
        nm = sb("neg_max", [P, 2 * NH])
        sums = sb("row_sums", [P, 2 * NH])
        es = sb("sink_terms", [P, 2 * HEADS])
        den = sb("denominators", [P, 2 * NH])
        rec = sb("reciprocals", [P, 2 * NH])
        ident, ones64, rot = mat[:, 0, :], mat[:, 1, :], mat[:, 2, :]
        with ExitStack() as first:
            ghi = sb("g_hi", [P, FT, T], F32R, first)
            glo = sb("g_lo", [P, FT, T], F32R, first)
            bt = sb("btab_sb", [P, HEADS, 3 * BLK], F32, first)
            q32 = sb("q_32", [P, QT, T], F32, first)
            k32 = sb("k_32", [P, T], F32, first)
            v32 = sb("v_32", [P, 2, P], F32, first)
            cc32 = sb("conv_c", [P, T], F32, first)
            u = sb("conv_u", [P, T + 2], F32, first)
            ya = sb("conv_ya", [P, T], F32, first)
            yb = sb("conv_yb", [P, T], F32, first)
            m32 = sb("mix_32", [P, 2, T], F32, first)
        with ExitStack() as second:
            yhi = sb("y_hi", [P, 16 * T], F32R, second)
            ylo = sb("y_lo", [P, 16 * T], F32R, second)
            kn = sb("k_heads", [P, 8, TM], F32, second)
            qn = sb("q_heads", [P, 8, T], F32, second)
            qp = sb("q_rope", [P, MH // 2, T], F32, second)
            V = sb("v_heads", [P, 3, D], F32, second)
            kp = sb("k_rope", [P, TM], F32, second)
            sgate = sb("silu_all", [P, 8, T], F32, second)
            rel = sb("rel_bias", [P, 2, 6, GW], F32, second)
        QL0 = 2 * TM + P - META
        latw = {"kv": (0, TM), "ql": (QL0, T)}

        bank = [ctx.enter_context(nc.psum_tensor(f"bank{i}", [P, 512], F32)) for i in range(8)]
        SCORE, TRANS, OUT, SUM = 4, 5, 6, 7

        raw_full = [sem(f"raw_full{s}") for s in range(SLOTS)]
        hi_ready = [sem(f"hi_ready{s}") for s in range(SLOTS)]
        lo_ready = [sem(f"lo_ready{s}") for s in range(SLOTS)]
        w_used = [sem(f"w_used{s}") for s in range(SLOTS)]
        x_loaded = [sem(f"x_loaded{p}") for p in range(2)]
        g_loaded = sem("g_loaded")
        c_loaded, b_loaded = sem("c_loaded"), sem("b_loaded")
        const_set, pad_set = sem("const_set"), sem("pad_set")
        sq_done = [sem(f"sq_done{p}") for p in range(2)]
        sq_used = [sem(f"sq_used{p}") for p in range(2)]
        ln_done, rstd_done = sem("ln_done"), sem("rstd_done")
        h32_done, h_hi, h_lo = sem("h32_done"), sem("h_hi_done"), sem("h_lo_done")
        x_ready = [sem(f"x_ready{p}") for p in range(2)]
        silu_done = [sem(f"silu_done{p}") for p in range(2)]
        g_mul = [sem(f"g_mul{p}") for p in range(2)]
        g_hi = [sem(f"g_hi_done{p}") for p in range(2)]
        g_lo = [sem(f"g_lo_done{p}") for p in range(2)]
        qkv_done = sem("qkv_done")
        cc_done, u_done, y_step = sem("cc_done"), sem("u_done"), sem("y_step")
        m_done, mix_hi, mix_lo = sem("m_done"), sem("mix_hi"), sem("mix_lo")
        sc_done, s_add, mx_done, nm_done = sem("sc_done"), sem("s_add"), sem("mx_done"), sem("nm_done")
        exp_done, den_done, rec_done = sem("exp_done"), sem("den_done"), sem("rec_done")
        tr_done, pt_done, pv_done, o_done = sem("tr_done"), sem("pt_done"), sem("pv_done"), sem("o_done")
        ot_done = sem("ot_done")
        fx_done = sem("fx_done")
        pj_done, pj_taken = sem("pj_done"), sem("pj_taken")
        rot_done, rt_done, rope_done = sem("rot_done"), sem("rt_done"), sem("rope_done")
        rel_loaded = [sem(f"rel_loaded{p}") for p in range(2)]
        rel_ready = sem("rel_ready")
        silu_all = sem("silu_all_done")
        th_done = sem("th_done")
        fill_taken = sem("fill_taken")
        y_done, y_hi, y_lo = sem("y_done"), sem("y_hi_done"), sem("y_lo_done")
        res_done, stored = sem("res_done"), sem("stored")

        block = ctx.enter_context(nc.Block())

        def uses(phase, i, layer, lap=0):
            ph = PHASES[phase]
            return layer * LAYER_USES[ph.slot(i)] + lap + (ph.uses(i) + PRIME)

        def uses0(n):
            return n + PRIME

        def uses2(i):
            return LAYERS * LAYER_USES[i % SLOTS] + i // SLOTS + (1 + PRIME)

        def wait_output(eng, outs, n):
            piece = outs[n][2]
            if ends_piece(outs, n):
                eng.wait_ge(w_used[piece % SLOTS], uses2(piece))
            else:
                eng.wait_ge(pj_done, mid_outputs(outs, n))

        C_LOADS = 16 * 5

        @block.sync
        def _(sp):
            for s in raw_full:
                sp.sem_inc(s, 16 * PRIME)
            for p in range(2):
                half = slice(p * KT // 2, (p + 1) * KT // 2)
                sp.dma_start(x[:, half, 0:T], xT[:, half]).then_inc(x_loaded[p], 16)

            def load(src, cols, slot, count):
                sp.wait_ge(lo_ready[slot], count - 1)
                sp.dma_start(raw[:, slot, 0:cols], src).then_inc(raw_full[slot], 16)

            def load_phase(name, l, ffn=None):
                ph = PHASES[name]

                def piece(i, j):
                    src = w8[l * W8_LAYER + (ph.w8 + i) + j * SLOTS] if ffn is None else \
                        wd[l * (2 * DN) + (ffn * DN + i) + j * SLOTS]
                    load(src, ph.cols, ph.slot(i), uses(name, i, l, j))

                with sp.Fori(0, ph.pieces // SLOTS) as j:
                    for r in range(SLOTS):
                        piece(r, j)
                for i in range(ph.pieces // SLOTS * SLOTS, ph.pieces):
                    piece(i, 0)

            with sp.Fori(0, LAYERS) as l:
                load_phase("gu1", l)
                load_phase("dn1", l, 0)
                load_phase("qkv", l)
                load_phase("conv", l)
                load_phase("wout", l)
                load_phase("gu2", l)
                load_phase("dn2", l, 1)
            with sp.Fori(0, SECOND // SLOTS) as j:
                for r in range(SLOTS):
                    load(w8[(LAYERS * W8_LAYER + r) + j * SLOTS], PT8, r, uses2(r) + j)
            for o in range(KT):
                sp.wait_ge(res_done, o + 1)
                sp.dma_start(out[o], x[:, o, 0:T]).then_inc(stored, 16)
            sp.wait_ge(stored, 16 * KT)

        @block.gpsimd
        def _(pool):
            pool.memset(ones[:], 1.0).then_inc(const_set, 1)
            pool.memset(u[:, 0:2], 0.0).then_inc(const_set, 1)
            pool.memset(hhi[:, KT * TM:].bitcast(F32), 0.0).then_inc(pad_set, 1)
            pool.memset(hlo[:, KT * TM:].bitcast(F32), 0.0).then_inc(pad_set, 1)
            pool.dma_start(mat[:], mats).then_inc(c_loaded, 16)
            pool.dma_start(rop[:], rope).then_inc(c_loaded, 16)
            pool.dma_start(cmask[:], colmask).then_inc(c_loaded, 16)
            pool.dma_start(metab[:], metabias).then_inc(c_loaded, 16)
            pool.dma_start(x[:, :, T:TM], metaT).then_inc(c_loaded, 16)
            pool.wait_ge(h32_done, KT)
            pool.dma_start(bt[:], btab).then_inc(b_loaded, 16)
            pool.wait_ge(fx_done, KT)
            pool.memset(yhi[:, 2 * TM:QL0].bitcast(F32), 0.0).then_inc(pad_set, 1)
            pool.memset(ylo[:, 2 * TM:QL0].bitcast(F32), 0.0).then_inc(pad_set, 1)
            for h in range(NH):
                if h >= 2:
                    pool.wait_ge(s_add, LAYERS * HEADS + 2 * (2 * (h - 1)) + PRIME)
                pool.dma_start(rel[:, h % 2], relbias[h]).then_inc(rel_loaded[h % 2], 16)
                pool.wait_ge(rel_loaded[h % 2], 16 * (h // 2 + 1))
                if h == 0:
                    pool.wait_ge(c_loaded, C_LOADS)
                pool.tensor_tensor(rel[:, h % 2], rel[:, h % 2],
                                   cmask[:].unsqueeze(1).broadcast_to([P, 6, GW]), ALU.add).then_inc(rel_ready, 1)

        @block.scalar
        def _(act):
            for s in (*hi_ready, *silu_done, cc_done, pt_done):
                act.sem_inc(s, PRIME)
            act.dma_start(sml[:], small).then_inc(g_loaded, 16)

            def split(slot, cols, count):
                act.wait_ge(raw_full[slot], count * 16)
                act.wait_ge(w_used[slot], count - 1)
                act.activation(whi[:, slot, 0:cols], raw[:, slot, 0:cols], ACT.Copy).then_inc(hi_ready[slot], 1)

            def split_ahead(name, nxt, l, i, j=0, last=True):
                ph, t = PHASES[name], i + LEAD
                if last and t >= ph.pieces:
                    n, t = PHASES[nxt], t - ph.pieces
                    split(n.slot(t), n.cols, uses(nxt, t, l + 1 if nxt == "gu1" else l))
                else:
                    split(ph.slot(t), ph.cols, uses(name, t, l, j))

            def square(p, count, src):
                act.wait_ge(sq_used[p], count - 1)
                act.activation(sq[:, p, 0:src.shape[-1]], src, ACT.Square).then_inc(sq_done[p], 1)

            def rstd(total, slot, width, n, count):
                act.activation(lnv[:, slot, 0:n], total, ACT.Ln, scale=1.0 / width, bias=EPS).then_inc(ln_done, 1)
                act.wait_ge(ln_done, count)
                act.activation(rs[:, slot, 0:n], lnv[:, slot, 0:n], ACT.Exp, scale=-0.5).then_inc(rstd_done, 1)

            def norm(q, n=T, h=None):
                h = q if h is None else h
                act.wait_ge(sq_used[1], q * 4 + 4)
                rstd(bank[SUM][:, 0:n], 0, D, n, q + 1)
                for k in range(KT):
                    act.wait_ge(h32_done, h * KT + k + 1)
                    act.activation(hhi[:, k * TM:k * TM + n], h32[:, k % 4, 0:n], ACT.Copy).then_inc(h_hi, 1)

            def gate_up(name, nxt, l, w):
                n11 = l * (2 * HALF) + w * HALF
                act.preload_act_table(ACT.Silu)

                def lap(j, last):
                    for r in range(SLOTS):
                        i = r if not last else GU - SLOTS + r
                        p = r // 2
                        split_ahead(name, nxt, l, i, j, last)
                        if r % 2 == 0:
                            act.wait_ge(w_used[r], uses(name, i, l, j))
                            act.activation(sg[:, p], bank[2 * p][:, 0:T], ACT.Silu).then_inc(silu_done[p], 1)
                        else:
                            count = n11 + j + 1 + (HALF - 1 if last else 0)
                            act.wait_ge(g_mul[p], count + PRIME)
                            f = j * 2 + p if not last else FT - 2 + p
                            act.activation(ghi[:, f, :], g32[:, p], ACT.Copy).then_inc(g_hi[p], 1)

                with act.Fori(0, GU // SLOTS - 1) as j:
                    lap(j, False)
                lap(0, True)

            def down(name, nxt, l, q):
                act.preload_act_table_set("natural_log_exp_and_others")

                def lap(j, last):
                    for r in range(SLOTS):
                        i = r if not last else DN - SLOTS + r
                        split_ahead(name, nxt, l, i, j, last)
                        if r % 2:
                            p, o2 = r // 2, j if not last else KT // 2 - 1
                            act.wait_ge(x_ready[p], q * 4 + o2 + (PRIME - 3))
                            square(p, q * 4 + o2 + 1, x[:, o2 * 2 + p, 0:T])

                with act.Fori(0, DN // SLOTS - 1) as j:
                    lap(j, False)
                lap(0, True)

            def qkv(l):
                dst = [q32[:, j, :] for j in range(QT)] + [k32[:], v32[:].rearrange("p t c -> p (t c)")]
                for i in range(QKV):
                    split_ahead("qkv", "conv", l, i)
                    act.wait_ge(w_used[PHASES["qkv"].slot(i)], uses("qkv", i, l))
                    act.activation(dst[i], bank[i % 4][:, 0:T], ACT.Copy).then_inc(qkv_done, 1)

            def exp_first(l, h):
                act.wait_ge(nm_done, l * HEADS + h + 1)
                s = h % 2
                act.activation(Pr[:, s, 0:BLK], S[:, s, 0:BLK], ACT.Exp, bias=nm[:, 2 * h:2 * h + 1],
                               accum_out=sums[:, 2 * h:2 * h + 1])
                act.activation(Pr[:, s, BLK:3 * BLK], S[:, s, BLK:3 * BLK], ACT.Exp,
                               bias=nm[:, 2 * h + 1:2 * h + 2], accum_out=sums[:, 2 * h + 1:2 * h + 2])
                sink = sml[:, bass.ds(l * HEADS + (G_SINK + h), 1)]
                act.activation(es[:, 2 * h:2 * h + 2], nm[:, 2 * h:2 * h + 2], ACT.Exp, bias=sink)\
                   .then_inc(exp_done, 1)

            def pt_first(l, h):
                act.wait_ge(tr_done, l * HEADS + h + 1)
                act.activation(PT[:, h % 2], bank[TRANS][:, 0:3 * BLK], ACT.Copy).then_inc(pt_done, 1)

            def conv(l):
                for i in range(CONV):
                    split_ahead("conv", "wout", l, i)
                    if 0 <= i - 3 < HEADS:
                        pt_first(l, i - 3)
                    if 0 <= i - 1 < HEADS:
                        exp_first(l, i - 1)
                    jj, kind = i // 3, i % 3
                    if kind == 0:
                        act.wait_ge(w_used[PHASES["conv"].slot(i)], uses("conv", i, l))
                        act.wait_ge(u_done, l * CT + (jj + PRIME))
                        act.activation(cc32[:], bank[2][:, 0:T], ACT.Copy).then_inc(cc_done, 1)
                    elif kind == 2:
                        act.wait_ge(m_done, l * CT + jj + (1 + PRIME))
                        act.activation(ghi[:, 4 + jj, :], m32[:, jj % 2], ACT.Copy).then_inc(mix_hi, 1)
                for j in range(QT):
                    act.wait_ge(ot_done, l * QT + j + 1)
                    act.activation(ghi[:, j, :], bank[4 + j][:, 0:T], ACT.Copy).then_inc(mix_hi, 1)

            def wout(l, q):
                for o in range(KT):
                    if o < KT - LEAD:
                        split_ahead("wout", "gu2", l, o)
                    act.wait_ge(x_ready[o % 2], q * 4 + (o // 2 + PRIME - 3))
                    square(o % 2, q * 4 + o // 2 + 1, x[:, o, 0:T])
                    if o >= KT - LEAD:
                        split_ahead("wout", "gu2", l, o)

            act.preload_act_table_set("natural_log_exp_and_others")
            for k in range(KT):
                act.wait_ge(x_loaded[k // (KT // 2)], 16)
                square(k % 2, k // 2 + 1, x[:, k, 0:T])
                if k in (3, 5, 7):
                    split((k - 3) // 2, PT8, uses0(1))
            with act.Fori(0, LAYERS) as l:
                norm(l * 3)
                gate_up("gu1", "dn1", l, 0)
                down("dn1", "qkv", l, l * 3 + 1)
                norm(l * 3 + 1)
                qkv(l)
                conv(l)
                wout(l, l * 3 + 2)
                norm(l * 3 + 2)
                gate_up("gu2", "dn2", l, 1)
                down("dn2", "gu1", l, l * 3 + 3)
            act.preload_act_table_set("natural_log_exp_and_others")
            act.wait_ge(sq_used[1], 6 * 4 + 4)
            rstd(bank[SUM][:, 0:T], 0, D, T, 7)
            act.wait_ge(c_loaded, C_LOADS)
            for k in range(KT):
                act.wait_ge(fx_done, k + 1)
                square(k % 2, 7 * 4 + k // 2 + 1, x[:, k, :])
            norm(7, TM, 6)

            def split2(piece):
                if piece < SECOND:
                    split(piece % SLOTS, PT8, uses2(piece))

            def gate_tanh(j, b):
                if 2 <= j < 8:
                    act.wait_ge(silu_all, j - 1)
                elif j >= 10:
                    act.wait_ge(fill_taken, j - 9)
                act.activation(sg[:, j % 2], b, ACT.Tanh, scale=0.5).then_inc(th_done, 1)

            def y_high(y):
                act.wait_ge(y_done, y + 1)
                act.activation(yhi[:, y * T:(y + 1) * T], g32[:, y % 2], ACT.Copy).then_inc(y_hi, 1)

            def projections(outs, st):
                for n in range(len(outs) + 4):
                    pieces = st["pieces"].get(n, [])
                    for piece in pieces[0:1]:
                        split2(piece + LEAD)
                    if n in st["normed"]:
                        m = st["normed"][n]
                        wait_output(act, outs, n)
                        square(m % 2, 32 + m // 2 + 1, bank[n % 4][:, 0:TOKENS[outs[n][0]]])
                    g = st["done_at"].get(n - LAG - 1)
                    if g is not None and outs[st["groups"][g][0]][0] in latw:
                        for i in st["groups"][g]:
                            kind, k, _ = outs[i]
                            c = st["latent"][i]
                            act.wait_ge(h32_done, 7 * KT + c + 1)
                            off, wid = latw[kind]
                            act.activation(yhi[:, off + k * wid:off + (k + 1) * wid], h32[:, c, 0:wid],
                                           ACT.Copy).then_inc(h_hi, 1)
                    i = n - LAG
                    g = st["done_at"].get(i)
                    if g is not None:
                        members = st["groups"][g]
                        kind = outs[members[0]][0]
                        m = st["normed"][members[-1]]
                        act.wait_ge(sq_used[m % 2], 32 + m // 2 + 1)
                        if g - st["g0"] >= 2:
                            act.wait_ge(pj_taken, st["n0"] + st["groups"][g - 2][-1] + 1)
                        rstd(bank[6 + g % 2][:, 0:TOKENS[kind]], g % 2, NORM_WIDTH[kind], TOKENS[kind], 8 + g + 1)
                    if outs is NA and 0 <= n - 2 < 8:
                        y_high(n - 2)
                    for piece in pieces[1:]:
                        split2(piece + LEAD)

            def probs_T(v):
                act.wait_ge(tr_done, LAYERS * HEADS + v + 1)
                b = 2 + v % 2
                act.activation(PT[:, v % 2, 0:2 * BLK], bank[b][:, 0:2 * BLK], ACT.Copy)
                act.activation(PT[0:META, v % 2, 2 * BLK:3 * BLK], bank[b][0:META, 2 * BLK:3 * BLK],
                               ACT.Copy).then_inc(pt_done, 1)

            def attention(v0, units, scale, from_psum):
                for i in range(units + 2):
                    m = i // 2
                    if i >= 2:
                        probs_T(v0 + i - 2)
                    if i < units:
                        v = v0 + i
                        act.wait_ge(nm_done, LAYERS * HEADS + v + 1)
                        src = bank[v % 2][:, 0:TM] if from_psum else S[:, v % 2, 0:TM]
                        act.activation(Pr[:, v % 2, 0:TM], src, ACT.Exp, bias=nm[:, v % 32:v % 32 + 1], scale=scale,
                                       accum_out=sums[:, v % 32:v % 32 + 1]).then_inc(exp_done, 1)
                    if from_psum and i % 2 and m < 8:
                        gate_tanh(m, sgate[:, m])
                    if not from_psum and i % 2 == 0 and m < FILL:
                        split2(FILL0 + m + LEAD)
                    if not from_psum and i % 2 and m < 8:
                        act.wait_ge(w_used[(FILL0 + m) % SLOTS], uses2(FILL0 + m))
                        gate_tanh(8 + m, bank[6 + m % 2][:, 0:T])

            projections(MLA, ST_MLA)
            act.preload_act_table_set("exp_and_others")
            attention(0, 2 * MH, MLA_SCALE, True)
            act.preload_act_table_set("natural_log_exp_and_others")
            projections(NA, ST_NA)
            act.preload_act_table_set("exp_and_others")
            attention(2 * MH, 2 * NH, 1.0, False)
            for i in range(8):
                y_high(8 + i)
            for piece in range(FILL0 + FILL, SECOND):
                split2(piece + LEAD)

        @block.vector
        def _(dve):
            for s in (*lo_ready, *g_mul, *x_ready, s_add, o_done, u_done, m_done, y_step):
                dve.sem_inc(s, PRIME)
            def split(slot, cols, count):
                dve.wait_ge(hi_ready[slot], count)
                dve.tensor_tensor(wlo[:, slot, 0:cols], raw[:, slot, 0:cols],
                                  whi[:, slot, 0:cols].bitcast(F32), ALU.subtract).then_inc(lo_ready[slot], 1)

            def split_ahead(name, nxt, l, i, j=0, last=True):
                ph, t = PHASES[name], i + LEAD
                if last and t >= ph.pieces:
                    n, t = PHASES[nxt], t - ph.pieces
                    split(n.slot(t), n.cols, uses(nxt, t, l + 1 if nxt == "gu1" else l))
                else:
                    split(ph.slot(t), ph.cols, uses(name, t, l, j))

            def norm(q, n=T, h=None):
                h = q if h is None else h
                dve.wait_ge(rstd_done, q + 1)
                for k in range(KT + 1):
                    if k < KT:
                        dve.scalar_tensor_tensor(out=h32[:, k % 4, 0:n], in0=x[:, k, 0:n],
                                                 scalar=sml[:, bass.ds(q * KT + k, 1)], in1=rs[:, 0, 0:n],
                                                 op0=ALU.mult, op1=ALU.mult).then_inc(h32_done, 1)
                    if k > 0:
                        dve.wait_ge(h_hi, h * KT + k)
                        c = (k - 1) * TM
                        dve.tensor_tensor(hlo[:, c:c + n], h32[:, (k - 1) % 4, 0:n], hhi[:, c:c + n].bitcast(F32),
                                          ALU.subtract).then_inc(h_lo, 1)

            def gate_up(name, nxt, l, w):
                n11 = l * (2 * HALF) + w * HALF

                def lap(j, last):
                    for r in range(SLOTS):
                        i = r if not last else GU - SLOTS + r
                        p = r // 2
                        split_ahead(name, nxt, l, i, j, last)
                        if r % 2:
                            count = n11 + j + 1 + (HALF - 1 if last else 0)
                            dve.wait_ge(silu_done[p], count + PRIME)
                            dve.wait_ge(w_used[r], uses(name, i, l, j))
                            dve.tensor_tensor(g32[:, p], bank[2 * p + 1][:, 0:T], sg[:, p], ALU.mult)\
                               .then_inc(g_mul[p], 1)
                            dve.wait_ge(g_hi[p], count)
                            f = j * 2 + p if not last else FT - 2 + p
                            dve.tensor_tensor(glo[:, f, :], g32[:, p], ghi[:, f, :].bitcast(F32), ALU.subtract)\
                               .then_inc(g_lo[p], 1)

                with dve.Fori(0, GU // SLOTS - 1) as j:
                    lap(j, False)
                lap(0, True)

            def down(name, nxt, l, q):
                def lap(j, last):
                    for r in range(SLOTS):
                        i = r if not last else DN - SLOTS + r
                        split_ahead(name, nxt, l, i, j, last)
                        if r % 2:
                            p, o2 = r // 2, j if not last else KT // 2 - 1
                            dve.wait_ge(w_used[r], uses(name, i, l, j))
                            xo = x[:, o2 * 2 + p, 0:T]
                            dve.scalar_tensor_tensor(out=xo, in0=bank[p][:, 0:T], scalar=0.5, in1=xo,
                                                     op0=ALU.mult, op1=ALU.add).then_inc(x_ready[p], 1)

                with dve.Fori(0, DN // SLOTS - 1) as j:
                    lap(j, False)
                lap(0, True)

            def qkv(l):
                for i in range(QKV):
                    split_ahead("qkv", "conv", l, i)

            def add_max(l, h):
                n, s = l * HEADS + h, h % 2
                dve.wait_ge(sc_done, n + 1)
                dve.scalar_tensor_tensor(out=S[:, s], in0=bank[SCORE][:, 0:3 * BLK], scalar=HD ** -0.5,
                                         in1=bt[:, h, :], op0=ALU.mult, op1=ALU.add).then_inc(s_add, 1)
                dve.wait_ge(s_add, n + (1 + PRIME))
                dve.reduce_max(mx[:, 2 * h:2 * h + 1], S[:, s, 0:BLK], AX_X)
                dve.reduce_max(mx[:, 2 * h + 1:2 * h + 2], S[:, s, BLK:3 * BLK], AX_X).then_inc(mx_done, 1)
                dve.wait_ge(mx_done, n + 1)
                sink = sml[:, bass.ds(l * HEADS + (G_SINK + h), 1)]
                dve.tensor_scalar(nm[:, 2 * h:2 * h + 2], mx[:, 2 * h:2 * h + 2], sink, -1.0, ALU.max, ALU.mult)\
                   .then_inc(nm_done, 1)

            def denominators(n, a, b, add_sink):
                dve.wait_ge(exp_done, n + 1)
                src = sums
                if add_sink:
                    dve.tensor_tensor(den[:, a:b], sums[:, a:b], es[:, a:b], ALU.add).then_inc(den_done, 1)
                    dve.wait_ge(den_done, n + 1)
                    src = den
                dve.reciprocal(rec[:, a:b], src[:, a:b]).then_inc(rec_done, 1)

            def out_first(l, h):
                n = l * HEADS + h
                dve.wait_ge(pv_done, n + 1)
                dve.wait_ge(rec_done, n + 1)
                col = (h % QT) * P + h // QT * HD
                for b in range(2):
                    o = dve.tensor_scalar(O32[:, b, col:col + HD], bank[OUT][:, b * HD:(b + 1) * HD],
                                          rec[:, 2 * h + b:2 * h + b + 1], None, ALU.mult)
                o.then_inc(o_done, 1)

            def conv(l):
                dve.wait_ge(b_loaded, 16)
                dve.wait_ge(const_set, 2)
                for i in range(CONV):
                    split_ahead("conv", "wout", l, i)
                    jj, kind = i // 3, i % 3
                    c = l * CT + jj
                    slot, count = PHASES["conv"].slot(i), uses("conv", i, l)
                    tap = [sml[:, bass.ds(l * (3 * CT) + (G_CONV + 3 * jj + t), 1)] for t in range(3)]
                    if kind == 1:
                        dve.wait_ge(w_used[slot], count)
                        dve.wait_ge(cc_done, c + (1 + PRIME))
                        dve.wait_ge(y_step, c * 3 + PRIME)
                        dve.tensor_tensor(u[:, 2:T + 2], bank[3][:, 0:T], cc32[:], ALU.mult).then_inc(u_done, 1)
                        dve.wait_ge(u_done, c + (1 + PRIME))
                        dve.tensor_scalar(ya[:], u[:, 2:T + 2], tap[2], None, ALU.mult).then_inc(y_step, 1)
                        dve.wait_ge(y_step, c * 3 + (1 + PRIME))
                        dve.scalar_tensor_tensor(out=yb[:], in0=u[:, 1:T + 1], scalar=tap[1], in1=ya[:],
                                                 op0=ALU.mult, op1=ALU.add).then_inc(y_step, 1)
                        dve.wait_ge(y_step, c * 3 + (2 + PRIME))
                        dve.scalar_tensor_tensor(out=ya[:], in0=u[:, 0:T], scalar=tap[0], in1=yb[:],
                                                 op0=ALU.mult, op1=ALU.add).then_inc(y_step, 1)
                    elif kind == 2:
                        dve.wait_ge(w_used[slot], count)
                        dve.wait_ge(y_step, c * 3 + (3 + PRIME))
                        dve.tensor_tensor(m32[:, jj % 2], bank[0][:, 0:T], ya[:], ALU.mult).then_inc(m_done, 1)
                        dve.wait_ge(mix_hi, l * 8 + jj + 1)
                        dve.tensor_tensor(glo[:, 4 + jj, :], m32[:, jj % 2], ghi[:, 4 + jj, :].bitcast(F32),
                                          ALU.subtract).then_inc(mix_lo, 1)
                    if 0 <= i - 1 < HEADS:
                        denominators(l * HEADS + i - 1, 2 * (i - 1), 2 * i, True)
                    if 0 <= i - 4 < HEADS:
                        out_first(l, i - 4)
                    if i < HEADS:
                        add_max(l, i)
                for j in range(QT):
                    dve.wait_ge(mix_hi, l * 8 + CT + j + 1)
                    dve.tensor_tensor(glo[:, j, :], bank[4 + j][:, 0:T], ghi[:, j, :].bitcast(F32),
                                      ALU.subtract).then_inc(mix_lo, 1)

            def wout(l, q):
                for o in range(KT):
                    if o < KT - LEAD:
                        split_ahead("wout", "gu2", l, o)
                    dve.wait_ge(w_used[PHASES["wout"].slot(o)], uses("wout", o, l))
                    xo = x[:, o, 0:T]
                    dve.tensor_tensor(xo, bank[o % 2][:, 0:T], xo, ALU.add).then_inc(x_ready[o % 2], 1)
                    if o >= KT - LEAD:
                        split_ahead("wout", "gu2", l, o)

            for i in range(LEAD):
                split(i, PT8, uses0(1))
            dve.wait_ge(g_loaded, 16)
            for p in range(2):
                dve.wait_ge(x_loaded[p], 16)
            with dve.Fori(0, LAYERS) as l:
                norm(l * 3)
                gate_up("gu1", "dn1", l, 0)
                down("dn1", "qkv", l, l * 3 + 1)
                norm(l * 3 + 1)
                qkv(l)
                conv(l)
                wout(l, l * 3 + 2)
                norm(l * 3 + 2)
                gate_up("gu2", "dn2", l, 1)
                down("dn2", "gu1", l, l * 3 + 3)
            dve.wait_ge(rstd_done, 7)
            for k in range(KT):
                dve.scalar_tensor_tensor(out=x[:, k, 0:T], in0=x[:, k, 0:T], scalar=sml[:, 6 * KT + k:6 * KT + k + 1],
                                         in1=rs[:, 0, 0:T], op0=ALU.mult, op1=ALU.mult).then_inc(fx_done, 1)
            dve.wait_ge(fx_done, KT)
            dve.wait_ge(c_loaded, C_LOADS)
            norm(7, TM, 6)

            def split2(piece):
                if piece < SECOND:
                    split(piece % SLOTS, PT8, uses2(piece))

            def normed_dst(kind, k, c):
                if kind in latw:
                    return h32[:, c, 0:TOKENS[kind]]
                if kind in ("kpe", "qpe"):
                    return S[:, c % 2, 0:TOKENS[kind]]
                return {"kn": kn, "nak": kn, "qn": qn, "naq": qn}[kind][:, k, :]

            def silu(count, j, gate, taken):
                dve.wait_ge(th_done, count + 1)
                dve.scalar_tensor_tensor(out=sgate[:, j], in0=sg[:, count % 2], scalar=1.0, in1=gate,
                                         op0=ALU.add, op1=ALU.mult).then_inc(taken, 1)

            def y_product(y, b):
                dve.wait_ge(ot_done, LAYERS * QT + y + 1)
                if y >= 2:
                    dve.wait_ge(y_lo, y - 1)
                dve.scalar_tensor_tensor(out=g32[:, y % 2], in0=b[:, 0:T], scalar=0.5, in1=sgate[:, y % 8],
                                         op0=ALU.mult, op1=ALU.mult).then_inc(y_done, 1)

            def y_low(y):
                dve.wait_ge(y_hi, y + 1)
                dve.tensor_tensor(ylo[:, y * T:(y + 1) * T], g32[:, y % 2],
                                  yhi[:, y * T:(y + 1) * T].bitcast(F32), ALU.subtract).then_inc(y_lo, 1)

            def projections(outs, st):
                for n in range(len(outs) + LAG + 3):
                    pieces = st["pieces"].get(n, [])
                    for piece in pieces[0:1]:
                        split2(piece + LEAD)
                    i = n - LAG - 2
                    if i in st["ropes"]:
                        c, nt = st["ropes"][i], TOKENS[outs[i][0]]
                        dst = kp[:] if outs[i][0] == "kpe" else qp[:, outs[i][1], :]
                        dve.wait_ge(rot_done, c + 1)
                        if c > 0:
                            dve.wait_ge(rope_done, c)
                        dve.tensor_tensor(Pr[:, 0, 0:nt], bank[SCORE][:, 0:nt], rop[:, 1, 0:nt], ALU.mult)
                        dve.tensor_tensor(Pr[:, 1, 0:nt], S[:, c % 2, 0:nt], rop[:, 0, 0:nt], ALU.mult)\
                           .then_inc(rt_done, 1)
                        dve.wait_ge(rt_done, c + 1)
                        dve.tensor_tensor(dst, Pr[:, 0, 0:nt], Pr[:, 1, 0:nt], ALU.add).then_inc(rope_done, 1)
                    g = st["done_at"].get(n - LAG - 1)
                    if g is not None and outs[st["groups"][g][0]][0] in latw:
                        for i in st["groups"][g]:
                            kind, k, _ = outs[i]
                            c = st["latent"][i]
                            off, wid = latw[kind]
                            dve.wait_ge(h_hi, 7 * KT + c + 1)
                            dve.tensor_tensor(ylo[:, off + k * wid:off + (k + 1) * wid], h32[:, c, 0:wid],
                                              yhi[:, off + k * wid:off + (k + 1) * wid].bitcast(F32), ALU.subtract)\
                               .then_inc(pj_taken, 1)
                    g = st["done_at"].get(n - LAG)
                    if g is not None:
                        dve.wait_ge(rstd_done, 8 + g + 1)
                        for i in st["groups"][g]:
                            kind, k, _ = outs[i]
                            c = st["latent"].get(i, st["ropes"].get(i))
                            if i in st["ropes"] and c >= 2:
                                dve.wait_ge(rope_done, c - 1)
                            gain = G_HEAD + HEAD_GAIN[kind] + (k if kind in latw else 0)
                            nt = TOKENS[kind]
                            ins = dve.scalar_tensor_tensor(
                                out=normed_dst(kind, k, c), in0=bank[i % 4][:, 0:nt], scalar=sml[:, gain:gain + 1],
                                in1=rs[:, g % 2, 0:nt], op0=ALU.mult, op1=ALU.mult)
                            if kind in latw:
                                ins.then_inc(h32_done, 1)
                            else:
                                ins.then_inc(pj_taken, 1)
                    i = n - LAG
                    if 0 <= i < len(outs):
                        kind, k, _ = outs[i]
                        if kind in ("uv", "nav"):
                            c, tt = divmod(k, 3)
                            np_ = P if tt < 2 else META
                            wait_output(dve, outs, i)
                            dve.tensor_copy(V[0:np_, tt, c * 512:(c + 1) * 512], bank[out_bank(outs, i)][0:np_, :])\
                               .then_inc(pj_taken, 1)
                        if kind == "gate":
                            wait_output(dve, outs, i)
                            dve.tensor_copy(sgate[:, k], bank[i % 4][:, 0:T]).then_inc(pj_taken, 1)
                    if outs is NA and 0 <= n - 3 < 8:
                        y_low(n - 3)
                    if outs is NA and 0 <= n - 1 < 8:
                        y_product(n - 1, bank[4 + (n - 1) % 2])
                    for piece in pieces[1:]:
                        split2(piece + LEAD)

            def out_second(v, width, dst):
                dve.wait_ge(pv_done, LAYERS * HEADS + v + 1)
                dve.wait_ge(rec_done, LAYERS * HEADS + v + 1)
                dve.tensor_scalar(dst, bank[4 + v % 2][:, 0:width], rec[:, v % 32:v % 32 + 1], None, ALU.mult)\
                   .then_inc(o_done, 1)

            def attention(v0, units, width, mla):
                for i in range(units + 3):
                    m = i // 2
                    if i < units:
                        v = v0 + i
                        h, t = i // 2, i % 2
                        c = v % 32
                        dve.wait_ge(sc_done, LAYERS * HEADS + v + 1)
                        if mla:
                            dve.reduce_max(mx[:, c:c + 1], bank[v % 2][:, 0:TM], AX_X).then_inc(mx_done, 1)
                        else:
                            if t == 0:
                                dve.wait_ge(rel_ready, h + 1)
                            if i >= 2:
                                dve.wait_ge(exp_done, LAYERS * HEADS + v - 1)
                            dve.scalar_tensor_tensor(
                                out=S[:, v % 2, 0:T], in0=bank[v % 2][:, 0:T], scalar=HD ** -0.5,
                                in1=rel[:, h % 2, 2 - 2 * t:6 - 2 * t, :].rearrange("p r c -> p (r c)"),
                                op0=ALU.mult, op1=ALU.add).then_inc(s_add, 1)
                            dve.scalar_tensor_tensor(
                                out=S[:, v % 2, T:TM], in0=bank[v % 2][:, T:TM], scalar=HD ** -0.5,
                                in1=metab[:, h, :], op0=ALU.mult, op1=ALU.add).then_inc(s_add, 1)
                            dve.wait_ge(s_add, LAYERS * HEADS + 2 * (i + 1) + PRIME)
                            dve.reduce_max(mx[:, c:c + 1], S[:, v % 2, 0:TM], AX_X).then_inc(mx_done, 1)
                        dve.wait_ge(mx_done, LAYERS * HEADS + v + 1)
                        dve.tensor_scalar(nm[:, c:c + 1], mx[:, c:c + 1], -(MLA_SCALE if mla else 1.0), None,
                                          ALU.mult).then_inc(nm_done, 1)
                    if i >= 1 and i <= units:
                        v = v0 + i - 1
                        denominators(LAYERS * HEADS + v, v % 32, v % 32 + 1, False)
                    if i >= 3:
                        h, t = (i - 3) // 2, (i - 3) % 2
                        out_second(v0 + i - 3, width, O32[:, t, h * width:(h + 1) * width])
                    if mla and i % 2 and m < 8:
                        silu(m, m, sgate[:, m], silu_all)
                    if not mla and i % 2 and m < FILL:
                        split2(FILL0 + m + LEAD)
                    m = i // 2 - 1
                    if not mla and i % 2 == 0 and 0 <= m < FILL:
                        if m < 8:
                            silu(8 + m, m, bank[6 + m % 2][:, 0:T], fill_taken)
                        else:
                            piece, o = FILL0 + m, m - 8
                            dve.wait_ge(w_used[piece % SLOTS], uses2(piece))
                            dve.tensor_tensor(x[:, o, 0:T], bank[6 + m % 2][:, 0:T], x[:, o, 0:T], ALU.add)\
                               .then_inc(fill_taken, 1)

            projections(MLA, ST_MLA)
            attention(0, 2 * MH, P, True)
            projections(NA, ST_NA)
            attention(2 * MH, 2 * NH, HD, False)
            for i in range(9):
                if i >= 1:
                    y_low(8 + i - 1)
                if i < 8:
                    y_product(8 + i, bank[2 + i % 4])
            for o in range(8):
                piece = FILL0 + FILL + o
                split2(piece + LEAD)
                dve.wait_ge(w_used[piece % SLOTS], uses2(piece))
                dve.wait_ge(fill_taken, FILL)
                dve.tensor_tensor(x[:, o, 0:T], bank[(0, 1, 6, 7)[o % 4]][:, 0:T], x[:, o, 0:T], ALU.add)\
                   .then_inc(res_done, 1)

        @block.tensor
        def _(pe):
            for s in w_used:
                pe.sem_inc(s, PRIME)

            def product(o, slot, t, xh, xl, first, last, n=P):
                h, lo = whi[:, slot, t * P:(t + 1) * P], wlo[:, slot, t * P:(t + 1) * P]
                pe.matmul(o, h, xh, start=first, stop=False)
                pe.matmul(o, h, xl, start=False, stop=False)
                return pe.matmul(o, lo, xh, start=False, stop=last)

            def hcols(k, n=T):
                return hhi[:, k * TM:k * TM + n], hlo[:, k * TM:k * TM + n]

            def tile8(o, slot, n=T):
                for k in range(KT):
                    mm = product(o, slot, k, *hcols(k, n), k == 0, k == KT - 1)
                mm.then_inc(w_used[slot], 1)

            def first_pair(o0, o1, slot0, slot1, q):
                for k in range(KT):
                    pe.wait_ge(h_lo, q * KT + k + 1)
                    a = product(o0, slot0, k, *hcols(k), k == 0, k == KT - 1)
                    b = product(o1, slot1, k, *hcols(k), k == 0, k == KT - 1)
                a.then_inc(w_used[slot0], 1)
                b.then_inc(w_used[slot1], 1)

            def sum_squares(p, count, first, last, n=T, total=SUM, lhs=None):
                pe.wait_ge(sq_done[p], count)
                pe.matmul(bank[total][:, 0:n], ones[:] if lhs is None else lhs, sq[:, p, 0:n], start=first, stop=last)\
                  .then_inc(sq_used[p], 1)

            def gate_up(name, l, w, q):
                n11 = l * (2 * HALF) + w * HALF

                def ready(r, j):
                    pe.wait_ge(lo_ready[r], uses(name, r, l, j))
                    pe.wait_ge(silu_done[r // 2] if r % 2 == 0 else g_mul[r // 2], n11 + (j + PRIME))

                ready(0, 0)
                ready(1, 0)
                first_pair(bank[0][:, 0:T], bank[1][:, 0:T], 0, 1, q)
                for r in (2, 3):
                    ready(r, 0)
                    tile8(bank[r][:, 0:T], r)
                with pe.Fori(1, GU // SLOTS) as j:
                    for r in range(SLOTS):
                        ready(r, j)
                        tile8(bank[r][:, 0:T], r)

            def down(name, l, w, q):
                n11 = l * (2 * HALF) + w * HALF

                def lap(j, first):
                    for r in range(SLOTS):
                        p, half = r // 2, r % 2
                        pe.wait_ge(lo_ready[r], uses(name, r, l, j))
                        if half == 0:
                            pe.wait_ge(x_ready[p], (q * 4 - 4) + (j + PRIME))
                        pe.wait_ge(g_lo[0], n11 + (HALF + 1) // 2 if half == 0 else n11 + HALF)
                        pe.wait_ge(g_lo[1], n11 + HALF // 2 if half == 0 else n11 + HALF)
                        for k in range(HALF):
                            f = half * HALF + k
                            mm = product(bank[p][:, 0:T], r, k, ghi[:, f, :], glo[:, f, :], f == 0, f == FT - 1)
                        mm.then_inc(w_used[r], 1)
                        if r == 1 and not first:
                            sum_squares(1, q * 4 + j, False, False)
                        if r == 3:
                            sum_squares(0, q * 4 + j + 1, first, False)

                pe.wait_ge(silu_done[0], n11 + (HALF + PRIME))
                lap(0, True)
                with pe.Fori(1, DN // SLOTS) as j:
                    lap(j, False)
                sum_squares(1, q * 4 + 4, False, True)

            def qkv(l, q):
                for i in range(2):
                    pe.wait_ge(lo_ready[PHASES["qkv"].slot(i)], uses("qkv", i, l))
                first_pair(bank[0][:, 0:T], bank[1][:, 0:T], 0, 1, q)
                for i in range(2, QKV):
                    slot = PHASES["qkv"].slot(i)
                    pe.wait_ge(lo_ready[slot], uses("qkv", i, l))
                    if i >= 4:
                        pe.wait_ge(qkv_done, l * QKV + i - 3)
                    if i < QKV - 1:
                        tile8(bank[i % 4][:, 0:T], slot)
                        continue
                    for t in range(2):
                        for k in range(KT):
                            xh, xl = (a[:, t * P:(t + 1) * P] for a in hcols(k))
                            wh, wl = whi[:, slot, k * P:(k + 1) * P], wlo[:, slot, k * P:(k + 1) * P]
                            o = bank[i % 4][:, t * P:(t + 1) * P]
                            pe.matmul(o, xh, wh, start=k == 0, stop=False)
                            pe.matmul(o, xl, wh, start=False, stop=False)
                            mm = pe.matmul(o, xh, wl, start=False, stop=k == KT - 1)
                    mm.then_inc(w_used[slot], 1)

            def scores_first(l, h):
                n, j, r = l * HEADS + h, h % QT, h // QT * HD
                pe.wait_ge(qkv_done, l * QKV + QKV - 1)
                pe.wait_ge(s_add, n + PRIME)
                pe.matmul(bank[SCORE][:, 0:BLK], q32[r:r + HD, j, 0:BLK], k32[r:r + HD, 0:BLK], start=True, stop=True)
                pe.matmul(bank[SCORE][:, BLK:3 * BLK], q32[r:r + HD, j, BLK:T], k32[r:r + HD, :], start=True,
                          stop=True).then_inc(sc_done, 1)

            def transpose_first(l, h):
                n = l * HEADS + h
                pe.wait_ge(exp_done, n + 1)
                pe.wait_ge(pt_done, n + PRIME)
                for b in range(3):
                    tr = pe.transpose(bank[TRANS][:, b * BLK:(b + 1) * BLK], Pr[:, h % 2, b * BLK:(b + 1) * BLK], ident)
                tr.then_inc(tr_done, 1)

            def pv_first(l, h):
                n, c = l * HEADS + h, h // QT * HD
                pe.wait_ge(qkv_done, l * QKV + QKV)
                pe.wait_ge(pt_done, n + (1 + PRIME))
                pe.wait_ge(o_done, n + PRIME)
                pt = PT[:, h % 2]
                pe.matmul(bank[OUT][:, 0:HD], pt[:, 0:BLK], v32[:, 0, c:c + HD], start=True, stop=True)
                pe.matmul(bank[OUT][:, HD:2 * HD], pt[:, BLK:2 * BLK], v32[:, 0, c:c + HD], start=True, stop=False)
                pe.matmul(bank[OUT][:, HD:2 * HD], pt[:, 2 * BLK:3 * BLK], v32[:, 1, c:c + HD], start=False,
                          stop=True).then_inc(pv_done, 1)

            def conv(l):
                for i in range(CONV):
                    jj, kind = i // 3, i % 3
                    slot = PHASES["conv"].slot(i)
                    pe.wait_ge(lo_ready[slot], uses("conv", i, l))
                    if i == 0:
                        pe.wait_ge(qkv_done, l * QKV + QKV - 1)
                    pe.wait_ge([cc_done, u_done, m_done][kind], l * CT + (jj + PRIME))
                    tile8(bank[(2, 3, 0)[kind]][:, 0:T], slot)
                    if i < HEADS:
                        scores_first(l, i)
                    if 0 <= i - 2 < HEADS:
                        transpose_first(l, i - 2)
                    if 0 <= i - 3 < HEADS:
                        pv_first(l, i - 3)
                pe.wait_ge(o_done, (l + 1) * HEADS + PRIME)
                for j in range(QT):
                    for t in range(2):
                        tr = pe.transpose(bank[4 + j][:, t * P:(t + 1) * P], O32[:, t, j * P:(j + 1) * P], ident)
                    tr.then_inc(ot_done, 1)

            order = list(range(QT, QT + CT)) + list(range(QT))

            def wout(l, q):
                for i in range(2):
                    slot = PHASES["wout"].slot(i)
                    pe.wait_ge(lo_ready[slot], uses("wout", i, l))
                pe.wait_ge(qkv_done, l * QKV + QKV)
                pe.wait_ge(m_done, (l + 1) * CT + PRIME)
                s0, s1 = PHASES["wout"].slot(0), PHASES["wout"].slot(1)
                for n, k in enumerate(order):
                    pe.wait_ge(mix_lo, l * 8 + n + 1)
                    a = product(bank[0][:, 0:T], s0, k, ghi[:, k, :], glo[:, k, :], n == 0, n == KT - 1)
                    b = product(bank[1][:, 0:T], s1, k, ghi[:, k, :], glo[:, k, :], n == 0, n == KT - 1)
                a.then_inc(w_used[s0], 1)
                b.then_inc(w_used[s1], 1)
                for o in range(2, KT):
                    slot = PHASES["wout"].slot(o)
                    pe.wait_ge(lo_ready[slot], uses("wout", o, l))
                    pe.wait_ge(x_ready[o % 2], q * 4 + (o // 2 + PRIME - 4))
                    for k in range(KT):
                        mm = product(bank[o % 2][:, 0:T], slot, k, ghi[:, k, :], glo[:, k, :], k == 0, k == KT - 1)
                    mm.then_inc(w_used[slot], 1)
                    sum_squares(o % 2, q * 4 + o // 2, o == 2, False)
                for o in (6, 7):
                    sum_squares(o % 2, q * 4 + o // 2 + 1, False, o == 7)

            pe.wait_ge(const_set, 2)
            for k in range(KT):
                sum_squares(k % 2, k // 2 + 1, k == 0, k == KT - 1)
            pe.wait_ge(pad_set, 2)
            pe.wait_ge(c_loaded, C_LOADS)
            with pe.Fori(0, LAYERS) as l:
                gate_up("gu1", l, 0, l * 3)
                down("dn1", l, 0, l * 3 + 1)
                qkv(l, l * 3 + 1)
                conv(l)
                wout(l, l * 3 + 2)
                gate_up("gu2", l, 1, l * 3 + 2)
                down("dn2", l, 1, l * 3 + 3)
            for k in range(KT):
                if k == 0:
                    pe.wait_ge(rstd_done, 7)
                sum_squares(k % 2, 7 * 4 + k // 2 + 1, k == 0, k == KT - 1, TM)

            def begin(piece):
                pe.wait_ge(lo_ready[piece % SLOTS], uses2(piece))

            def run(outs, n):
                kind, k, piece = outs[n]
                slot, last = piece % SLOTS, ends_piece(outs, n)
                o = bank[n % 4]
                if kind in ("kv", "kpe", "ql", "naq", "nak", "gate"):
                    begin(piece)
                    if piece == 0:
                        pe.wait_ge(h_lo, 7 * KT)
                    for i in range(KT):
                        mm = product(o[:, 0:TOKENS[kind]], slot, i, *hcols(i, TOKENS[kind]), i == 0, i == KT - 1)
                elif kind in ("kn", "qn", "qpe"):
                    src, wid = latw["kv" if kind == "kn" else "ql"]
                    if k % 4 == 0:
                        begin(piece)
                    if k == 0:
                        pe.wait_ge(pj_taken, 2 if kind == "kn" else 5)
                    for i in range(2):
                        c = src + i * wid
                        mm = product(o[:, 0:TOKENS[kind]], slot, 2 * (k % 4) + i, yhi[:, c:c + wid],
                                     ylo[:, c:c + wid], i == 0, i == 1)
                elif kind == "uv":
                    tt = k % 3
                    if tt == 0:
                        begin(piece)
                    if k == 0:
                        pe.wait_ge(pad_set, 4)
                    for i in range(2):
                        c = latw["kv"][0] + i * TM + tt * P
                        wh, wl = whi[:, slot, i * 512:(i + 1) * 512], wlo[:, slot, i * 512:(i + 1) * 512]
                        pe.matmul(o[:], yhi[:, c:c + P], wh, start=i == 0, stop=False)
                        pe.matmul(o[:], ylo[:, c:c + P], wh, start=False, stop=False)
                        mm = pe.matmul(o[:], yhi[:, c:c + P], wl, start=False, stop=i == 1)
                else:
                    tt = k % 3

                    def values(kp_, tile):
                        s = (piece - 3 + kp_) % SLOTS
                        for i in range(2):
                            c = (2 * kp_ + i) * TM + tile * P
                            b = bank[out_bank(outs, n - tt + tile)]
                            wh, wl = whi[:, s, i * 512:(i + 1) * 512], wlo[:, s, i * 512:(i + 1) * 512]
                            pe.matmul(b[:], hhi[:, c:c + P], wh, start=kp_ + i == 0, stop=False)
                            pe.matmul(b[:], hlo[:, c:c + P], wh, start=False, stop=False)
                            mm = pe.matmul(b[:], hhi[:, c:c + P], wl, start=False, stop=kp_ == 3 and i == 1)
                        return mm

                    if tt == 0:
                        for kp_ in range(3):
                            begin(piece - 3 + kp_)
                            for tile in range(3):
                                mm = values(kp_, tile)
                            mm.then_inc(w_used[(piece - 3 + kp_) % SLOTS], 1)
                        begin(piece)
                    mm = values(3, tt)
                mm.then_inc(w_used[slot] if last else pj_done, 1)

            def sums_of(outs, st, n):
                g = st["done_at"].get(n)
                if g is not None:
                    kind = outs[st["groups"][g][0]][0]
                    lhs = ones64 if NORM_WIDTH[kind] == 64 else ones[:]
                    if g - st["g0"] >= 2:
                        pe.wait_ge(rstd_done, 8 + g - 1)
                    for a, i in enumerate(st["groups"][g]):
                        m = st["normed"][i]
                        sum_squares(m % 2, 32 + m // 2 + 1, a == 0, i == st["groups"][g][-1], TOKENS[kind],
                                    6 + g % 2, lhs)

            def projections(outs, st):
                for n in range(len(outs) + LAG + 2):
                    nav = n < len(outs) and outs[n][0] == "nav"
                    if n < len(outs):
                        if nav and outs[n][1] == 0:
                            pe.wait_ge(y_done, 8)
                        if n >= 4:
                            pe.wait_ge(pj_taken, st["n0"] + n - 3)
                        run(outs, n)
                    sums_of(outs, st, n - LAG)
                    i = n - LAG - 1
                    if i in st["ropes"]:
                        c, nt = st["ropes"][i], TOKENS[outs[i][0]]
                        pe.wait_ge(pj_taken, st["n0"] + i + 1)
                        if c >= 1:
                            pe.wait_ge(rt_done, c)
                        pe.matmul(bank[SCORE][:, 0:nt], rot, S[:, c % 2, 0:nt], start=True, stop=True)\
                          .then_inc(rot_done, 1)
                    if outs is NA and n < 8:
                        if n == 0:
                            pe.wait_ge(o_done, LAYERS * HEADS + 2 * MH + PRIME)
                        if n >= 2:
                            pe.wait_ge(y_done, n - 1)
                        feature_major(bank[4 + n % 2], n)

            def feature_major(b, j):
                for t in range(2):
                    tr = pe.transpose(b[:, t * P:(t + 1) * P], O32[:, t, j * P:(j + 1) * P], ident)
                tr.then_inc(ot_done, 1)

            def transposes(v):
                pe.wait_ge(exp_done, LAYERS * HEADS + v + 1)
                pe.wait_ge(pt_done, LAYERS * HEADS + v - 1 + PRIME)
                o, pr = bank[2 + v % 2], Pr[:, v % 2]
                pe.transpose(o[:, 0:BLK], pr[:, 0:BLK], ident)
                pe.transpose(o[:, BLK:2 * BLK], pr[:, BLK:2 * BLK], ident)
                pe.transpose(o[0:META, 2 * BLK:3 * BLK], pr[:, 2 * BLK:TM], ident).then_inc(tr_done, 1)

            def values_of(v, h, width):
                pe.wait_ge(pt_done, LAYERS * HEADS + v + (1 + PRIME))
                pe.wait_ge(o_done, LAYERS * HEADS + v - 1 + PRIME)
                o, pt = bank[4 + v % 2][:, 0:width], PT[:, v % 2]
                c = slice(h * width, (h + 1) * width)
                pe.matmul(o, pt[:, 0:BLK], V[:, 0, c], start=True, stop=False)
                pe.matmul(o, pt[:, BLK:2 * BLK], V[:, 1, c], start=False, stop=False)
                pe.matmul(o, pt[0:META, 2 * BLK:3 * BLK], V[0:META, 2, c], start=False, stop=True)\
                  .then_inc(pv_done, 1)

            def fill(m, half):
                piece = FILL0 + m
                if half == 0:
                    begin(piece)
                    if m >= 2:
                        pe.wait_ge(fill_taken, m - 1)
                    if m == 8:
                        pe.wait_ge(y_lo, 8)
                for k in range(4 * half, 4 * half + 4):
                    xh, xl = hcols(k) if m < 8 else (yhi[:, k * T:(k + 1) * T], ylo[:, k * T:(k + 1) * T])
                    mm = product(bank[6 + m % 2][:, 0:T], piece % SLOTS, k, xh, xl, k == 0, k == KT - 1)
                if half:
                    mm.then_inc(w_used[piece % SLOTS], 1)

            def attention(v0, units, width, mla):
                for i in range(units + 3):
                    if i < units:
                        v, h, t = v0 + i, i // 2, i % 2
                        if i >= 2:
                            if mla:
                                pe.wait_ge(exp_done, LAYERS * HEADS + v - 1)
                            else:
                                pe.wait_ge(s_add, LAYERS * HEADS + 2 * (i - 1) + PRIME)
                        o, tok = bank[v % 2][:, 0:TM], slice(t * P, (t + 1) * P)
                        if mla:
                            r = h % 2 * MR
                            pe.matmul(o, qn[:, h, tok], kn[:, h, :], start=True, stop=False)
                            pe.matmul(o, qp[r:r + MR, h // 2, tok], kp[r:r + MR, :], start=False, stop=True)\
                              .then_inc(sc_done, 1)
                        else:
                            r = h % 2 * HD
                            pe.matmul(o, qn[r:r + HD, h // 2, tok], kn[r:r + HD, h // 2, :], start=True, stop=True)\
                              .then_inc(sc_done, 1)
                    if not mla and i // 2 < FILL:
                        fill(i // 2, i % 2)
                    if 3 <= i:
                        values_of(v0 + i - 3, (i - 3) // 2, width)
                    if 1 <= i <= units:
                        transposes(v0 + i - 1)

            def y_tiles(o, slot, y0):
                for k in range(KT):
                    y = slice((y0 + k) * T, (y0 + k + 1) * T)
                    mm = product(o, slot, k, yhi[:, y], ylo[:, y], k == 0, k == KT - 1)
                mm.then_inc(w_used[slot], 1)

            projections(MLA, ST_MLA)
            pe.wait_ge(rope_done, 1 + MH // 2)
            pe.wait_ge(pj_taken, len(MLA))
            attention(0, 2 * MH, P, True)
            projections(NA, ST_NA)
            pe.wait_ge(pj_taken, len(MLA) + len(NA))
            pe.wait_ge(y_done, 8)
            attention(2 * MH, 2 * NH, HD, False)
            pe.wait_ge(o_done, LAYERS * HEADS + 2 * MH + 2 * NH + PRIME)
            for j in range(4):
                feature_major(bank[2 + j], j)
            for piece in (FILL0 + FILL, FILL0 + FILL + 1):
                begin(piece)
            pe.wait_ge(fill_taken, FILL)
            for k in range(KT):
                if k < 4:
                    pe.wait_ge(y_done, 8 + k + 1)
                    feature_major(bank[2 + k], 4 + k)
                pe.wait_ge(y_lo, 8 + k + 1)
                for o in range(2):
                    slot, y = (FILL0 + FILL + o) % SLOTS, slice((8 + k) * T, (9 + k) * T)
                    mm = product(bank[o][:, 0:T], slot, k, yhi[:, y], ylo[:, y], k == 0, k == KT - 1)
                    if k == KT - 1:
                        mm.then_inc(w_used[slot], 1)
            for o in range(2, 8):
                piece = FILL0 + FILL + o
                begin(piece)
                if o >= 4:
                    pe.wait_ge(res_done, o - 3)
                y_tiles(bank[(0, 1, 6, 7)[o % 4]][:, 0:T], piece % SLOTS, 8)


def out_bank(outs, n):
    return (4, 5, 0, 1, 2, 3)[outs[n][1]] if outs[n][0] == "nav" else n % 4


def ends_piece(outs, n):
    return n + 1 == len(outs) or outs[n + 1][2] != outs[n][2]


def mid_outputs(outs, n):
    before = 0 if outs is MLA else sum(not ends_piece(MLA, i) for i in range(len(MLA)))
    return before + sum(not ends_piece(outs, i) for i in range(n + 1))


def structure(outs, n0, g0, m0, base):
    st = {"n0": n0, "g0": g0, "groups": {}, "done_at": {}, "normed": {}, "latent": {}, "ropes": {}, "pieces": {}}
    g, seen = g0, base
    for n, (kind, k, piece) in enumerate(outs):
        st["pieces"][n] = list(range(seen, piece + 1))
        seen = piece + 1
        if kind in NORM_WIDTH:
            st["normed"][n] = m0 + len(st["normed"])
            if kind in ("kv", "ql"):
                st["latent"][n] = len(st["latent"])
            if kind in ("kpe", "qpe"):
                st["ropes"][n] = len(st["ropes"])
            st["groups"].setdefault(g, []).append(n)
            if kind not in ("kv", "ql") or k == 1:
                st["done_at"][n] = g
                g += 1
    return st


MLA, NA = mla_outputs(), na_outputs()
ST_MLA = structure(MLA, 0, 0, 0, 0)
ST_NA = structure(NA, len(MLA), len(ST_MLA["groups"]), len(ST_MLA["normed"]), MLA_PIECES)
MLA_SCALE = float(np.float32((MN + MR) ** -0.5))


def tiles(w):
    k, n = w.shape
    return w.reshape(k // P, P, n // P, P).transpose(0, 2, 1, 3)


def by_output(w):
    t = tiles(w)
    kt, nt = t.shape[:2]
    t = t.transpose(1, 0, 2, 3).reshape(nt * (kt // 8), 8, P, P)
    return t.transpose(0, 2, 1, 3).reshape(-1, P, PT8)


def short_k(w):
    t = tiles(w).transpose(1, 0, 2, 3)
    return t.reshape(-1, 8, P, P).transpose(0, 2, 1, 3).reshape(-1, P, PT8)


def by_columns(w):
    k, n = w.shape
    t = w.reshape(k // (2 * P), 2, P, n // 512, 512).transpose(3, 0, 2, 1, 4)
    return t.reshape(-1, P, PT8)


def kernel(**inputs):
    import concourse.bacc as bacc
    from concourse.bass_utils import run_bass_kernel_spmd

    a = {k: np.asarray(v) for k, v in inputs.items()}
    heads = np.arange(HEADS).reshape(2, QT).T.reshape(-1)
    hcol = (heads[:, None] * HD + np.arange(HD)[None]).reshape(-1)
    pieces, downs = [], []
    for l in range(LAYERS):
        def ffn(name):
            g, up = by_output(a[name + "_wg"][l]), by_output(a[name + "_wu"][l])
            pieces.append(np.stack([g, up], 1).reshape(-1, P, PT8))
            d = tiles(a[name + "_wd"][l]).transpose(1, 0, 2, 3).reshape(DN, HALF, P, P)
            downs.append(d.transpose(0, 2, 1, 3).reshape(DN, P, PTD))

        ffn("ffn1")
        w = a["w_in"][l]
        attn = HEADS * HD
        qkv = np.concatenate([w[:, 0:attn][:, hcol], w[:, attn:attn + 2 * P]], 1)
        cb, cc, ch = (w[:, attn + 2 * P + i * 512:attn + 2 * P + (i + 1) * 512] for i in range(3))
        pieces.append(by_output(qkv))
        pieces.append(np.stack([by_output(cc), by_output(ch), by_output(cb)], 1).reshape(-1, P, PT8))
        wo = a["w_out"][l]
        pieces.append(by_output(np.concatenate([wo[0:attn][hcol], wo[attn:]], 0)))
        ffn("ffn2")
    w = a["w_in_2"][0]
    cut = np.cumsum([0, 256, 256, MR, D, D, D, D, D])
    qlat, kvlat, kpe, gmla, naq, nak, nav, gna = (w[:, cut[i]:cut[i + 1]] for i in range(8))
    ukv = a["w_ukv_2"][0].reshape(256, MH, 2, P)
    uq = a["w_uq_2"][0].reshape(256, MH, MN + MR)
    kinds = {"kv": by_output(kvlat), "kpe": by_output(np.concatenate([kpe, kpe], 1)), "ql": by_output(qlat),
             "kn": short_k(ukv[:, :, 0].reshape(256, -1)), "uv": by_columns(ukv[:, :, 1].reshape(256, -1)),
             "qn": short_k(uq[:, :, 0:MN].reshape(256, -1)), "qpe": short_k(uq[:, :, MN:].reshape(256, -1)),
             "gate": by_output(gmla)}
    taken = dict.fromkeys(kinds, 0)
    for n, (kind, _, _) in enumerate(MLA):
        if ends_piece(MLA, n):
            pieces.append(kinds[kind][taken[kind]:taken[kind] + 1])
            taken[kind] += 1
    wo2 = by_output(a["w_out_2"][0])
    pieces += [by_output(naq), by_output(nak), by_columns(nav), by_output(gna), wo2[0::2], wo2[1::2]]
    w8, wd = np.concatenate(pieces, 0), np.concatenate(downs, 0)

    def cols(v):
        return v.reshape(-1, P).T

    def twice(v):
        return np.concatenate([v, v])[:, None]

    norms = [a[n][l] for l in range(LAYERS) for n in ("ffn1_norm", "mix_norm", "ffn2_norm")]
    norms += [a["final_norm"], a["norm_w_2"][0]]
    conv = a["conv_w"].reshape(LAYERS, 3, CT, P).transpose(3, 0, 2, 1).reshape(P, -1)
    small = np.concatenate(
        [cols(np.concatenate(norms)), conv, np.broadcast_to(a["attn_sink"].reshape(1, -1), (P, LAYERS * HEADS)),
         cols(a["kv_lat_norm_w_2"][0]), cols(a["q_lat_norm_w_2"][0]), cols(a["mla_kn_w_2"][0]), cols(a["mla_qn_w_2"][0]),
         twice(a["mla_kpe_w_2"][0]), twice(a["mla_qpe_w_2"][0]), twice(a["na_q_norm_w_2"][0]),
         twice(a["na_k_norm_w_2"][0])], 1)

    f = np.float32
    i = np.arange(P)
    same = (i[:, None] // 64 == i[None] // 64)
    swap = same & (i[:, None] % 64 == (i[None] + 32) % 64)
    mats = np.stack([np.eye(P), same, np.where(swap, np.where(i[None] % 64 < 32, -1, 1), 0)], 1).astype(f)
    qi, kj = np.arange(BLK)[:, None], np.arange(2 * BLK)[None]
    dist = qi + BLK - kj
    slopes = np.exp2(-8.0 * np.arange(1, HEADS + 1, dtype=f) / HEADS).astype(f)
    band = np.where((dist >= 0) & (dist < BLK), -slopes[:, None, None] * dist.astype(f), f(MASKED)).astype(f)
    btab = np.concatenate([band[:, :, BLK:], band], 2).transpose(1, 0, 2)
    pos = np.concatenate([np.arange(META, TM), np.arange(META)]).astype(f)
    freq = (f(10000.0) ** -(np.arange(0, MR, 2, dtype=f) / f(MR))).astype(f)
    ang = (pos[None] * freq[i % 32][:, None]).astype(f)
    rope = np.stack([np.cos(ang), np.sin(ang)], 1).astype(f)
    c = np.arange(GW)
    c0 = np.clip(c - WC // 2, 0, GW - WC)[:, None]
    mask = np.where((c[None] >= c0) & (c[None] < c0 + WC), 0, MASKED).astype(f)
    bias = a["na_rel_bias_2"][0].reshape(NH, -1)
    at = [((np.arange(6)[None, :, None] + 5 - half) * RELC + WC - 1 + c[None, None, :] - c[:, None, None])
          for half in range(2)]
    rel = bias[:, np.concatenate(at, 0)]
    arrays = {
        "in_xT": a["x"][0].T.reshape(KT, P, T).transpose(1, 0, 2),
        "in_metaT": a["meta_tokens_2"].T.reshape(KT, P, META).transpose(1, 0, 2),
        "in_w8": w8, "in_wd": wd, "in_small": small, "in_mats": mats, "in_btab": btab, "in_rope": rope,
        "in_colmask": np.concatenate([mask, mask], 0),
        "in_metabias": np.broadcast_to(a["na_meta_bias_2"][0][None], (P, NH, META)),
        "in_relbias": rel,
    }
    arrays = {k: np.ascontiguousarray(v) for k, v in arrays.items()}
    nc = bacc.Bacc("TRN2", target_bir_lowering=False, num_devices=1)
    args = [nc.dram_tensor(k, v.shape, F32, kind="ExternalInput").ap() for k, v in arrays.items()]
    out = nc.dram_tensor("out_T", (KT, P, T), F32, kind="ExternalOutput").ap()
    build(nc, *args, out)
    r = run_bass_kernel_spmd(nc, [arrays], core_ids=[0])
    return r.results[0]["out_T"].reshape(1, D, T).transpose(0, 2, 1)
```

```python
from contextlib import ExitStack

import numpy as np
import concourse.bass as bass
from concourse import mybir

F32 = mybir.dt.float32
F32R = mybir.dt.float32r
ACT = mybir.ActivationFunctionType
ALU = mybir.AluOpType
AX_X = mybir.AxisListType.X

P = 128
D = 1024
KT = D // P
T = 256
META = 16
TM = T + META
LAYERS = 2
FF = 2816
FT = FF // P
EPS = 1e-6
MASKED = -1e30
HEADS, HD, BLK = 8, 64, 128
QT = HEADS * HD // P
CT = 4
MH, MN, MR = 8, 128, 64
NH = 16
GW, WR, WC = 64, 4, 16
RELR, RELC = 15, 31
SLOTS = 4
PRIME = 1
LEAD = SLOTS - 1
PT8 = 8 * P
HALF = FT // 2
PTD = HALF * P
GU, DN, QKV, CONV, WOUT = 2 * FT, 2 * KT, QT + 2, 3 * CT, KT
W8_LAYER = 2 * GU + QKV + CONV + WOUT


def slot_uses(pieces, start=0):
    return [len(range((s - start) % SLOTS, pieces, SLOTS)) for s in range(SLOTS)]


class Phase:

    def __init__(self, pieces, start, before, w8, cols):
        self.pieces, self.start, self.before, self.w8, self.cols = pieces, start, before, w8, cols

    def slot(self, i):
        return (self.start + i) % SLOTS

    def uses(self, i, lap=0):
        return self.before[self.slot(i)] + i // SLOTS + 1 + lap


def plan_layer():
    phases, before, w8 = {}, [0] * SLOTS, 0
    for name, pieces, start, cols in (
        ("gu1", GU, 0, PT8), ("dn1", DN, 0, PTD), ("qkv", QKV, 0, PT8), ("conv", CONV, 0, PT8),
        ("wout", WOUT, CONV % SLOTS, PT8), ("gu2", GU, 0, PT8), ("dn2", DN, 0, PTD),
    ):
        phases[name] = Phase(pieces, start, list(before), w8, cols)
        before = [b + u for b, u in zip(before, slot_uses(pieces, start))]
        if cols == PT8:
            w8 += pieces
    return phases, before


PHASES, LAYER_USES = plan_layer()

MLA_PIECES = 2 + 1 + 2 + 2 + 2 + 2 + 1 + 8
NA_PIECES = 24
FILL = 8 + 8
FILL0 = MLA_PIECES + NA_PIECES
SECOND = FILL0 + FILL + 8


def mla_outputs():
    outs, piece = [], 0
    for kinds in ([("kv", 0)], [("kv", 1)], [("kpe", 0)], [("ql", 0)], [("ql", 1)], [("gate", 0)],
                  [("uv", t) for t in range(3)], [("kn", h) for h in range(4)], [("gate", 1)],
                  [("kn", h) for h in range(4, 8)], [("gate", 2)], [("uv", 3 + t) for t in range(3)],
                  [("qn", h) for h in range(4)], [("gate", 3)], [("qn", h) for h in range(4, 8)], [("gate", 4)],
                  [("qpe", j) for j in range(MH // 2)], [("gate", 5)], [("gate", 6)], [("gate", 7)]):
        outs += [(kind, k, piece) for kind, k in kinds]
        piece += 1
    return outs


def na_outputs():
    base = MLA_PIECES
    outs = [("naq", j, base + j) for j in range(8)]
    outs += [("nak", j, base + 8 + j) for j in range(8)]
    outs += [("nav", 3 * c + t, base + 16 + 4 * c + 3) for c in range(2) for t in range(3)]
    return outs


MIX_ORDER = [*range(QT, QT + CT - 1), *range(QT), QT + CT - 1]
LAG = 1
NORM_WIDTH = {"kv": 256, "kpe": 64, "ql": 256, "kn": 128, "qn": 128, "qpe": 64, "naq": 64, "nak": 64}
TOKENS = {"kv": TM, "kpe": TM, "ql": T, "kn": TM, "qn": T, "qpe": T, "naq": T, "nak": TM, "gate": T}

G_NORM = 0
G_CONV = G_NORM + 8 * KT
G_SINK = G_CONV + LAYERS * CT * 3
G_HEAD = G_SINK + LAYERS * HEADS
HEAD_GAIN = {"kv": 0, "ql": 2, "kn": 4, "qn": 5, "kpe": 6, "qpe": 7, "naq": 8, "nak": 9}
SMALL = G_HEAD + 10


def build(nc, xT, metaT, w8, wd, small, mats, btab, rope, colmask, metabias, relbias, out):
    with ExitStack() as ctx:
        def sem(name):
            return ctx.enter_context(nc.semaphore(name))

        def sb(name, shape, dt=F32, stack=ctx):
            return stack.enter_context(nc.sbuf_tensor(name, shape, dt))

        x = sb("x_res", [P, KT, TM])
        raw = sb("w_raw", [P, SLOTS, PTD])
        whi = sb("w_hi", [P, SLOTS, PTD], F32R)
        wlo = sb("w_lo", [P, SLOTS, PTD], F32R)
        hhi = sb("h_hi", [P, KT * TM + P - META], F32R)
        hlo = sb("h_lo", [P, KT * TM + P - META], F32R)
        sq = sb("squares", [P, 2, TM])
        h32 = sb("h_32", [P, 4, TM])
        sg = sb("silu_gate", [P, 2, T])
        g32 = sb("gated_32", [P, 2, T])
        lnv = sb("ln_mean", [P, 2, TM])
        acc = lnv[:, 1]
        rs = sb("rstd", [P, 2, TM])
        S = sb("scores_sb", [P, 2, 3 * BLK])
        Pr = sb("probs", [P, 2, 3 * BLK])
        PT = sb("probs_T", [P, 2, 3 * BLK])
        O32 = sb("attn_out", [P, 2, D])
        sml = sb("small_sb", [P, SMALL])
        mat = sb("mats_sb", [P, 3, P])
        ones = sb("ones_sb", [P, P])
        rop = sb("rope_sb", [P, 2, TM])
        cmask = sb("colmask_sb", [P, GW])
        metab = sb("metabias_sb", [P, NH, META])
        mx = sb("row_max", [P, 2 * NH])
        nm = sb("neg_max", [P, 2 * NH])
        sums = sb("row_sums", [P, 2 * NH])
        es = sb("sink_terms", [P, 2 * HEADS])
        den = sb("denominators", [P, 2 * NH])
        rec = sb("reciprocals", [P, 2 * NH])
        ident, ones64, rot = mat[:, 0, :], mat[:, 1, :], mat[:, 2, :]
        with ExitStack() as first:
            ghi = sb("g_hi", [P, FT, T], F32R, first)
            glo = sb("g_lo", [P, FT, T], F32R, first)
            bt = sb("btab_sb", [P, HEADS, 3 * BLK], F32, first)
            q32 = sb("q_32", [P, QT, T], F32, first)
            k32 = sb("k_32", [P, T], F32, first)
            v32 = sb("v_32", [P, 2, P], F32, first)
            cc32 = sb("conv_c", [P, T], F32, first)
            u = sb("conv_u", [P, T + 2], F32, first)
            ya = sb("conv_ya", [P, T], F32, first)
            yb = sb("conv_yb", [P, T], F32, first)
            yc = sb("conv_yc", [P, T], F32, first)
            m32 = sb("mix_32", [P, 2, T], F32, first)
        with ExitStack() as second:
            yhi = sb("y_hi", [P, 16 * T], F32R, second)
            ylo = sb("y_lo", [P, 16 * T], F32R, second)
            kn = sb("k_heads", [P, 8, TM], F32, second)
            qn = sb("q_heads", [P, 8, T], F32, second)
            qp = sb("q_rope", [P, MH // 2, T], F32, second)
            V = sb("v_heads", [P, 3, D], F32, second)
            kp = sb("k_rope", [P, TM], F32, second)
            sgate = sb("silu_all", [P, 8, T], F32, second)
            rel = sb("rel_bias", [P, 2, 6, GW], F32, second)
        QL0 = 2 * TM + P - META
        latw = {"kv": (0, TM), "ql": (QL0, T)}

        bank = [ctx.enter_context(nc.psum_tensor(f"bank{i}", [P, 512], F32)) for i in range(8)]
        SCORE, TRANS, OUT, SUM = 4, (5, 7), (6, 1), 7

        raw_full = [sem(f"raw_full{s}") for s in range(SLOTS)]
        hi_ready = [sem(f"hi_ready{s}") for s in range(SLOTS)]
        lo_ready = [sem(f"lo_ready{s}") for s in range(SLOTS)]
        w_used = [sem(f"w_used{s}") for s in range(SLOTS)]
        x_loaded = [sem(f"x_loaded{p}") for p in range(2)]
        g_loaded = sem("g_loaded")
        c_loaded, b_loaded = sem("c_loaded"), sem("b_loaded")
        const_set, pad_set = sem("const_set"), sem("pad_set")
        sq_done = [sem(f"sq_done{p}") for p in range(2)]
        acc_step, sum_done = sem("acc_step"), sem("sum_done")
        sq_used = [sem(f"sq_used{p}") for p in range(2)]
        ln_done, rstd_done = sem("ln_done"), sem("rstd_done")
        h32_done, h_hi, h_lo = sem("h32_done"), sem("h_hi_done"), sem("h_lo_done")
        x_ready = [sem(f"x_ready{p}") for p in range(2)]
        gate_scaled = [sem(f"gate_scaled{p}") for p in range(2)]
        up_scaled = [sem(f"up_scaled{p}") for p in range(2)]
        silu_done = [sem(f"silu_done{p}") for p in range(2)]
        g_mul = [sem(f"g_mul{p}") for p in range(2)]
        g_hi = [sem(f"g_hi_done{p}") for p in range(2)]
        g_lo = [sem(f"g_lo_done{p}") for p in range(2)]
        qkv_done = sem("qkv_done")
        rs2_done = sem("rs2_done")
        vt_done, v_done = sem("vt_done"), sem("v_done")
        cc_done, u_done, y_step = sem("cc_done"), sem("u_done"), sem("y_step")
        m_done, mix_hi, mix_lo = sem("m_done"), sem("mix_hi"), sem("mix_lo")
        sc_done, s_add, mx_done, nm_done = sem("sc_done"), sem("s_add"), sem("mx_done"), sem("nm_done")
        exp_done, den_done, rec_done = sem("exp_done"), sem("den_done"), sem("rec_done")
        tr_done, pt_done, pv_done, o_done = sem("tr_done"), sem("pt_done"), sem("pv_done"), sem("o_done")
        ot_done = sem("ot_done")
        fx_done = sem("fx_done")
        pj_done, pj_taken = sem("pj_done"), sem("pj_taken")
        rot_done, rt_done, rope_done = sem("rot_done"), sem("rt_done"), sem("rope_done")
        rel_loaded = [sem(f"rel_loaded{p}") for p in range(2)]
        rel_ready = sem("rel_ready")
        silu_all = sem("silu_all_done")
        th_done = sem("th_done")
        fill_taken = sem("fill_taken")
        y_done, y_hi, y_lo = sem("y_done"), sem("y_hi_done"), sem("y_lo_done")
        res_done, stored = sem("res_done"), sem("stored")

        block = ctx.enter_context(nc.Block())

        def uses(phase, i, layer, lap=0):
            ph = PHASES[phase]
            return layer * LAYER_USES[ph.slot(i)] + lap + (ph.uses(i) + PRIME)

        def uses0(n):
            return n + PRIME

        def uses2(i):
            return LAYERS * LAYER_USES[i % SLOTS] + i // SLOTS + (1 + PRIME)

        def y32(y):
            return (sg if y >= 8 and y // 2 % 2 else g32)[:, y % 2]

        def wait_output(eng, outs, n):
            piece = outs[n][2]
            if ends_piece(outs, n):
                eng.wait_ge(w_used[piece % SLOTS], uses2(piece))
            else:
                eng.wait_ge(pj_done, mid_outputs(outs, n))

        C_LOADS = 16 * 5

        @block.sync
        def _(sp):
            for s in raw_full:
                sp.sem_inc(s, 16 * PRIME)
            for p in range(2):
                half = slice(p * KT // 2, (p + 1) * KT // 2)
                sp.dma_start(x[:, half, 0:T], xT[:, half]).then_inc(x_loaded[p], 16)

            def load(src, cols, slot, count):
                sp.wait_ge(lo_ready[slot], count - 1)
                sp.dma_start(raw[:, slot, 0:cols], src).then_inc(raw_full[slot], 16)

            def load_phase(name, l, ffn=None):
                ph = PHASES[name]

                def piece(i, j):
                    src = w8[l * W8_LAYER + (ph.w8 + i) + j * SLOTS] if ffn is None else \
                        wd[l * (2 * DN) + (ffn * DN + i) + j * SLOTS]
                    load(src, ph.cols, ph.slot(i), uses(name, i, l, j))

                with sp.Fori(0, ph.pieces // SLOTS) as j:
                    for r in range(SLOTS):
                        piece(r, j)
                for i in range(ph.pieces // SLOTS * SLOTS, ph.pieces):
                    piece(i, 0)

            with sp.Fori(0, LAYERS) as l:
                load_phase("gu1", l)
                load_phase("dn1", l, 0)
                load_phase("qkv", l)
                load_phase("conv", l)
                load_phase("wout", l)
                load_phase("gu2", l)
                load_phase("dn2", l, 1)
            with sp.Fori(0, SECOND // SLOTS) as j:
                for r in range(SLOTS):
                    load(w8[(LAYERS * W8_LAYER + r) + j * SLOTS], PT8, r, uses2(r) + j)
            for o in range(KT):
                sp.wait_ge(res_done, o + 1)
                sp.dma_start(out[o], x[:, o, 0:T]).then_inc(stored, 16)
            sp.wait_ge(stored, 16 * KT)

        @block.gpsimd
        def _(pool):
            pool.sem_inc(y_step, PRIME)
            pool.memset(ones[:], 1.0).then_inc(const_set, 1)
            pool.memset(u[:, 0:2], 0.0).then_inc(const_set, 1)
            pool.memset(hhi[:, KT * TM:].bitcast(F32), 0.0).then_inc(pad_set, 1)
            pool.memset(hlo[:, KT * TM:].bitcast(F32), 0.0).then_inc(pad_set, 1)

            def add_squares(q, n=T, tiles=range(KT - 1)):
                for i, k in enumerate(tiles):
                    pool.wait_ge(sq_done[k % 2], q * 4 + k // 2 + 1)
                    if k == 0:
                        pool.tensor_copy(acc[:, 0:n], sq[:, 0, 0:n]).then_inc(acc_step, 1)
                    else:
                        pool.wait_ge(acc_step, q * 7 + i)
                        pool.tensor_tensor(acc[:, 0:n], acc[:, 0:n], sq[:, k % 2, 0:n], ALU.add)\
                            .then_inc(acc_step, 1)

            add_squares(0)
            pool.wait_ge(h32_done, KT)
            pool.dma_start(mat[:], mats).then_inc(c_loaded, 16)
            pool.dma_start(rop[:], rope).then_inc(c_loaded, 16)
            pool.dma_start(cmask[:], colmask).then_inc(c_loaded, 16)
            pool.dma_start(metab[:], metabias).then_inc(c_loaded, 16)
            pool.dma_start(x[:, :, T:TM], metaT).then_inc(c_loaded, 16)
            pool.dma_start(bt[:], btab).then_inc(b_loaded, 16)
            pool.wait_ge(g_loaded, 16)
            for l in range(LAYERS):
                add_squares(3 * l + 1)
                for jj in range(CT):
                    c = l * CT + jj
                    tap = [sml[:, at:at + 1] for at in range(G_CONV + 3 * c, G_CONV + 3 * c + 3)]
                    pool.wait_ge(u_done, c + (1 + PRIME))
                    if c > 0:
                        pool.wait_ge(m_done, c + PRIME)
                    for n, at in enumerate((ya, yb, yc)):
                        pool.tensor_scalar(at[:], u[:, 2 - n:T + 2 - n], tap[2 - n], None, ALU.mult).then_inc(y_step, 1)
                    pool.wait_ge(y_step, c * 6 + (3 + PRIME))
                    pool.tensor_tensor(yb[:], yb[:], yc[:], ALU.add).then_inc(y_step, 1)
                    pool.wait_ge(y_step, c * 6 + (4 + PRIME))
                    pool.tensor_tensor(ya[:], ya[:], yb[:], ALU.add).then_inc(y_step, 1)
                    pool.wait_ge(y_step, c * 6 + (5 + PRIME))
                    pool.tensor_tensor(ya[:], ya[:], rs[:, 0, 0:T], ALU.mult).then_inc(y_step, 1)
                add_squares(3 * l + 2)
                add_squares(3 * l + 3)
            add_squares(7, TM, range(0, KT, 2))
            pool.wait_ge(fx_done, KT)
            pool.memset(yhi[:, 2 * TM:QL0].bitcast(F32), 0.0).then_inc(pad_set, 1)
            pool.memset(ylo[:, 2 * TM:QL0].bitcast(F32), 0.0).then_inc(pad_set, 1)
            for h in range(NH):
                if h >= 2:
                    pool.wait_ge(s_add, LAYERS * HEADS + 2 * (2 * (h - 1)) + PRIME)
                pool.dma_start(rel[:, h % 2], relbias[h]).then_inc(rel_loaded[h % 2], 16)
                pool.wait_ge(rel_loaded[h % 2], 16 * (h // 2 + 1))
                if h == 0:
                    pool.wait_ge(c_loaded, C_LOADS)
                pool.tensor_tensor(rel[:, h % 2], rel[:, h % 2],
                                   cmask[:].unsqueeze(1).broadcast_to([P, 6, GW]), ALU.add).then_inc(rel_ready, 1)

        @block.scalar
        def _(act):
            for s in (*hi_ready, *silu_done, pt_done):
                act.sem_inc(s, PRIME)
            act.dma_start(sml[:], small).then_inc(g_loaded, 16)

            def split(slot, cols, count):
                act.wait_ge(raw_full[slot], count * 16)
                act.wait_ge(w_used[slot], count - 1)
                act.activation(whi[:, slot, 0:cols], raw[:, slot, 0:cols], ACT.Copy).then_inc(hi_ready[slot], 1)

            def split_ahead(name, nxt, l, i, j=0, last=True):
                ph, t = PHASES[name], i + LEAD
                if last and t >= ph.pieces:
                    n, t = PHASES[nxt], t - ph.pieces
                    split(n.slot(t), n.cols, uses(nxt, t, l + 1 if nxt == "gu1" else l))
                else:
                    split(ph.slot(t), ph.cols, uses(name, t, l, j))

            def square(p, src):
                act.activation(sq[:, p, 0:src.shape[-1]], src, ACT.Square).then_inc(sq_done[p], 1)

            def rstd(total, slot, width, n, count):
                act.activation(lnv[:, slot, 0:n], total, ACT.Ln, scale=1.0 / width, bias=EPS).then_inc(ln_done, 1)
                act.wait_ge(ln_done, count)
                act.activation(rs[:, slot, 0:n], lnv[:, slot, 0:n], ACT.Exp, scale=-0.5).then_inc(rstd_done, 1)

            def norm(q, n=T):
                act.wait_ge(sum_done, q + 1)
                rstd(bank[SUM][:, 0:n], 0, D, n, q + 1)
                for k in range(KT):
                    act.wait_ge(h32_done, q * KT + k + 1)
                    act.activation(hhi[:, k * TM:k * TM + n], h32[:, k % 4, 0:n], ACT.Copy).then_inc(h_hi, 1)

            def high(q, k, slot):
                act.wait_ge(h32_done, q * KT + k + 1)
                act.activation(hhi[:, bass.ds(k * TM, T)], h32[:, slot, 0:T], ACT.Copy).then_inc(h_hi, 1)

            def late_rstd(q):
                act.wait_ge(sum_done, q + 1)
                rstd(bank[SUM][:, 0:T], 0, D, T, q + 1)

            def gate_up(name, nxt, l, w):
                n11 = l * (2 * HALF) + w * HALF
                act.preload_act_table(ACT.Silu)

                def lap(j, last):
                    for r in range(SLOTS):
                        i = r if not last else GU - SLOTS + r
                        p = r // 2
                        split_ahead(name, nxt, l, i, j, last)
                        count = n11 + j + 1 + (HALF - 1 if last else 0)
                        if r % 2 == 0:
                            act.wait_ge(gate_scaled[p], count + PRIME)
                            act.activation(sg[:, p], sq[:, p, 0:T], ACT.Silu).then_inc(silu_done[p], 1)
                        else:
                            act.wait_ge(g_mul[p], count + PRIME)
                            f = j * 2 + p if not last else FT - 2 + p
                            act.activation(ghi[:, f, :], g32[:, p], ACT.Copy).then_inc(g_hi[p], 1)

                with act.Fori(0, GU // SLOTS - 1) as j:
                    lap(j, False)
                lap(0, True)

            def down(name, nxt, l, q):
                act.preload_act_table_set("natural_log_exp_and_others")

                act.wait_ge(sum_done, q)

                def lap(j, last):
                    for r in range(SLOTS):
                        i = r if not last else DN - SLOTS + r
                        split_ahead(name, nxt, l, i, j, last)
                        if r % 2:
                            p, o2 = r // 2, j if not last else KT // 2 - 1
                            act.wait_ge(acc_step, q * 7 + o2 * 2 + p - 1)
                            act.wait_ge(x_ready[p], q * 4 + o2 + (PRIME - 3))
                            square(p, x[:, o2 * 2 + p, 0:T])
                            high(q, o2 * 2 + p, p)

                with act.Fori(0, DN // SLOTS - 1) as j:
                    lap(j, False)
                lap(0, True)

            def qkv(l):
                for i in range(LEAD):
                    split_ahead("qkv", "conv", l, i)
                for i in range(QKV - LEAD, QKV):
                    split_ahead("qkv", "conv", l, i)

            def exp_first(l, h):
                act.wait_ge(nm_done, l * HEADS + h + 1)
                s = h % 2
                act.activation(Pr[:, s, 0:BLK], S[:, s, 0:BLK], ACT.Exp, bias=nm[:, 2 * h:2 * h + 1],
                               accum_out=sums[:, 2 * h:2 * h + 1])
                act.activation(Pr[:, s, BLK:3 * BLK], S[:, s, BLK:3 * BLK], ACT.Exp,
                               bias=nm[:, 2 * h + 1:2 * h + 2], accum_out=sums[:, 2 * h + 1:2 * h + 2])
                sink = sml[:, bass.ds(l * HEADS + (G_SINK + h), 1)]
                act.activation(es[:, 2 * h:2 * h + 2], nm[:, 2 * h:2 * h + 2], ACT.Exp, bias=sink)\
                   .then_inc(exp_done, 1)

            def pt_first(l, h):
                act.wait_ge(tr_done, l * HEADS + h + 1)
                act.activation(PT[:, h % 2], bank[TRANS[h % 2]][:, 0:3 * BLK], ACT.Copy).then_inc(pt_done, 1)

            def mix_high(l, jj):
                act.wait_ge(m_done, l * CT + jj + (1 + PRIME))
                act.activation(ghi[:, 4 + jj, :], m32[:, jj % 2], ACT.Copy).then_inc(mix_hi, 1)

            def conv(l):
                for i in range(CONV):
                    split_ahead("conv", "wout", l, i)
                    if i == 1:
                        act.wait_ge(vt_done, l + 1)
                        act.activation(v32[:].rearrange("p t c -> p (t c)"), bank[OUT[0]][:, 0:T], ACT.Copy)\
                           .then_inc(v_done, 1)
                    if 0 <= i - 2 < HEADS:
                        pt_first(l, i - 2)
                    if i < HEADS:
                        exp_first(l, i)
                    jj, kind = i // 3, i % 3
                    if i == CONV - 1:
                        for j in range(QT):
                            act.wait_ge(ot_done, l * QT + j + 1)
                            act.activation(ghi[:, j, :], bank[4 + j][:, 0:T], ACT.Copy).then_inc(mix_hi, 1)
                    if kind == 1 and jj > 0:
                        mix_high(l, jj - 1)
                mix_high(l, CT - 1)

            def wout(l, q):
                for o in range(KT):
                    if o < KT - 1:
                        split_ahead("wout", "gu2", l, o)
                    act.wait_ge(x_ready[o % 2], q * 4 + (o // 2 + PRIME - 3))
                    if o == 0:
                        act.wait_ge(sum_done, q)
                    else:
                        act.wait_ge(acc_step, q * 7 + o - 1)
                    square(o % 2, x[:, o, 0:T])
                    high(q, o, o % 2)
                    if o == KT - 1:
                        split_ahead("wout", "gu2", l, o)

            act.preload_act_table_set("natural_log_exp_and_others")
            for k in range(KT):
                act.wait_ge(x_loaded[k // (KT // 2)], 16)
                if k >= 2:
                    act.wait_ge(acc_step, k - 1)
                square(k % 2, x[:, k, 0:T])
                high(0, k, k % 4)
                if k in (3, 5, 7):
                    split((k - 3) // 2, PT8, uses0(1))
            with act.Fori(0, LAYERS) as l:
                late_rstd(l * 3)
                gate_up("gu1", "dn1", l, 0)
                down("dn1", "qkv", l, l * 3 + 1)
                late_rstd(l * 3 + 1)
                qkv(l)
                conv(l)
                wout(l, l * 3 + 2)
                late_rstd(l * 3 + 2)
                gate_up("gu2", "dn2", l, 1)
                down("dn2", "gu1", l, l * 3 + 3)
            act.wait_ge(sum_done, 7)
            rstd(bank[SUM][:, 0:T], 0, D, T, 7)
            act.wait_ge(c_loaded, C_LOADS)
            for k in range(KT):
                act.wait_ge(fx_done, k + 1)
                if k >= 2:
                    act.wait_ge(sq_used[1] if k % 2 else acc_step, k // 2 if k % 2 else 7 * 7 + k // 2)
                square(k % 2, x[:, k, :])
            norm(7, TM)

            def split2(piece):
                if piece < SECOND:
                    split(piece % SLOTS, PT8, uses2(piece))

            def gate_tanh(j, b):
                if 2 <= j < 8:
                    act.wait_ge(silu_all, j - 1)
                elif j >= 10:
                    act.wait_ge(fill_taken, j - 9)
                act.activation(sg[:, j % 2], b, ACT.Tanh, scale=0.5).then_inc(th_done, 1)

            def y_high(y):
                act.wait_ge(y_done, y + 1)
                act.activation(yhi[:, y * T:(y + 1) * T], y32(y), ACT.Copy).then_inc(y_hi, 1)

            def projections(outs, st):
                for n in range(len(outs) + 4):
                    pieces = st["pieces"].get(n, [])
                    for piece in pieces[0:1]:
                        split2(piece + LEAD)
                    if n in st["normed"]:
                        m = st["normed"][n]
                        wait_output(act, outs, n)
                        if m >= 2:
                            act.wait_ge(sq_used[m % 2], 3 * (m % 2) + m // 2)
                        square(m % 2, bank[n % 4][:, 0:TOKENS[outs[n][0]]])
                    g = st["done_at"].get(n - LAG - 1)
                    if g is not None and outs[st["groups"][g][0]][0] in latw:
                        for i in st["groups"][g]:
                            kind, k, _ = outs[i]
                            c = st["latent"][i]
                            act.wait_ge(pj_taken, st["n0"] + i + 1)
                            off, wid = latw[kind]
                            act.activation(yhi[:, off + k * wid:off + (k + 1) * wid], h32[:, c, 0:wid],
                                           ACT.Copy).then_inc(h_hi, 1)
                    i = n - LAG
                    g = st["done_at"].get(i)
                    if g is not None:
                        members = st["groups"][g]
                        kind = outs[members[0]][0]
                        m = st["normed"][members[-1]]
                        act.wait_ge(sq_used[m % 2], 3 * (m % 2) + m // 2 + 1)
                        if g - st["g0"] >= 2:
                            act.wait_ge(pj_taken, st["n0"] + st["groups"][g - 2][-1] + 1)
                        rstd(bank[6 + g % 2][:, 0:TOKENS[kind]], g % 2, NORM_WIDTH[kind], TOKENS[kind], 8 + g + 1)
                    if outs is NA and 0 <= n - 2 < 8:
                        y_high(n - 2)
                    for piece in pieces[1:]:
                        split2(piece + LEAD)

            def probs_T(v):
                act.wait_ge(tr_done, LAYERS * HEADS + v + 1)
                b = 2 + v % 2
                act.activation(PT[:, v % 2, 0:2 * BLK], bank[b][:, 0:2 * BLK], ACT.Copy)
                act.activation(PT[0:META, v % 2, 2 * BLK:3 * BLK], bank[b][0:META, 2 * BLK:3 * BLK],
                               ACT.Copy).then_inc(pt_done, 1)

            def attention(v0, units, scale, from_psum):
                for i in range(units + 2):
                    m = i // 2
                    if i >= 2:
                        probs_T(v0 + i - 2)
                    if i < units:
                        v = v0 + i
                        act.wait_ge(nm_done, LAYERS * HEADS + v + 1)
                        src = bank[v % 2][:, 0:TM] if from_psum else S[:, v % 2, 0:TM]
                        act.activation(Pr[:, v % 2, 0:TM], src, ACT.Exp, bias=nm[:, v % 32:v % 32 + 1], scale=scale,
                                       accum_out=sums[:, v % 32:v % 32 + 1]).then_inc(exp_done, 1)
                    if from_psum and i % 2 and m < 8:
                        gate_tanh(m, sgate[:, m])
                    if not from_psum and i % 2 == 0 and m < FILL:
                        split2(FILL0 + m + LEAD)
                    if not from_psum and i % 2 and m < 8:
                        act.wait_ge(w_used[(FILL0 + m) % SLOTS], uses2(FILL0 + m))
                        gate_tanh(8 + m, bank[6 + m % 2][:, 0:T])

            projections(MLA, ST_MLA)
            act.preload_act_table_set("exp_and_others")
            attention(0, 2 * MH, MLA_SCALE, True)
            act.preload_act_table_set("natural_log_exp_and_others")
            projections(NA, ST_NA)
            act.preload_act_table_set("exp_and_others")
            attention(2 * MH, 2 * NH, 1.0, False)
            for i in range(8):
                y_high(8 + i)
            for piece in range(FILL0 + FILL, SECOND):
                split2(piece + LEAD)

        @block.vector
        def _(dve):
            for s in (*lo_ready, *gate_scaled, *up_scaled, *g_mul, *x_ready, s_add, o_done, cc_done, u_done, m_done):
                dve.sem_inc(s, PRIME)
            def split(slot, cols, count):
                dve.wait_ge(hi_ready[slot], count)
                dve.tensor_tensor(wlo[:, slot, 0:cols], raw[:, slot, 0:cols],
                                  whi[:, slot, 0:cols].bitcast(F32), ALU.subtract).then_inc(lo_ready[slot], 1)

            def split_ahead(name, nxt, l, i, j=0, last=True):
                ph, t = PHASES[name], i + LEAD
                if last and t >= ph.pieces:
                    n, t = PHASES[nxt], t - ph.pieces
                    split(n.slot(t), n.cols, uses(nxt, t, l + 1 if nxt == "gu1" else l))
                else:
                    split(ph.slot(t), ph.cols, uses(name, t, l, j))

            def scaled(q, k, slot):
                dve.tensor_scalar(h32[:, slot, 0:T], x[:, k, 0:T], sml[:, bass.ds(q * KT + k, 1)], None, ALU.mult)\
                   .then_inc(h32_done, 1)

            def low(q, k, slot):
                dve.wait_ge(h_hi, q * KT + k + 1)
                h = bass.ds(k * TM, T)
                dve.tensor_tensor(hlo[:, h], h32[:, slot, 0:T], hhi[:, h].bitcast(F32), ALU.subtract)\
                   .then_inc(h_lo, 1)

            def norm(q, n=T):
                dve.wait_ge(rstd_done, q + 1)
                for k in range(KT + 1):
                    if k < KT:
                        dve.scalar_tensor_tensor(out=h32[:, k % 4, 0:n], in0=x[:, k, 0:n],
                                                 scalar=sml[:, bass.ds(q * KT + k, 1)], in1=rs[:, 0, 0:n],
                                                 op0=ALU.mult, op1=ALU.mult).then_inc(h32_done, 1)
                    if k > 0:
                        dve.wait_ge(h_hi, q * KT + k)
                        c = (k - 1) * TM
                        dve.tensor_tensor(hlo[:, c:c + n], h32[:, (k - 1) % 4, 0:n], hhi[:, c:c + n].bitcast(F32),
                                          ALU.subtract).then_inc(h_lo, 1)

            def gate_up(name, nxt, l, w, q):
                n11 = l * (2 * HALF) + w * HALF

                def lap(j, last):
                    for r in range(SLOTS):
                        i = r if not last else GU - SLOTS + r
                        p = r // 2
                        count = n11 + j + 1 + (HALF - 1 if last else 0)
                        dve.wait_ge(w_used[r], uses(name, i, l, j))
                        if r % 2 == 0:
                            if p == 0:
                                dve.wait_ge(rstd_done, q + 1)
                            dve.tensor_tensor(sq[:, p, 0:T], bank[2 * p][:, 0:T], rs[:, 0, 0:T], ALU.mult)\
                               .then_inc(gate_scaled[p], 1)
                            split_ahead(name, nxt, l, i, j, last)
                        else:
                            dve.tensor_tensor(g32[:, p], bank[2 * p + 1][:, 0:T], rs[:, 0, 0:T], ALU.mult)\
                               .then_inc(up_scaled[p], 1)
                            dve.wait_ge(silu_done[p], count + PRIME)
                            dve.wait_ge(up_scaled[p], count + PRIME)
                            dve.tensor_tensor(g32[:, p], g32[:, p], sg[:, p], ALU.mult).then_inc(g_mul[p], 1)
                            split_ahead(name, nxt, l, i, j, last)
                            dve.wait_ge(g_hi[p], count)
                            f = j * 2 + p if not last else FT - 2 + p
                            dve.tensor_tensor(glo[:, f, :], g32[:, p], ghi[:, f, :].bitcast(F32), ALU.subtract)\
                               .then_inc(g_lo[p], 1)

                with dve.Fori(0, GU // SLOTS - 1) as j:
                    lap(j, False)
                lap(0, True)

            def down(name, nxt, l, q):
                def lap(j, last):
                    for r in range(SLOTS):
                        i = r if not last else DN - SLOTS + r
                        split_ahead(name, nxt, l, i, j, last)
                        if r % 2:
                            p, o2 = r // 2, j if not last else KT // 2 - 1
                            dve.wait_ge(w_used[r], uses(name, i, l, j))
                            xo = x[:, o2 * 2 + p, 0:T]
                            dve.scalar_tensor_tensor(out=xo, in0=bank[4 + p][:, 0:T], scalar=0.5, in1=xo,
                                                     op0=ALU.mult, op1=ALU.add).then_inc(x_ready[p], 1)
                            dve.wait_ge(x_ready[p], q * 4 + o2 + (PRIME - 3))
                            scaled(q, o2 * 2 + p, p)
                            low(q, o2 * 2 + p, p)

                with dve.Fori(0, DN // SLOTS - 1) as j:
                    lap(j, False)
                lap(0, True)

            def qkv(l):
                rstd = rs[:, 0, 0:T]
                dst = [q32[:, j, :] for j in range(QT)] + [k32[:], m32[:, 0, :]]
                dve.wait_ge(rstd_done, l * 3 + 2)
                for i in range(QKV):
                    dve.wait_ge(w_used[PHASES["qkv"].slot(i)], uses("qkv", i, l))
                    dve.tensor_tensor(dst[i], bank[i % 4][:, 0:T], rstd, ALU.mult).then_inc(qkv_done, 1)
                    if i < LEAD:
                        split_ahead("qkv", "conv", l, i)
                    elif i == QKV - 2:
                        split_ahead("qkv", "conv", l, QKV - 3)
                    elif i == QKV - 1:
                        split_ahead("qkv", "conv", l, QKV - 2)
                        split_ahead("qkv", "conv", l, QKV - 1)
                dve.tensor_tensor(rs[:, 1, 0:T], rstd, rstd, ALU.mult).then_inc(rs2_done, 1)

            def add_max(l, h):
                n, s = l * HEADS + h, h % 2
                dve.wait_ge(sc_done, n + 1)
                dve.scalar_tensor_tensor(out=S[:, s], in0=bank[SCORE][:, 0:3 * BLK], scalar=HD ** -0.5,
                                         in1=bt[:, h, :], op0=ALU.mult, op1=ALU.add).then_inc(s_add, 1)
                dve.wait_ge(s_add, n + (1 + PRIME))
                dve.reduce_max(mx[:, 2 * h:2 * h + 1], S[:, s, 0:BLK], AX_X)
                dve.reduce_max(mx[:, 2 * h + 1:2 * h + 2], S[:, s, BLK:3 * BLK], AX_X).then_inc(mx_done, 1)
                dve.wait_ge(mx_done, n + 1)
                sink = sml[:, bass.ds(l * HEADS + (G_SINK + h), 1)]
                dve.tensor_scalar(nm[:, 2 * h:2 * h + 2], mx[:, 2 * h:2 * h + 2], sink, -1.0, ALU.max, ALU.mult)\
                   .then_inc(nm_done, 1)

            def denominators(n, a, b, add_sink):
                dve.wait_ge(exp_done, n + 1)
                src = sums
                if add_sink:
                    dve.tensor_tensor(den[:, a:b], sums[:, a:b], es[:, a:b], ALU.add).then_inc(den_done, 1)
                    dve.wait_ge(den_done, n + 1)
                    src = den
                dve.reciprocal(rec[:, a:b], src[:, a:b]).then_inc(rec_done, 1)

            def out_first(l, h):
                n = l * HEADS + h
                dve.wait_ge(pv_done, n + 1)
                dve.wait_ge(rec_done, n + 1)
                col = (h % QT) * P + h // QT * HD
                for b in range(2):
                    o = dve.tensor_scalar(O32[:, b, col:col + HD], bank[OUT[h % 2]][:, b * HD:(b + 1) * HD],
                                          rec[:, 2 * h + b:2 * h + b + 1], None, ALU.mult)
                o.then_inc(o_done, 1)

            def mix_low(l, n, src):
                k = MIX_ORDER[n]
                dve.wait_ge(mix_hi, l * 8 + n + 1)
                dve.tensor_tensor(glo[:, k, :], src, ghi[:, k, :].bitcast(F32), ALU.subtract).then_inc(mix_lo, 1)

            def gated(l, jj):
                i = 3 * jj + 2
                dve.wait_ge(w_used[PHASES["conv"].slot(i)], uses("conv", i, l))
                dve.wait_ge(y_step, (l * CT + jj) * 6 + (6 + PRIME))
                dve.tensor_tensor(m32[:, jj % 2], bank[0][:, 0:T], ya[:], ALU.mult).then_inc(m_done, 1)

            def conv(l):
                dve.wait_ge(b_loaded, 16)
                dve.wait_ge(const_set, 2)
                for i in range(CONV):
                    jj, kind = i // 3, i % 3
                    c = l * CT + jj
                    slot, count = PHASES["conv"].slot(i), uses("conv", i, l)
                    if i < HEADS:
                        add_max(l, i)
                    split_ahead("conv", "wout", l, i)
                    if 0 <= i - 1 < HEADS:
                        denominators(l * HEADS + i - 1, 2 * (i - 1), 2 * i, True)
                    if 0 <= i - 3 < HEADS:
                        out_first(l, i - 3)
                    if kind == 0 and jj > 0:
                        gated(l, jj - 1)
                    if i == CONV - 1:
                        for j in range(QT):
                            mix_low(l, CT - 1 + j, bank[4 + j][:, 0:T])
                    if kind == 0:
                        dve.wait_ge(w_used[slot], count)
                        dve.wait_ge(rs2_done, l + 1)
                        dve.wait_ge(u_done, c + PRIME)
                        dve.tensor_tensor(cc32[:], bank[2][:, 0:T], rs[:, 1, 0:T], ALU.mult).then_inc(cc_done, 1)
                    if kind == 1:
                        dve.wait_ge(w_used[slot], count)
                        dve.wait_ge(cc_done, c + (1 + PRIME))
                        dve.wait_ge(y_step, c * 6 + PRIME)
                        dve.tensor_tensor(u[:, 2:T + 2], bank[3][:, 0:T], cc32[:], ALU.mult).then_inc(u_done, 1)
                        if jj > 0:
                            mix_low(l, jj - 1, m32[:, (jj - 1) % 2])
                gated(l, CT - 1)
                mix_low(l, CT + QT - 1, m32[:, (CT - 1) % 2])

            def wout(l, q):
                for o in range(KT):
                    dve.wait_ge(w_used[PHASES["wout"].slot(o)], uses("wout", o, l))
                    xo = x[:, o, 0:T]
                    dve.tensor_tensor(xo, bank[2 + o % 2][:, 0:T], xo, ALU.add).then_inc(x_ready[o % 2], 1)
                    dve.wait_ge(x_ready[o % 2], q * 4 + (o // 2 + PRIME - 3))
                    scaled(q, o, o % 2)
                    if o < KT - 1:
                        split_ahead("wout", "gu2", l, o)
                    low(q, o, o % 2)
                    if o == KT - 1:
                        split_ahead("wout", "gu2", l, o)

            dve.wait_ge(g_loaded, 16)
            for k in range(KT + 1):
                if k < KT:
                    dve.wait_ge(x_loaded[k // (KT // 2)], 16)
                    scaled(0, k, k % 4)
                if k > 0:
                    low(0, k - 1, (k - 1) % 4)
                if k in (4, 6, 8):
                    split((k - 4) // 2, PT8, uses0(1))
            with dve.Fori(0, LAYERS) as l:
                gate_up("gu1", "dn1", l, 0, l * 3)
                down("dn1", "qkv", l, l * 3 + 1)
                qkv(l)
                conv(l)
                wout(l, l * 3 + 2)
                gate_up("gu2", "dn2", l, 1, l * 3 + 2)
                down("dn2", "gu1", l, l * 3 + 3)
            dve.wait_ge(rstd_done, 7)
            for k in range(KT):
                dve.scalar_tensor_tensor(out=x[:, k, 0:T], in0=x[:, k, 0:T], scalar=sml[:, 6 * KT + k:6 * KT + k + 1],
                                         in1=rs[:, 0, 0:T], op0=ALU.mult, op1=ALU.mult).then_inc(fx_done, 1)
            dve.wait_ge(fx_done, KT)
            dve.wait_ge(c_loaded, C_LOADS)
            norm(7, TM)

            def split2(piece):
                if piece < SECOND:
                    split(piece % SLOTS, PT8, uses2(piece))

            def normed_dst(kind, k, c):
                if kind in latw:
                    return h32[:, c, 0:TOKENS[kind]]
                if kind in ("kpe", "qpe"):
                    return S[:, c % 2, 0:TOKENS[kind]]
                return {"kn": kn, "nak": kn, "qn": qn, "naq": qn}[kind][:, k, :]

            def silu(count, j, gate, taken):
                dve.wait_ge(th_done, count + 1)
                dve.scalar_tensor_tensor(out=sgate[:, j], in0=sg[:, count % 2], scalar=1.0, in1=gate,
                                         op0=ALU.add, op1=ALU.mult).then_inc(taken, 1)

            def y_product(y, b):
                dve.wait_ge(ot_done, LAYERS * QT + y + 1)
                if 2 <= y < 10:
                    dve.wait_ge(y_lo, min(y - 1, 8))
                elif y >= 10:
                    dve.wait_ge(y_lo, max(y - 3, 8))
                dve.scalar_tensor_tensor(out=y32(y), in0=b[:, 0:T], scalar=0.5, in1=sgate[:, y % 8],
                                         op0=ALU.mult, op1=ALU.mult).then_inc(y_done, 1)

            def y_low(y):
                dve.wait_ge(y_hi, y + 1)
                dve.tensor_tensor(ylo[:, y * T:(y + 1) * T], y32(y),
                                  yhi[:, y * T:(y + 1) * T].bitcast(F32), ALU.subtract).then_inc(y_lo, 1)

            def projections(outs, st):
                for n in range(len(outs) + LAG + 3):
                    pieces = st["pieces"].get(n, [])
                    for piece in pieces[0:1]:
                        split2(piece + LEAD)
                    i = n - LAG - 2
                    if i in st["ropes"]:
                        c, nt = st["ropes"][i], TOKENS[outs[i][0]]
                        dst = kp[:] if outs[i][0] == "kpe" else qp[:, outs[i][1], :]
                        dve.wait_ge(rot_done, c + 1)
                        if c > 0:
                            dve.wait_ge(rope_done, c)
                        dve.tensor_tensor(Pr[:, 0, 0:nt], bank[SCORE][:, 0:nt], rop[:, 1, 0:nt], ALU.mult)
                        dve.tensor_tensor(Pr[:, 1, 0:nt], S[:, c % 2, 0:nt], rop[:, 0, 0:nt], ALU.mult)\
                           .then_inc(rt_done, 1)
                        dve.wait_ge(rt_done, c + 1)
                        dve.tensor_tensor(dst, Pr[:, 0, 0:nt], Pr[:, 1, 0:nt], ALU.add).then_inc(rope_done, 1)
                    g = st["done_at"].get(n - LAG - 1)
                    if g is not None and outs[st["groups"][g][0]][0] in latw:
                        for i in st["groups"][g]:
                            kind, k, _ = outs[i]
                            c = st["latent"][i]
                            off, wid = latw[kind]
                            dve.wait_ge(h_hi, 8 * KT + c + 1)
                            dve.tensor_tensor(ylo[:, off + k * wid:off + (k + 1) * wid], h32[:, c, 0:wid],
                                              yhi[:, off + k * wid:off + (k + 1) * wid].bitcast(F32), ALU.subtract)\
                               .then_inc(h_lo, 1)
                    g = st["done_at"].get(n - LAG)
                    if g is not None:
                        dve.wait_ge(rstd_done, 8 + g + 1)
                        for i in st["groups"][g]:
                            kind, k, _ = outs[i]
                            c = st["latent"].get(i, st["ropes"].get(i))
                            if i in st["ropes"] and c >= 2:
                                dve.wait_ge(rope_done, c - 1)
                            gain = G_HEAD + HEAD_GAIN[kind] + (k if kind in latw else 0)
                            nt = TOKENS[kind]
                            ins = dve.scalar_tensor_tensor(
                                out=normed_dst(kind, k, c), in0=bank[i % 4][:, 0:nt], scalar=sml[:, gain:gain + 1],
                                in1=rs[:, g % 2, 0:nt], op0=ALU.mult, op1=ALU.mult)
                            ins.then_inc(pj_taken, 1)
                    i = n - LAG
                    if 0 <= i < len(outs):
                        kind, k, _ = outs[i]
                        if kind in ("uv", "nav"):
                            c, tt = divmod(k, 3)
                            np_ = P if tt < 2 else META
                            wait_output(dve, outs, i)
                            dve.tensor_copy(V[0:np_, tt, c * 512:(c + 1) * 512], bank[out_bank(outs, i)][0:np_, :])\
                               .then_inc(pj_taken, 1)
                        if kind == "gate":
                            wait_output(dve, outs, i)
                            dve.tensor_copy(sgate[:, k], bank[i % 4][:, 0:T]).then_inc(pj_taken, 1)
                    if outs is NA and 0 <= n - 3 < 8:
                        y_low(n - 3)
                    if outs is NA and 0 <= n - 1 < 8:
                        y_product(n - 1, bank[4 + (n - 1) % 2])
                    for piece in pieces[1:]:
                        split2(piece + LEAD)

            def out_second(v, width, dst):
                dve.wait_ge(pv_done, LAYERS * HEADS + v + 1)
                dve.wait_ge(rec_done, LAYERS * HEADS + v + 1)
                dve.tensor_scalar(dst, bank[4 + v % 2][:, 0:width], rec[:, v % 32:v % 32 + 1], None, ALU.mult)\
                   .then_inc(o_done, 1)

            def attention(v0, units, width, mla):
                for i in range(units + 3):
                    m = i // 2
                    if i < units:
                        v = v0 + i
                        h, t = i // 2, i % 2
                        c = v % 32
                        dve.wait_ge(sc_done, LAYERS * HEADS + v + 1)
                        if mla:
                            dve.reduce_max(mx[:, c:c + 1], bank[v % 2][:, 0:TM], AX_X).then_inc(mx_done, 1)
                        else:
                            if t == 0:
                                dve.wait_ge(rel_ready, h + 1)
                            if i >= 2:
                                dve.wait_ge(exp_done, LAYERS * HEADS + v - 1)
                            dve.scalar_tensor_tensor(
                                out=S[:, v % 2, 0:T], in0=bank[v % 2][:, 0:T], scalar=HD ** -0.5,
                                in1=rel[:, h % 2, 2 - 2 * t:6 - 2 * t, :].rearrange("p r c -> p (r c)"),
                                op0=ALU.mult, op1=ALU.add).then_inc(s_add, 1)
                            dve.scalar_tensor_tensor(
                                out=S[:, v % 2, T:TM], in0=bank[v % 2][:, T:TM], scalar=HD ** -0.5,
                                in1=metab[:, h, :], op0=ALU.mult, op1=ALU.add).then_inc(s_add, 1)
                            dve.wait_ge(s_add, LAYERS * HEADS + 2 * (i + 1) + PRIME)
                            dve.reduce_max(mx[:, c:c + 1], S[:, v % 2, 0:TM], AX_X).then_inc(mx_done, 1)
                        dve.wait_ge(mx_done, LAYERS * HEADS + v + 1)
                        dve.tensor_scalar(nm[:, c:c + 1], mx[:, c:c + 1], -(MLA_SCALE if mla else 1.0), None,
                                          ALU.mult).then_inc(nm_done, 1)
                    if i >= 1 and i <= units:
                        v = v0 + i - 1
                        denominators(LAYERS * HEADS + v, v % 32, v % 32 + 1, False)
                    if i >= 3:
                        h, t = (i - 3) // 2, (i - 3) % 2
                        out_second(v0 + i - 3, width, O32[:, t, h * width:(h + 1) * width])
                    if mla and i % 2 and m < 8:
                        silu(m, m, sgate[:, m], silu_all)
                    if not mla and i % 2 and m < FILL:
                        split2(FILL0 + m + LEAD)
                    m = i // 2 - 1
                    if not mla and i % 2 == 0 and 0 <= m < FILL:
                        if m < 8:
                            silu(8 + m, m, bank[6 + m % 2][:, 0:T], fill_taken)
                        else:
                            piece, o = FILL0 + m, m - 8
                            dve.wait_ge(w_used[piece % SLOTS], uses2(piece))
                            dve.tensor_tensor(x[:, o, 0:T], bank[6 + m % 2][:, 0:T], x[:, o, 0:T], ALU.add)\
                               .then_inc(fill_taken, 1)

            projections(MLA, ST_MLA)
            attention(0, 2 * MH, P, True)
            projections(NA, ST_NA)
            attention(2 * MH, 2 * NH, HD, False)
            for i in range(10):
                if i < 8:
                    y_product(8 + i, bank[2 + i % 4])
                if i >= 2:
                    y_low(8 + i - 2)
            for o in range(8):
                piece = FILL0 + FILL + o
                split2(piece + LEAD)
                dve.wait_ge(w_used[piece % SLOTS], uses2(piece))
                dve.wait_ge(fill_taken, FILL)
                dve.tensor_tensor(x[:, o, 0:T], bank[(0, 1, 6, 7)[o % 4]][:, 0:T], x[:, o, 0:T], ALU.add)\
                   .then_inc(res_done, 1)

        @block.tensor
        def _(pe):
            for s in w_used:
                pe.sem_inc(s, PRIME)

            def product(o, slot, t, xh, xl, first, last, n=P):
                h, lo = whi[:, slot, t * P:(t + 1) * P], wlo[:, slot, t * P:(t + 1) * P]
                pe.matmul(o, h, xh, start=first, stop=False)
                pe.matmul(o, h, xl, start=False, stop=False)
                return pe.matmul(o, lo, xh, start=False, stop=last)

            def hcols(k, n=T):
                return hhi[:, k * TM:k * TM + n], hlo[:, k * TM:k * TM + n]

            def tile8(o, slot, n=T):
                for k in range(KT):
                    mm = product(o, slot, k, *hcols(k, n), k == 0, k == KT - 1)
                mm.then_inc(w_used[slot], 1)

            def first_pair(ready, q):
                ready(0)
                for k in range(KT - 1):
                    pe.wait_ge(h_lo, q * KT + k + 1)
                    product(bank[0][:, 0:T], 0, k, *hcols(k), k == 0, False)
                ready(1)
                sum_norm(q)
                for k in range(KT - 1):
                    product(bank[1][:, 0:T], 1, k, *hcols(k), k == 0, False)
                pe.wait_ge(h_lo, q * KT + KT)
                for o in range(2):
                    mm = product(bank[o][:, 0:T], o, KT - 1, *hcols(KT - 1), False, True)
                    mm.then_inc(w_used[o], 1)

            def sum_norm(q, n=T, first=True, steps=KT - 1):
                pe.wait_ge(acc_step, q * 7 + steps)
                pe.matmul(bank[SUM][:, 0:n], ones[:], acc[:, 0:n], start=first, stop=False)
                pe.wait_ge(sq_done[1], q * 4 + 4)
                pe.matmul(bank[SUM][:, 0:n], ones[:], sq[:, 1, 0:n], start=False, stop=True).then_inc(sum_done, 1)

            def sum_squares(p, count, first, last, n, total, lhs):
                pe.wait_ge(sq_done[p], count)
                pe.matmul(bank[total][:, 0:n], lhs, sq[:, p, 0:n], start=first, stop=last)\
                  .then_inc(sq_used[p], 1)

            def gate_up(name, l, w, q):
                n11 = l * (2 * HALF) + w * HALF

                def ready(r, j):
                    pe.wait_ge(lo_ready[r], uses(name, r, l, j))
                    pe.wait_ge((up_scaled if r % 2 else gate_scaled)[r // 2], n11 + (j + PRIME))

                first_pair(lambda r: ready(r, 0), q)
                for r in (2, 3):
                    ready(r, 0)
                    tile8(bank[r][:, 0:T], r)
                with pe.Fori(1, GU // SLOTS) as j:
                    for r in range(SLOTS):
                        ready(r, j)
                        tile8(bank[r][:, 0:T], r)

            def down(name, l, w, q):
                n11 = l * (2 * HALF) + w * HALF

                def lap(j):
                    for r in range(SLOTS):
                        p, half = r // 2, r % 2
                        pe.wait_ge(lo_ready[r], uses(name, r, l, j))
                        if half == 0:
                            pe.wait_ge(x_ready[p], (q * 4 - 4) + (j + PRIME))
                        pe.wait_ge(g_lo[0], n11 + (HALF + 1) // 2 if half == 0 else n11 + HALF)
                        pe.wait_ge(g_lo[1], n11 + HALF // 2 if half == 0 else n11 + HALF)
                        for k in range(HALF):
                            f = half * HALF + k
                            mm = product(bank[4 + p][:, 0:T], r, k, ghi[:, f, :], glo[:, f, :], f == 0, f == FT - 1)
                        mm.then_inc(w_used[r], 1)

                with pe.Fori(0, DN // SLOTS) as j:
                    lap(j)

            def qkv(l, q):
                first_pair(lambda i: pe.wait_ge(lo_ready[PHASES["qkv"].slot(i)], uses("qkv", i, l)), q)
                for i in range(2, QKV):
                    slot = PHASES["qkv"].slot(i)
                    pe.wait_ge(lo_ready[slot], uses("qkv", i, l))
                    if i >= 4:
                        pe.wait_ge(qkv_done, l * QKV + i - 3)
                    tile8(bank[i % 4][:, 0:T], slot)

            def scores_first(l, h):
                n, j, r = l * HEADS + h, h % QT, h // QT * HD
                pe.wait_ge(qkv_done, l * QKV + QKV - 1)
                pe.wait_ge(s_add, n + PRIME)
                pe.matmul(bank[SCORE][:, 0:BLK], q32[r:r + HD, j, 0:BLK], k32[r:r + HD, 0:BLK], start=True, stop=True)
                pe.matmul(bank[SCORE][:, BLK:3 * BLK], q32[r:r + HD, j, BLK:T], k32[r:r + HD, :], start=True,
                          stop=True).then_inc(sc_done, 1)

            def transpose_first(l, h):
                n = l * HEADS + h
                pe.wait_ge(exp_done, n + 1)
                if h >= 2:
                    pe.wait_ge(pt_done, n - 1 + PRIME)
                for b in range(3):
                    tr = pe.transpose(bank[TRANS[h % 2]][:, b * BLK:(b + 1) * BLK], Pr[:, h % 2, b * BLK:(b + 1) * BLK], ident)
                tr.then_inc(tr_done, 1)

            def pv_first(l, h):
                n, c = l * HEADS + h, h // QT * HD
                pe.wait_ge(v_done, l + 1)
                pe.wait_ge(pt_done, n + (1 + PRIME))
                if h >= 2:
                    pe.wait_ge(o_done, n - 1 + PRIME)
                pt, o = PT[:, h % 2], bank[OUT[h % 2]]
                pe.matmul(o[:, 0:HD], pt[:, 0:BLK], v32[:, 0, c:c + HD], start=True, stop=True)
                pe.matmul(o[:, HD:2 * HD], pt[:, BLK:2 * BLK], v32[:, 0, c:c + HD], start=True, stop=False)
                pe.matmul(o[:, HD:2 * HD], pt[:, 2 * BLK:3 * BLK], v32[:, 1, c:c + HD], start=False,
                          stop=True).then_inc(pv_done, 1)

            def conv(l):
                pe.wait_ge(c_loaded, C_LOADS)
                for i in range(CONV):
                    jj, kind = i // 3, i % 3
                    slot = PHASES["conv"].slot(i)
                    if i < HEADS:
                        scores_first(l, i)
                    if i == 1:
                        pe.wait_ge(qkv_done, l * QKV + QKV)
                        for t in range(2):
                            tr = pe.transpose(bank[OUT[0]][:, t * P:(t + 1) * P], m32[:, 0, t * P:(t + 1) * P], ident)
                        tr.then_inc(vt_done, 1)
                    if i == CONV - 1:
                        pe.wait_ge(o_done, (l + 1) * HEADS + PRIME)
                        for j in range(QT):
                            for t in range(2):
                                tr = pe.transpose(bank[4 + j][:, t * P:(t + 1) * P],
                                                  O32[:, t, j * P:(j + 1) * P], ident)
                            tr.then_inc(ot_done, 1)
                    pe.wait_ge(lo_ready[slot], uses("conv", i, l))
                    if i == 0:
                        pe.wait_ge(qkv_done, l * QKV + QKV - 1)
                    pe.wait_ge([cc_done, u_done, m_done][kind], l * CT + (jj + PRIME))
                    tile8(bank[(2, 3, 0)[kind]][:, 0:T], slot)
                    if 0 <= i - 1 < HEADS:
                        transpose_first(l, i - 1)
                    if 0 <= i - 2 < HEADS:
                        pv_first(l, i - 2)

            def wout(l, q):
                for i in range(2):
                    slot = PHASES["wout"].slot(i)
                    pe.wait_ge(lo_ready[slot], uses("wout", i, l))
                pe.wait_ge(u_done, (l + 1) * CT + PRIME)
                s0, s1 = PHASES["wout"].slot(0), PHASES["wout"].slot(1)
                for n, k in enumerate(MIX_ORDER):
                    pe.wait_ge(mix_lo, l * 8 + n + 1)
                    a = product(bank[2][:, 0:T], s0, k, ghi[:, k, :], glo[:, k, :], n == 0, n == KT - 1)
                    b = product(bank[3][:, 0:T], s1, k, ghi[:, k, :], glo[:, k, :], n == 0, n == KT - 1)
                a.then_inc(w_used[s0], 1)
                b.then_inc(w_used[s1], 1)
                for o in range(2, KT):
                    slot = PHASES["wout"].slot(o)
                    pe.wait_ge(lo_ready[slot], uses("wout", o, l))
                    pe.wait_ge(x_ready[o % 2], q * 4 + (o // 2 + PRIME - 4))
                    for k in range(KT):
                        mm = product(bank[2 + o % 2][:, 0:T], slot, k, ghi[:, k, :], glo[:, k, :], k == 0, k == KT - 1)
                    mm.then_inc(w_used[slot], 1)

            pe.wait_ge(const_set, 2)
            pe.wait_ge(pad_set, 2)
            with pe.Fori(0, LAYERS) as l:
                gate_up("gu1", l, 0, l * 3)
                down("dn1", l, 0, l * 3 + 1)
                qkv(l, l * 3 + 1)
                conv(l)
                wout(l, l * 3 + 2)
                gate_up("gu2", l, 1, l * 3 + 2)
                down("dn2", l, 1, l * 3 + 3)
            sum_norm(6)
            pe.wait_ge(rstd_done, 7)
            for k in range(1, KT - 2, 2):
                sum_squares(1, 7 * 4 + k // 2 + 1, k == 1, False, TM, SUM, ones[:])
            sum_norm(7, TM, False, 4)

            def begin(piece):
                pe.wait_ge(lo_ready[piece % SLOTS], uses2(piece))

            def run(outs, n):
                kind, k, piece = outs[n]
                slot, last = piece % SLOTS, ends_piece(outs, n)
                o = bank[n % 4]
                if kind == "kv":
                    if k == 0:
                        begin(0)
                        begin(1)
                        for i in range(KT):
                            pe.wait_ge(h_lo, 7 * KT + i + 1)
                            for a in range(2):
                                mm = product(bank[a][:, 0:TM], a, i, *hcols(i, TM), i == 0, i == KT - 1)
                                if i == KT - 1:
                                    mm.then_inc(w_used[a], 1)
                    return
                if kind in ("kpe", "ql", "naq", "nak", "gate"):
                    begin(piece)
                    for i in range(KT):
                        mm = product(o[:, 0:TOKENS[kind]], slot, i, *hcols(i, TOKENS[kind]), i == 0, i == KT - 1)
                elif kind in ("kn", "qn", "qpe"):
                    src, wid = latw["kv" if kind == "kn" else "ql"]
                    if k % 4 == 0:
                        begin(piece)
                    if k == 0:
                        pe.wait_ge(h_lo, 8 * KT + (2 if kind == "kn" else 4))
                    for i in range(2):
                        c = src + i * wid
                        mm = product(o[:, 0:TOKENS[kind]], slot, 2 * (k % 4) + i, yhi[:, c:c + wid],
                                     ylo[:, c:c + wid], i == 0, i == 1)
                elif kind == "uv":
                    tt = k % 3
                    if tt == 0:
                        begin(piece)
                    if k == 0:
                        pe.wait_ge(h_lo, 8 * KT + 2)
                        pe.wait_ge(pad_set, 4)
                    for i in range(2):
                        c = latw["kv"][0] + i * TM + tt * P
                        wh, wl = whi[:, slot, i * 512:(i + 1) * 512], wlo[:, slot, i * 512:(i + 1) * 512]
                        pe.matmul(o[:], yhi[:, c:c + P], wh, start=i == 0, stop=False)
                        pe.matmul(o[:], ylo[:, c:c + P], wh, start=False, stop=False)
                        mm = pe.matmul(o[:], yhi[:, c:c + P], wl, start=False, stop=i == 1)
                else:
                    tt = k % 3

                    def values(kp_, tile):
                        s = (piece - 3 + kp_) % SLOTS
                        for i in range(2):
                            c = (2 * kp_ + i) * TM + tile * P
                            b = bank[out_bank(outs, n - tt + tile)]
                            wh, wl = whi[:, s, i * 512:(i + 1) * 512], wlo[:, s, i * 512:(i + 1) * 512]
                            pe.matmul(b[:], hhi[:, c:c + P], wh, start=kp_ + i == 0, stop=False)
                            pe.matmul(b[:], hlo[:, c:c + P], wh, start=False, stop=False)
                            mm = pe.matmul(b[:], hhi[:, c:c + P], wl, start=False, stop=kp_ == 3 and i == 1)
                        return mm

                    if tt == 0:
                        for kp_ in range(3):
                            begin(piece - 3 + kp_)
                            for tile in range(3):
                                mm = values(kp_, tile)
                            mm.then_inc(w_used[(piece - 3 + kp_) % SLOTS], 1)
                        begin(piece)
                    mm = values(3, tt)
                mm.then_inc(w_used[slot] if last else pj_done, 1)

            def sums_of(outs, st, n):
                g = st["done_at"].get(n)
                if g is not None:
                    kind = outs[st["groups"][g][0]][0]
                    lhs = ones64 if NORM_WIDTH[kind] == 64 else ones[:]
                    if g - st["g0"] >= 2:
                        pe.wait_ge(rstd_done, 8 + g - 1)
                    for a, i in enumerate(st["groups"][g]):
                        m = st["normed"][i]
                        sum_squares(m % 2, 32 + m // 2 + 1, a == 0, i == st["groups"][g][-1], TOKENS[kind],
                                    6 + g % 2, lhs)

            def projections(outs, st):
                for n in range(len(outs) + LAG + 2):
                    nav = n < len(outs) and outs[n][0] == "nav"
                    if n < len(outs):
                        if nav and outs[n][1] == 0:
                            pe.wait_ge(y_done, 8)
                        if n >= 4:
                            pe.wait_ge(pj_taken, st["n0"] + n - 3)
                        run(outs, n)
                    sums_of(outs, st, n - LAG)
                    i = n - LAG - 1
                    if i in st["ropes"]:
                        c, nt = st["ropes"][i], TOKENS[outs[i][0]]
                        pe.wait_ge(pj_taken, st["n0"] + i + 1)
                        if c >= 1:
                            pe.wait_ge(rt_done, c)
                        pe.matmul(bank[SCORE][:, 0:nt], rot, S[:, c % 2, 0:nt], start=True, stop=True)\
                          .then_inc(rot_done, 1)
                    if outs is NA and n < 8:
                        if n == 0:
                            pe.wait_ge(o_done, LAYERS * HEADS + 2 * MH + PRIME)
                        if n >= 2:
                            pe.wait_ge(y_done, n - 1)
                        feature_major(bank[4 + n % 2], n)

            def feature_major(b, j):
                for t in range(2):
                    tr = pe.transpose(b[:, t * P:(t + 1) * P], O32[:, t, j * P:(j + 1) * P], ident)
                tr.then_inc(ot_done, 1)

            def transposes(v):
                pe.wait_ge(exp_done, LAYERS * HEADS + v + 1)
                pe.wait_ge(pt_done, LAYERS * HEADS + v - 1 + PRIME)
                o, pr = bank[2 + v % 2], Pr[:, v % 2]
                pe.transpose(o[:, 0:BLK], pr[:, 0:BLK], ident)
                pe.transpose(o[:, BLK:2 * BLK], pr[:, BLK:2 * BLK], ident)
                pe.transpose(o[0:META, 2 * BLK:3 * BLK], pr[:, 2 * BLK:TM], ident).then_inc(tr_done, 1)

            def values_of(v, h, width):
                pe.wait_ge(pt_done, LAYERS * HEADS + v + (1 + PRIME))
                pe.wait_ge(o_done, LAYERS * HEADS + v - 1 + PRIME)
                o, pt = bank[4 + v % 2][:, 0:width], PT[:, v % 2]
                c = slice(h * width, (h + 1) * width)
                pe.matmul(o, pt[:, 0:BLK], V[:, 0, c], start=True, stop=False)
                pe.matmul(o, pt[:, BLK:2 * BLK], V[:, 1, c], start=False, stop=False)
                pe.matmul(o, pt[0:META, 2 * BLK:3 * BLK], V[0:META, 2, c], start=False, stop=True)\
                  .then_inc(pv_done, 1)

            def fill(m, half):
                piece = FILL0 + m
                if half == 0:
                    begin(piece)
                    if m >= 2:
                        pe.wait_ge(fill_taken, m - 1)
                    if m == 8:
                        pe.wait_ge(y_lo, 8)
                for k in range(4 * half, 4 * half + 4):
                    xh, xl = hcols(k) if m < 8 else (yhi[:, k * T:(k + 1) * T], ylo[:, k * T:(k + 1) * T])
                    mm = product(bank[6 + m % 2][:, 0:T], piece % SLOTS, k, xh, xl, k == 0, k == KT - 1)
                if half:
                    mm.then_inc(w_used[piece % SLOTS], 1)

            def attention(v0, units, width, mla):
                for i in range(units + 3):
                    if i < units:
                        v, h, t = v0 + i, i // 2, i % 2
                        if i >= 2:
                            if mla:
                                pe.wait_ge(exp_done, LAYERS * HEADS + v - 1)
                            else:
                                pe.wait_ge(s_add, LAYERS * HEADS + 2 * (i - 1) + PRIME)
                        o, tok = bank[v % 2][:, 0:TM], slice(t * P, (t + 1) * P)
                        if mla:
                            r = h % 2 * MR
                            pe.matmul(o, qn[:, h, tok], kn[:, h, :], start=True, stop=False)
                            pe.matmul(o, qp[r:r + MR, h // 2, tok], kp[r:r + MR, :], start=False, stop=True)\
                              .then_inc(sc_done, 1)
                        else:
                            r = h % 2 * HD
                            pe.matmul(o, qn[r:r + HD, h // 2, tok], kn[r:r + HD, h // 2, :], start=True, stop=True)\
                              .then_inc(sc_done, 1)
                    if not mla and i // 2 < FILL:
                        fill(i // 2, i % 2)
                    if 3 <= i:
                        values_of(v0 + i - 3, (i - 3) // 2, width)
                    if 1 <= i <= units:
                        transposes(v0 + i - 1)

            def y_tiles(o, slot, y0):
                for k in range(KT):
                    y = slice((y0 + k) * T, (y0 + k + 1) * T)
                    mm = product(o, slot, k, yhi[:, y], ylo[:, y], k == 0, k == KT - 1)
                mm.then_inc(w_used[slot], 1)

            projections(MLA, ST_MLA)
            pe.wait_ge(rope_done, 1 + MH // 2)
            pe.wait_ge(pj_taken, len(MLA))
            attention(0, 2 * MH, P, True)
            projections(NA, ST_NA)
            pe.wait_ge(pj_taken, len(MLA) + len(NA))
            pe.wait_ge(y_done, 8)
            attention(2 * MH, 2 * NH, HD, False)
            pe.wait_ge(o_done, LAYERS * HEADS + 2 * MH + 2 * NH + PRIME)
            for j in range(4):
                feature_major(bank[2 + j], j)
            for piece in (FILL0 + FILL, FILL0 + FILL + 1):
                begin(piece)
            pe.wait_ge(fill_taken, FILL)
            for k in range(KT):
                if k < 4:
                    pe.wait_ge(y_done, 8 + k + 1)
                    feature_major(bank[2 + k], 4 + k)
                pe.wait_ge(y_lo, 8 + k + 1)
                for o in range(2):
                    slot, y = (FILL0 + FILL + o) % SLOTS, slice((8 + k) * T, (9 + k) * T)
                    mm = product(bank[o][:, 0:T], slot, k, yhi[:, y], ylo[:, y], k == 0, k == KT - 1)
                    if k == KT - 1:
                        mm.then_inc(w_used[slot], 1)
            for o in range(2, 8):
                piece = FILL0 + FILL + o
                begin(piece)
                if o >= 4:
                    pe.wait_ge(res_done, o - 3)
                y_tiles(bank[(0, 1, 6, 7)[o % 4]][:, 0:T], piece % SLOTS, 8)


def out_bank(outs, n):
    return (4, 5, 0, 1, 2, 3)[outs[n][1]] if outs[n][0] == "nav" else n % 4


def ends_piece(outs, n):
    return n + 1 == len(outs) or outs[n + 1][2] != outs[n][2]


def mid_outputs(outs, n):
    before = 0 if outs is MLA else sum(not ends_piece(MLA, i) for i in range(len(MLA)))
    return before + sum(not ends_piece(outs, i) for i in range(n + 1))


def structure(outs, n0, g0, m0, base):
    st = {"n0": n0, "g0": g0, "groups": {}, "done_at": {}, "normed": {}, "latent": {}, "ropes": {}, "pieces": {}}
    g, seen = g0, base
    for n, (kind, k, piece) in enumerate(outs):
        st["pieces"][n] = list(range(seen, piece + 1))
        seen = piece + 1
        if kind in NORM_WIDTH:
            st["normed"][n] = m0 + len(st["normed"])
            if kind in ("kv", "ql"):
                st["latent"][n] = len(st["latent"])
            if kind in ("kpe", "qpe"):
                st["ropes"][n] = len(st["ropes"])
            st["groups"].setdefault(g, []).append(n)
            if kind not in ("kv", "ql") or k == 1:
                st["done_at"][n] = g
                g += 1
    return st


MLA, NA = mla_outputs(), na_outputs()
ST_MLA = structure(MLA, 0, 0, 0, 0)
ST_NA = structure(NA, len(MLA), len(ST_MLA["groups"]), len(ST_MLA["normed"]), MLA_PIECES)
MLA_SCALE = float(np.float32((MN + MR) ** -0.5))


def tiles(w):
    k, n = w.shape
    return w.reshape(k // P, P, n // P, P).transpose(0, 2, 1, 3)


def by_output(w):
    t = tiles(w)
    kt, nt = t.shape[:2]
    t = t.transpose(1, 0, 2, 3).reshape(nt * (kt // 8), 8, P, P)
    return t.transpose(0, 2, 1, 3).reshape(-1, P, PT8)


def short_k(w):
    t = tiles(w).transpose(1, 0, 2, 3)
    return t.reshape(-1, 8, P, P).transpose(0, 2, 1, 3).reshape(-1, P, PT8)


def by_columns(w):
    k, n = w.shape
    t = w.reshape(k // (2 * P), 2, P, n // 512, 512).transpose(3, 0, 2, 1, 4)
    return t.reshape(-1, P, PT8)


def kernel(**inputs):
    import concourse.bacc as bacc
    from concourse.bass_utils import run_bass_kernel_spmd

    a = {k: np.asarray(v) for k, v in inputs.items()}
    heads = np.arange(HEADS).reshape(2, QT).T.reshape(-1)
    hcol = (heads[:, None] * HD + np.arange(HD)[None]).reshape(-1)
    pieces, downs = [], []
    for l in range(LAYERS):
        def ffn(name):
            g, up = by_output(a[name + "_wg"][l]), by_output(a[name + "_wu"][l])
            pieces.append(np.stack([g, up], 1).reshape(-1, P, PT8))
            d = tiles(a[name + "_wd"][l]).transpose(1, 0, 2, 3).reshape(DN, HALF, P, P)
            downs.append(d.transpose(0, 2, 1, 3).reshape(DN, P, PTD))

        ffn("ffn1")
        w = a["w_in"][l]
        attn = HEADS * HD
        qkv = np.concatenate([w[:, 0:attn][:, hcol], w[:, attn:attn + 2 * P]], 1)
        cb, cc, ch = (w[:, attn + 2 * P + i * 512:attn + 2 * P + (i + 1) * 512] for i in range(3))
        pieces.append(by_output(qkv))
        pieces.append(np.stack([by_output(cc), by_output(ch), by_output(cb)], 1).reshape(-1, P, PT8))
        wo = a["w_out"][l]
        pieces.append(by_output(np.concatenate([wo[0:attn][hcol], wo[attn:]], 0)))
        ffn("ffn2")
    w = a["w_in_2"][0]
    cut = np.cumsum([0, 256, 256, MR, D, D, D, D, D])
    qlat, kvlat, kpe, gmla, naq, nak, nav, gna = (w[:, cut[i]:cut[i + 1]] for i in range(8))
    ukv = a["w_ukv_2"][0].reshape(256, MH, 2, P)
    uq = a["w_uq_2"][0].reshape(256, MH, MN + MR)
    kinds = {"kv": by_output(kvlat), "kpe": by_output(np.concatenate([kpe, kpe], 1)), "ql": by_output(qlat),
             "kn": short_k(ukv[:, :, 0].reshape(256, -1)), "uv": by_columns(ukv[:, :, 1].reshape(256, -1)),
             "qn": short_k(uq[:, :, 0:MN].reshape(256, -1)), "qpe": short_k(uq[:, :, MN:].reshape(256, -1)),
             "gate": by_output(gmla)}
    taken = dict.fromkeys(kinds, 0)
    for n, (kind, _, _) in enumerate(MLA):
        if ends_piece(MLA, n):
            pieces.append(kinds[kind][taken[kind]:taken[kind] + 1])
            taken[kind] += 1
    wo2 = by_output(a["w_out_2"][0])
    pieces += [by_output(naq), by_output(nak), by_columns(nav), by_output(gna), wo2[0::2], wo2[1::2]]
    w8, wd = np.concatenate(pieces, 0), np.concatenate(downs, 0)

    def cols(v):
        return v.reshape(-1, P).T

    def twice(v):
        return np.concatenate([v, v])[:, None]

    norms = [a[n][l] for l in range(LAYERS) for n in ("ffn1_norm", "mix_norm", "ffn2_norm")]
    norms += [a["final_norm"], a["norm_w_2"][0]]
    conv = a["conv_w"].reshape(LAYERS, 3, CT, P).transpose(3, 0, 2, 1).reshape(P, -1)
    small = np.concatenate(
        [cols(np.concatenate(norms)), conv, np.broadcast_to(a["attn_sink"].reshape(1, -1), (P, LAYERS * HEADS)),
         cols(a["kv_lat_norm_w_2"][0]), cols(a["q_lat_norm_w_2"][0]), cols(a["mla_kn_w_2"][0]), cols(a["mla_qn_w_2"][0]),
         twice(a["mla_kpe_w_2"][0]), twice(a["mla_qpe_w_2"][0]), twice(a["na_q_norm_w_2"][0]),
         twice(a["na_k_norm_w_2"][0])], 1)

    f = np.float32
    i = np.arange(P)
    same = (i[:, None] // 64 == i[None] // 64)
    swap = same & (i[:, None] % 64 == (i[None] + 32) % 64)
    mats = np.stack([np.eye(P), same, np.where(swap, np.where(i[None] % 64 < 32, -1, 1), 0)], 1).astype(f)
    qi, kj = np.arange(BLK)[:, None], np.arange(2 * BLK)[None]
    dist = qi + BLK - kj
    slopes = np.exp2(-8.0 * np.arange(1, HEADS + 1, dtype=f) / HEADS).astype(f)
    band = np.where((dist >= 0) & (dist < BLK), -slopes[:, None, None] * dist.astype(f), f(MASKED)).astype(f)
    btab = np.concatenate([band[:, :, BLK:], band], 2).transpose(1, 0, 2)
    pos = np.concatenate([np.arange(META, TM), np.arange(META)]).astype(f)
    freq = (f(10000.0) ** -(np.arange(0, MR, 2, dtype=f) / f(MR))).astype(f)
    ang = (pos[None] * freq[i % 32][:, None]).astype(f)
    rope = np.stack([np.cos(ang), np.sin(ang)], 1).astype(f)
    c = np.arange(GW)
    c0 = np.clip(c - WC // 2, 0, GW - WC)[:, None]
    mask = np.where((c[None] >= c0) & (c[None] < c0 + WC), 0, MASKED).astype(f)
    bias = a["na_rel_bias_2"][0].reshape(NH, -1)
    at = [((np.arange(6)[None, :, None] + 5 - half) * RELC + WC - 1 + c[None, None, :] - c[:, None, None])
          for half in range(2)]
    rel = bias[:, np.concatenate(at, 0)]
    arrays = {
        "in_xT": a["x"][0].T.reshape(KT, P, T).transpose(1, 0, 2),
        "in_metaT": a["meta_tokens_2"].T.reshape(KT, P, META).transpose(1, 0, 2),
        "in_w8": w8, "in_wd": wd, "in_small": small, "in_mats": mats, "in_btab": btab, "in_rope": rope,
        "in_colmask": np.concatenate([mask, mask], 0),
        "in_metabias": np.broadcast_to(a["na_meta_bias_2"][0][None], (P, NH, META)),
        "in_relbias": rel,
    }
    arrays = {k: np.ascontiguousarray(v) for k, v in arrays.items()}
    nc = bacc.Bacc("TRN2", target_bir_lowering=False, num_devices=1)
    args = [nc.dram_tensor(k, v.shape, F32, kind="ExternalInput").ap() for k, v in arrays.items()]
    out = nc.dram_tensor("out_T", (KT, P, T), F32, kind="ExternalOutput").ap()
    build(nc, *args, out)
    r = run_bass_kernel_spmd(nc, [arrays], core_ids=[0])
    return r.results[0]["out_T"].reshape(1, D, T).transpose(0, 2, 1)
```
